# Optimizing a Trainium2 kernel written in Bass

```python
import jax, jax.numpy as jnp
from jax import lax
import numpy as np

D_MODEL = 1024
BATCH = 1
SEQ = 2048
DEPTH = 1

CTX_LEN = 256
GRID_W = 64
D_MIX = D_MODEL
D_RNN = D_MIX // 2
D_ATTN = D_MIX - D_RNN
HEAD_DIM = 64
N_Q_HEADS = D_ATTN // HEAD_DIM
N_KV_HEADS = 2
GQ = N_Q_HEADS // N_KV_HEADS
D_KV = N_KV_HEADS * HEAD_DIM
WINDOW = 128
BLK = 128
ATTN_SCALE = HEAD_DIM ** -0.5
AXIS_DIM = HEAD_DIM // 2
ROPE_BASE = 10000.0
RG_BLOCKS = 8
RG_BD = D_RNN // RG_BLOCKS
RG_C = 8.0
CONV_W = 4
CONV_LEFT = 2
N_GROUPS = 4
EXP_PER_GROUP = 8
N_EXPERTS = N_GROUPS * EXP_PER_GROUP
TOP_K = 2
D_EXPERT = 512
MOE_BLK = 128
D_IN = 2 * D_RNN + D_ATTN + 2 * D_KV
ALPHA = (2 * DEPTH) ** 0.25
BETA = (8 * DEPTH) ** -0.25
LN_EPS = 1e-6
NEG_INF = -1e30

kernel_name = "hybrid_rglru_swa_hmoe_diffusion_trunk"

def layer_norm(x, g, b):
    xf = x.astype(jnp.float32)
    mu = jnp.mean(xf, -1, keepdims=True)
    var = jnp.mean(jnp.square(xf - mu), -1, keepdims=True)
    return ((xf - mu) * lax.rsqrt(var + LN_EPS) * g + b).astype(x.dtype)

def modulate(x, shift, scale):
    xf = x.astype(jnp.float32)
    mu = jnp.mean(xf, -1, keepdims=True)
    var = jnp.mean(jnp.square(xf - mu), -1, keepdims=True)
    return ((xf - mu) * lax.rsqrt(var + LN_EPS)).astype(x.dtype) * (1.0 + scale) + shift

def rms_norm(x, g):
    xf = x.astype(jnp.float32)
    return (xf * lax.rsqrt(jnp.mean(jnp.square(xf), -1, keepdims=True) + LN_EPS) * g).astype(x.dtype)

def axial_rope_tables(seq):
    rows = seq // GRID_W
    row = jnp.repeat(jnp.arange(rows, dtype=jnp.float32), GRID_W)
    col = jnp.tile(jnp.arange(GRID_W, dtype=jnp.float32), rows)
    inv = ROPE_BASE ** (-jnp.arange(0, AXIS_DIM, 2, dtype=jnp.float32) / AXIS_DIM)
    ang_r = row[:, None] * inv
    ang_c = col[:, None] * inv
    return (jnp.cos(ang_r), jnp.sin(ang_r), jnp.cos(ang_c), jnp.sin(ang_c))

def _rotate(x, cos, sin):
    cos = cos[None, :, None, :].astype(x.dtype)
    sin = sin[None, :, None, :].astype(x.dtype)
    x1, x2 = jnp.split(x, 2, axis=-1)
    return jnp.concatenate([x1 * cos - x2 * sin, x2 * cos + x1 * sin], -1)

def rope_axial(x, rope):
    cos_r, sin_r, cos_c, sin_c = rope
    return jnp.concatenate([_rotate(x[..., :AXIS_DIM], cos_r, sin_r),
                            _rotate(x[..., AXIS_DIM:], cos_c, sin_c)], -1)

def centred_dwconv(u, w, b):
    L = u.shape[1]
    up = jnp.pad(u, ((0, 0), (CONV_LEFT, CONV_W - 1 - CONV_LEFT), (0, 0)))
    out = b
    for j in range(CONV_W):
        out = out + up[:, j:j + L] * w[j]
    return out

def _linear_recurrence_combine(e1, e2):
    a1, b1 = e1
    a2, b2 = e2
    return a1 * a2, a2 * b1 + b2

def rglru_scan(x, wa, ba, wx, bx, lam, h0, reverse):
    B, L, C = x.shape
    xh = x.reshape(B, L, RG_BLOCKS, RG_BD)
    r = jax.nn.sigmoid(jnp.einsum('blhi,hij->blhj', xh, wa).reshape(B, L, C) + ba)
    gi = jax.nn.sigmoid(jnp.einsum('blhi,hij->blhj', xh, wx).reshape(B, L, C) + bx)
    log_a = -RG_C * r.astype(jnp.float32) * jax.nn.softplus(-lam.astype(jnp.float32))
    a = jnp.exp(log_a)
    b = jnp.sqrt(-jnp.expm1(2.0 * log_a)) * (gi * x).astype(jnp.float32)
    if reverse:
        a = jnp.flip(a, 1)
        b = jnp.flip(b, 1)
    b = b.at[:, 0].add(a[:, 0] * h0)
    _, h = lax.associative_scan(_linear_recurrence_combine, (a, b), axis=1)
    h_end = h[:, -1]
    if reverse:
        h = jnp.flip(h, 1)
    return h.astype(x.dtype), h_end

def rglru_group(u_lat, u_ctx, conv_w, conv_b, wa, ba, wx, bx, lam, with_ctx_out):
    x_lat = centred_dwconv(u_lat, conv_w, conv_b)
    x_ctx = centred_dwconv(u_ctx, conv_w, conv_b)
    h0 = jnp.zeros((u_ctx.shape[0], D_RNN), jnp.float32)
    y_lat = 0.0
    y_ctx = 0.0
    for d in range(2):
        rev = d == 1
        h_ctx, h_end = rglru_scan(x_ctx, wa[d], ba[d], wx[d], bx[d], lam[d], h0, rev)
        h_lat, _ = rglru_scan(x_lat, wa[d], ba[d], wx[d], bx[d], lam[d], h_end, rev)
        y_lat = y_lat + h_lat
        if with_ctx_out:
            y_ctx = y_ctx + h_ctx
    return y_lat, (y_ctx if with_ctx_out else None)

def window_attention(q, k, v, kc, vc, sink):
    B, S = q.shape[:2]
    nb = S // BLK
    qb = q.reshape(B, nb, BLK, N_KV_HEADS, GQ, HEAD_DIM)
    pad = ((0, 0), (BLK, BLK), (0, 0), (0, 0))
    kp = jnp.pad(k, pad).reshape(B, nb + 2, BLK, N_KV_HEADS, HEAD_DIM)
    vp = jnp.pad(v, pad).reshape(B, nb + 2, BLK, N_KV_HEADS, HEAD_DIM)
    kb = jnp.concatenate([kp[:, :-2], kp[:, 1:-1], kp[:, 2:]], axis=2)
    vb = jnp.concatenate([vp[:, :-2], vp[:, 1:-1], vp[:, 2:]], axis=2)
    s_band = jnp.einsum('bnqhgd,bnkhd->bnhgqk', qb, kb).astype(jnp.float32) * ATTN_SCALE
    offs = jnp.arange(3 * BLK) - BLK
    in_win = jnp.abs(offs[None, :] - jnp.arange(BLK)[:, None]) <= WINDOW
    kpos = jnp.arange(nb)[:, None] * BLK + offs[None, :]
    in_rng = (kpos >= 0) & (kpos < S)
    mask = in_win[None] & in_rng[:, None, :]
    s_band = jnp.where(mask[None, :, None, None], s_band, NEG_INF)
    s_ctx = jnp.einsum('bnqhgd,bchd->bnhgqc', qb, kc).astype(jnp.float32) * ATTN_SCALE
    s_sink = jnp.broadcast_to(sink.astype(jnp.float32).reshape(1, 1, N_KV_HEADS, GQ, 1, 1),
                              s_band.shape[:-1] + (1,))
    p = jax.nn.softmax(jnp.concatenate([s_band, s_ctx, s_sink], -1), axis=-1)
    C = kc.shape[1]
    p_band = p[..., :3 * BLK].astype(v.dtype)
    p_ctx = p[..., 3 * BLK:3 * BLK + C].astype(v.dtype)
    o = (jnp.einsum('bnhgqk,bnkhd->bnqhgd', p_band, vb)
         + jnp.einsum('bnhgqc,bchd->bnqhgd', p_ctx, vc))
    return o.reshape(B, S, D_ATTN)

def context_attention(qc, kc, vc, sink):
    B, C = qc.shape[:2]
    qg = qc.reshape(B, C, N_KV_HEADS, GQ, HEAD_DIM)
    s = jnp.einsum('bqhgd,bkhd->bhgqk', qg, kc).astype(jnp.float32) * ATTN_SCALE
    s_sink = jnp.broadcast_to(sink.astype(jnp.float32).reshape(1, N_KV_HEADS, GQ, 1, 1),
                              s.shape[:-1] + (1,))
    p = jax.nn.softmax(jnp.concatenate([s, s_sink], -1), axis=-1)[..., :C]
    o = jnp.einsum('bhgqk,bkhd->bqhgd', p.astype(vc.dtype), vc)
    return o.reshape(B, C, D_ATTN)

def token_mixer(h_lat, h_ctx, rope, w_in, conv_w, conv_b, rg_wa, rg_ba, rg_wx, rg_bx, rg_lam,
                sink, gn_rnn, gn_attn, w_out, with_ctx_out):
    B, S, _ = h_lat.shape
    C = h_ctx.shape[1]
    cuts = [D_RNN, 2 * D_RNN, 2 * D_RNN + D_ATTN, 2 * D_RNN + D_ATTN + D_KV]
    u_l, g_l, q_l, k_l, v_l = jnp.split(h_lat @ w_in, cuts, axis=-1)
    u_c, g_c, q_c, k_c, v_c = jnp.split(h_ctx @ w_in, cuts, axis=-1)
    r_l, r_c = rglru_group(u_l, u_c, conv_w, conv_b, rg_wa, rg_ba, rg_wx, rg_bx, rg_lam, with_ctx_out)
    q_l = rope_axial(q_l.reshape(B, S, N_Q_HEADS, HEAD_DIM), rope)
    k_l = rope_axial(k_l.reshape(B, S, N_KV_HEADS, HEAD_DIM), rope)
    v_l = v_l.reshape(B, S, N_KV_HEADS, HEAD_DIM)
    k_c = k_c.reshape(B, C, N_KV_HEADS, HEAD_DIM)
    v_c = v_c.reshape(B, C, N_KV_HEADS, HEAD_DIM)
    a_l = window_attention(q_l, k_l, v_l, k_c, v_c, sink)
    o_lat = jnp.concatenate([rms_norm(r_l * jax.nn.gelu(g_l), gn_rnn),
                             rms_norm(a_l, gn_attn)], -1) @ w_out
    if not with_ctx_out:
        return o_lat, None
    a_c = context_attention(q_c, k_c, v_c, sink)
    o_ctx = jnp.concatenate([rms_norm(r_c * jax.nn.gelu(g_c), gn_rnn),
                             rms_norm(a_c, gn_attn)], -1) @ w_out
    return o_lat, o_ctx

def hier_moe(xf, wg, bg, we, be, w1, w3, w2):
    T, D = xf.shape
    g_logits = (xf @ wg + bg).astype(jnp.float32)
    g_prob = jax.nn.softmax(g_logits, -1)
    _, g_sel = lax.top_k(g_logits, 1)
    p_g = jnp.take_along_axis(g_prob, g_sel, axis=-1)
    e_logits = (xf @ we + be).astype(jnp.float32).reshape(T, N_GROUPS, EXP_PER_GROUP)
    e_in = jnp.take_along_axis(e_logits, g_sel[:, :, None], axis=1)[:, 0]
    top_v, top_i = lax.top_k(e_in, TOP_K)
    gate = (jax.nn.softmax(top_v, -1) * p_g).astype(xf.dtype)
    expert_id = (g_sel * EXP_PER_GROUP + top_i).astype(jnp.int32)
    TK = T * TOP_K
    n_blocks = (TK + N_EXPERTS * (MOE_BLK - 1) + MOE_BLK - 1) // MOE_BLK
    flat_e = expert_id.reshape(-1)
    order = jnp.argsort(flat_e)
    sorted_e = flat_e[order]
    counts = jax.ops.segment_sum(jnp.ones_like(flat_e), flat_e, num_segments=N_EXPERTS)
    starts = jnp.cumsum(counts) - counts
    pcounts = (counts + MOE_BLK - 1) // MOE_BLK * MOE_BLK
    pends = jnp.cumsum(pcounts)
    pstarts = pends - pcounts
    dest = pstarts[sorted_e] + (jnp.arange(TK, dtype=jnp.int32) - starts[sorted_e])
    tok_sorted = (order // TOP_K).astype(jnp.int32)
    slot_tok = jnp.full((n_blocks * MOE_BLK,), T, jnp.int32).at[dest].set(tok_sorted)
    x_pad = jnp.concatenate([xf, jnp.zeros((1, D), xf.dtype)], 0)
    xb = x_pad[slot_tok].reshape(n_blocks, MOE_BLK, D)
    blk_e = jnp.minimum(jnp.searchsorted(pends, jnp.arange(n_blocks) * MOE_BLK, side='right'),
                        N_EXPERTS - 1)

    def run_block(args):
        xblk, e = args
        h = jax.nn.silu(xblk @ w1[e]) * (xblk @ w3[e])
        return h @ w2[e]

    yb = lax.map(run_block, (xb, blk_e)).reshape(n_blocks * MOE_BLK, D)
    y_assign = yb[dest] * gate.reshape(-1)[order][:, None]
    return jax.ops.segment_sum(y_assign, tok_sorted, num_segments=T)

def setup_inputs(seed: int = 0) -> dict:
    key = jax.random.key(seed)
    ks = jax.random.split(key, 32)
    L = DEPTH

    def nrm(k, shape, s):
        return jax.random.normal(k, shape, jnp.float32) * s

    u = jax.random.uniform(ks[10], (L, 2, D_RNN), jnp.float32, minval=0.9, maxval=0.999)
    a0 = u ** (1.0 / RG_C)
    rg_lam = jnp.log(a0) - jnp.log1p(-a0)
    return {
        "x": nrm(ks[0], (BATCH, SEQ, D_MODEL), 1.0),
        "c": nrm(ks[1], (BATCH, D_MODEL), 1.0),
        "ctx": nrm(ks[2], (BATCH, CTX_LEN, D_MODEL), 1.0),
        "c_ctx": nrm(ks[3], (D_MODEL,), 1.0),
        "w_mod": nrm(ks[4], (L, D_MODEL, 6 * D_MODEL), 0.5 * D_MODEL ** -0.5),
        "b_mod": nrm(ks[5], (L, 6 * D_MODEL), 0.01),
        "w_in": nrm(ks[6], (L, D_MODEL, D_IN), D_MODEL ** -0.5),
        "conv_w": nrm(ks[7], (L, CONV_W, D_RNN), CONV_W ** -0.5),
        "conv_b": nrm(ks[8], (L, D_RNN), 0.01),
        "rg_wa": nrm(ks[9], (L, 2, RG_BLOCKS, RG_BD, RG_BD), RG_BD ** -0.5),
        "rg_ba": nrm(ks[11], (L, 2, D_RNN), 0.01),
        "rg_wx": nrm(ks[12], (L, 2, RG_BLOCKS, RG_BD, RG_BD), RG_BD ** -0.5),
        "rg_bx": nrm(ks[13], (L, 2, D_RNN), 0.01),
        "rg_lam": rg_lam,
        "attn_sink": nrm(ks[14], (L, N_Q_HEADS), 0.5),
        "gn_rnn": 1.0 + nrm(ks[15], (L, D_RNN), 0.02),
        "gn_attn": 1.0 + nrm(ks[16], (L, D_ATTN), 0.02),
        "w_out": nrm(ks[17], (L, D_MIX, D_MODEL), BETA * D_MIX ** -0.5),
        "ln1_g": 1.0 + nrm(ks[18], (L, D_MODEL), 0.02),
        "ln1_b": nrm(ks[19], (L, D_MODEL), 0.01),
        "router_g": nrm(ks[20], (L, D_MODEL, N_GROUPS), D_MODEL ** -0.5),
        "router_gb": nrm(ks[21], (L, N_GROUPS), 0.01),
        "router_e": nrm(ks[22], (L, D_MODEL, N_EXPERTS), D_MODEL ** -0.5),
        "router_eb": nrm(ks[23], (L, N_EXPERTS), 0.01),
        "w1": nrm(ks[24], (L, N_EXPERTS, D_MODEL, D_EXPERT), D_MODEL ** -0.5),
        "w3": nrm(ks[25], (L, N_EXPERTS, D_MODEL, D_EXPERT), D_MODEL ** -0.5),
        "w2": nrm(ks[26], (L, N_EXPERTS, D_EXPERT, D_MODEL), BETA * D_EXPERT ** -0.5),
        "ln2_g": 1.0 + nrm(ks[27], (L, D_MODEL), 0.02),
        "ln2_b": nrm(ks[28], (L, D_MODEL), 0.01),
    }

def reference(x, c, ctx, c_ctx, w_mod, b_mod, w_in, conv_w, conv_b, rg_wa, rg_ba, rg_wx, rg_bx,
              rg_lam, attn_sink, gn_rnn, gn_attn, w_out, ln1_g, ln1_b, router_g, router_gb,
              router_e, router_eb, w1, w3, w2, ln2_g, ln2_b):
    B, S, D = x.shape
    rope = axial_rope_tables(S)
    silu_c = jax.nn.silu(c)
    silu_cc = jax.nn.silu(c_ctx)
    xc = ctx
    for l in range(DEPTH):
        last = l == DEPTH - 1
        m_lat = silu_c @ w_mod[l] + b_mod[l]
        m_ctx = silu_cc @ w_mod[l] + b_mod[l]
        sh1, sc1, g1, sh2, sc2, g2 = jnp.split(m_lat[:, None, :], 6, axis=-1)
        sh1c, sc1c, g1c, sh2c, sc2c, g2c = jnp.split(m_ctx, 6)
        h_lat = modulate(x, sh1, sc1)
        h_ctx = modulate(xc, sh1c, sc1c)
        y_lat, y_ctx = token_mixer(h_lat, h_ctx, rope, w_in[l], conv_w[l], conv_b[l], rg_wa[l],
                                   rg_ba[l], rg_wx[l], rg_bx[l], rg_lam[l], attn_sink[l],
                                   gn_rnn[l], gn_attn[l], w_out[l], not last)
        x = layer_norm(ALPHA * x + g1 * y_lat, ln1_g[l], ln1_b[l])
        h_lat = modulate(x, sh2, sc2).reshape(B * S, D)
        if last:
            y = hier_moe(h_lat, router_g[l], router_gb[l], router_e[l], router_eb[l],
                         w1[l], w3[l], w2[l])
            x = layer_norm(ALPHA * x + g2 * y.reshape(B, S, D), ln2_g[l], ln2_b[l])
        else:
            xc = layer_norm(ALPHA * xc + g1c * y_ctx, ln1_g[l], ln1_b[l])
            h_ctx = modulate(xc, sh2c, sc2c).reshape(-1, D)
            y = hier_moe(jnp.concatenate([h_lat, h_ctx], 0), router_g[l], router_gb[l],
                         router_e[l], router_eb[l], w1[l], w3[l], w2[l])
            x = layer_norm(ALPHA * x + g2 * y[:B * S].reshape(B, S, D), ln2_g[l], ln2_b[l])
            xc = layer_norm(ALPHA * xc + g2c * y[B * S:].reshape(xc.shape), ln2_g[l], ln2_b[l])
    return x


_drawn_inputs = setup_inputs


def setup_inputs(seed=0):
    import zlib

    import numpy as np

    out = dict(_drawn_inputs(seed))
    spreads = {}
    factors = {'b_mod': 5.982,
     'conv_b': 8.0,
     'rg_wa': 3.981,
     'rg_ba': 64.0,
     'rg_bx': 35.512,
     'attn_sink': 8.0,
     'gn_rnn': 48.716,
     'gn_attn': 40.804,
     'ln1_g': 8.117,
     'ln1_b': 15.603,
     'router_gb': 64.0,
     'router_eb': 64.0,
     'ln2_g': 9.512,
     'ln2_b': 17.096,
     'router_g': 3.882,
     'router_e': 4.066,
     'w1': 3.661,
     'w3': 3.407,
     'w2': 3.44}
    for name, (base, spread) in spreads.items():
        noise = np.random.default_rng([zlib.crc32(name.encode()), seed]).standard_normal(out[name].shape)
        drawn = base * np.exp(spread * noise) if base else spread * noise
        out[name] = __import__('jax').numpy.asarray(drawn.astype(out[name].dtype))
    for name, factor in factors.items():
        out[name] = (out[name] * factor).astype(out[name].dtype)
    return out
```

```python
from contextlib import ExitStack

import numpy as np

import concourse.bass as bass
from concourse import mybir

F32 = mybir.dt.float32
F16 = mybir.dt.float16
I32 = mybir.dt.int32
U32 = mybir.dt.uint32
ALU = mybir.AluOpType
ACT = mybir.ActivationFunctionType
AX_X = mybir.AxisListType.X

P = 128
D = 1024
KD = D // P
SEQ = 2048
CTX = 256
T_LAT = SEQ // P
D_RNN = 512
C_RNN = D_RNN // P
D_ATTN = 512
HD = 64
NH = D_ATTN // HD
NKV = 2
PAIRS = NH // NKV
QKV = D_ATTN + 2 * NKV * HD
D_IN = 2 * D_RNN + QKV
TIME = CTX + SEQ
U_CTX = 2
U_LAT = U_CTX + CTX + 2
U_ROW = U_LAT + SEQ + 4
WIN = 3 * P
KEYS = CTX + WIN
K_LAT = CTX + P
K_ROW = K_LAT + SEQ + P
CONV_W = 4
NE = 32
NG = 4
EPG = NE // NG
D_EXP = 512
KE = D_EXP // P
MAX_BLOCKS = (2 * SEQ + NE * (P - 1)) // P + 1
NPAR = 9
ALPHA = 2 ** 0.25
START = 1
W_SCALE, X_SCALE = 64.0, 16.0
TAB_RANK, TAB_BUF, TAB_NEW, TAB_EXPERT = 0, 64, 128, 192
TAB_NB, TAB_NB1, TAB_NB2, TAB_NR, TAB_FREE = 224, 225, 226, 227, 228
TAB_SIZE = 264
EPS = 1e-6
NEG = -1e30
CHUNK = 512
TPC = CHUNK // P

SEMAPHORES = """
b_mcol_ld b_rope_ld b_x_ld b_g_st b_q_st b_pads b_sc b_stats b_agg b_var b_rstd b_normed b_tr_x b_hT_a b_hT_v
b_u_mm b_g_mm b_u_ev b_g_ev b_qkv_mm b_rope_a b_rope_b b_rope_o b_v_ev b_q_tr b_k_tr b_q_ev b_k_ev c_lam_ld
c_par_ld c_gw_ld c_gate_ld c_zero c_sp_v c_sp_a c_cur c_conv c_g_mm c_g_ev c_tanh c_exp c_sqrt c_frac c_drive
c_scan c_y c_y_st d_mask_ld d_q_ld d_s_mm d_s_max d_nm d_p d_p_tr d_p_ev d_pv d_o_free d_es d_es_e d_den d_o
e_w_ld e_in_ld e_x_st e_h_st e_w_ok e_sq e_ssm e_ss e_pw e_a_tr e_a_ev e_o_mm e_o_act e_v e_pool e_h_tr e_h_ev
e_r_mm e_lg e_p_ok f_ld f_v f_act f_mm f_tab_ld f_tr g_st_ld0 g_st_ld1 g_st_ld2 g_st_ld3 g_st_ld4 g_st_ld5
g_hi13 g_lo13 g_hi2 g_lo2 g_g2_ld g_x_ix g_x_tr g_x_hi g_x_lo g_up_mm g_silu g_h g_h_tr g_h_hi g_h_lo g_y_mm
g_y_ev g_y_st g_zero g_z_st h_ld h_ix h_x_ld h_o_st h_v h_pw h_a_x h_a_n h_fin h_hold h_mh
""".split()


def arena_slices(arena, start, sizes):
    out = {}
    for name, size in sizes:
        out[name] = arena[:, start:start + size]
        start += size
    assert start <= arena.shape[1], start
    return out


def hybrid_layer(nc, x, c2, w_mod, b_mod, w_in, rg_par, lam, rg_wa, rg_wx, ctx_x, sink, w_out, gn, ln1, router, router_b,
                 w1, w3, w2, ln2, cos_t, sin_t, ident, masks, tri, iota, tok_id, out):
    with ExitStack() as stack:
        def plain_sem(name):
            return stack.enter_context(nc.semaphore(name))

        from_one = {name: plain_sem(name) for name in SEMAPHORES}

        def sem(name):
            return from_one[name]

        def sb(name, shape, dt=F32):
            return stack.enter_context(nc.sbuf_tensor(name, shape, dt))

        def dram(name, shape, dt=F32):
            return nc.dram_tensor(name, shape, dt, kind="Internal").ap()

        mod_rows = dram("mod_rows", [2, 6 * D])
        gate_d = dram("gate_d", [C_RNN, P, SEQ])
        qT_d = dram("qT_d", [T_LAT, P, PAIRS * P])
        yT_d = dram("yT_d", [C_RNN, P, SEQ])
        attn_d = dram("attn_d", [T_LAT, P, D_ATTN])
        x1_d = dram("x1_d", [SEQ, D])
        h2_d = dram("h2_d", [SEQ, D])
        slot_tok_d = dram("slot_tok_d", [64 * P, 1], I32)
        y_d = dram("y_d", [64 * P, D])

        idn = sb("idn", [P, P])
        small = sb("small", [P, 640])
        arena = sb("arena", [P, 50500])
        slot_i = sb("slot_i", [P, 2 * T_LAT], I32)
        gates = sb("gates", [P, 2 * T_LAT])
        blk_tab = sb("blk_tab", [1, TAB_SIZE], I32)
        gidx = sb("gidx", [P, 66], I32)
        ps = stack.enter_context(nc.psum_tensor("ps", [P, 8, 512], F32))
        ps_row = ps[:, :, :].rearrange("p b n -> p (b n)")

        const_ld = plain_sem("const_ld")
        win_ld = plain_sem("win_ld")
        alone = plain_sem("alone")
        env = dict(locals())
        phase_modulation(nc, env)
        phase_project(nc, env)
        phase_recurrence(nc, env)
        phase_attention(nc, env)
        phase_output(nc, env)
        phase_route(nc, env)
        phase_experts(nc, env)
        phase_combine(nc, env)


UT0 = 0
KT0 = UT0 + C_RNN * U_ROW
V0 = KT0 + 2 * K_ROW
V_SLOTS = 2 + 1 + T_LAT + 1
B0 = V0 + V_SLOTS * P
WIN0 = 50500 - KD * D_IN


def phase_modulation(nc, env):
    g = env
    sem, arena, ps, small = g["plain_sem"], g["arena"], g["ps"], g["small"]
    c_ld, silu_done = sem("a_c_ld"), sem("a_silu_done")
    wmod_ld = [sem(f"a_wmod_ld{j}") for j in range(3)]
    mod_mm, rows_done, rows_st = sem("a_mod_mm"), sem("a_rows_done"), sem("a_rows_st")
    a = arena_slices(arena, 0, [("w0", KD * 512), ("w1", KD * 512), ("w2", KD * 512), ("rows", 6 * D)])
    ring = [a[f"w{j}"].rearrange("p (k n) -> p k n", k=KD) for j in range(3)]
    c2s = small[:, 0:2 * KD]
    c2a = small[:, 2 * KD:4 * KD]
    zi = small[0:64, 128:256].bitcast(I32)
    wmod_v = g["w_mod"].rearrange("(k p) n -> p k n", p=P)
    with nc.Block() as block:
        @block.sync
        def _(sp):
            sp.dma_start(c2s, g["c2"]).then_inc(c_ld, 16)
            sp.dma_start(a["rows"][0:2, :], g["b_mod"]).then_inc(c_ld, 16)
            sp.dma_start(g["idn"][:], g["ident"]).then_inc(g["const_ld"], 16)
            for j in range(3):
                sp.dma_start(ring[j], wmod_v[:, :, j * 512:(j + 1) * 512]).then_inc(wmod_ld[j], 16)
            with sp.Fori(0, 3) as i:
                for j in range(3):
                    sp.wait_ge(mod_mm, i * 3 + j + 1)
                    sp.dma_start(ring[j], wmod_v[:, :, bass.ds(i * 1536 + (j + 3) * 512, 512)]).then_inc(wmod_ld[j], 16)
            win = arena[:, WIN0:].rearrange("p (k n) -> p k n", k=KD)
            sp.dma_start(win, g["w_in"].rearrange("(k p) n -> p k n", p=P)).then_inc(g["win_ld"], 16)
            sp.wait_ge(rows_done, 1)
            sp.dma_start(g["slot_tok_d"].rearrange("(a b) o -> a (b o)", a=64), zi).then_inc(rows_st, 16)
            sp.wait_ge(rows_done, 13)
            sp.dma_start(g["mod_rows"], a["rows"][0:2, :]).then_inc(rows_st, 16)
            sp.wait_ge(rows_st, 32)
            sp.wait_ge(c_ld, 32)
            sp.wait_ge(g["const_ld"], 16)

        @block.gpsimd
        def _(pool):
            for s in g["from_one"].values():
                pool.sem_inc(s, START)

        @block.scalar
        def _(act):
            act.wait_ge(c_ld, 32)
            nc.scalar.activation(c2a, c2s, ACT.Silu).then_inc(silu_done, 1)

        @block.tensor
        def _(pe):
            pe.wait_ge(silu_done, 1)
            with pe.Fori(0, 4) as i:
                for j in range(3):
                    pe.wait_ge(wmod_ld[j], i * 16 + 16)
                    pe.wait_ge(rows_done, i * 3 + 1)
                    for k in range(KD):
                        mm = pe.matmul(ps[0:2, j, :], c2a[:, 2 * k:2 * k + 2], ring[j][:, k, :],
                                       start=(k == 0), stop=(k == KD - 1))
                    mm.then_inc(mod_mm, 1)

        @block.vector
        def _(dve):
            nc.vector.memset(zi, 0).then_inc(rows_done, 1)
            dve.wait_ge(c_ld, 32)
            with dve.Fori(0, 4) as i:
                for j in range(3):
                    row = a["rows"][0:2, bass.ds(i * 1536 + j * 512, 512)]
                    dve.wait_ge(mod_mm, i * 3 + j + 1)
                    nc.vector.tensor_tensor(row, ps[0:2, j, :], row, ALU.add).then_inc(rows_done, 1)


def phase_project(nc, env):
    g = env
    sem, arena, ps, ps_row, small, idn = g["sem"], g["arena"], g["ps"], g["ps_row"], g["small"], g["idn"]
    uT = arena[:, UT0:KT0].rearrange("p (c t) -> p c t", c=C_RNN)
    kTz = arena[:, KT0:V0].rearrange("p (z t) -> p z t", z=2)
    vt = arena[:, V0:B0].rearrange("p (s d) -> p s d", s=V_SLOTS)
    b = arena_slices(arena, B0, [("xr", TPC * D), ("xn", TPC * D), ("hT", KD * CHUNK), ("gout", 2 * CHUNK),
                                 ("qr", 640), ("ta", 320), ("tb", 320), ("qTs", 512)])
    assert B0 + 2 * TPC * D + KD * CHUNK + 2 * CHUNK + 1792 <= WIN0, (B0, WIN0)
    win = arena[:, WIN0:].rearrange("p (k n) -> p k n", k=KD)
    xr = b["xr"].rearrange("p (t d) -> p t d", t=TPC)
    xn = b["xn"].rearrange("p (t d) -> p t d", t=TPC)
    hT = b["hT"].rearrange("p (k n) -> p k n", k=KD)
    gout = b["gout"].rearrange("p (a n) -> p a n", a=2)
    qr, ta, tb = b["qr"], b["ta"], b["tb"]
    mcol = small[:, 0:32].rearrange("p (s n) -> p s n", s=2)
    st = small[:, 32:32 + 12 * TPC].rearrange("p (t a s) -> p t a s", t=TPC, a=2)
    mv = small[:, 80:80 + 2 * TPC].rearrange("p (t s) -> p t s", t=TPC)
    ve = small[:, 96:96 + TPC]
    rs = small[:, 100:100 + TPC]
    mh = small[:, 104:104 + TPC]
    rope = g["stack"].enter_context(nc.sbuf_tensor("rope", [P, 2, 2, 32], F32))

    mcol_ld, rope_ld, x_ld, g_st, q_st = sem("b_mcol_ld"), sem("b_rope_ld"), sem("b_x_ld"), sem("b_g_st"), sem("b_q_st")
    pads, sc_ok, stats, agg, var_e, rstd = sem("b_pads"), sem("b_sc"), sem("b_stats"), sem("b_agg"), sem("b_var"), sem("b_rstd")
    normed, tr_x, hT_a, hT_v = sem("b_normed"), sem("b_tr_x"), sem("b_hT_a"), sem("b_hT_v")
    u_mm, g_mm, u_ev, g_ev = sem("b_u_mm"), sem("b_g_mm"), sem("b_u_ev"), sem("b_g_ev")
    qkv_mm, rope_a, rope_b, rope_o = sem("b_qkv_mm"), sem("b_rope_a"), sem("b_rope_b"), sem("b_rope_o")
    v_ev, q_tr, k_tr, q_ev, k_ev = sem("b_v_ev"), sem("b_q_tr"), sem("b_k_tr"), sem("b_q_ev"), sem("b_k_ev")

    NT_C = CTX // P
    x_lat = g["x"].rearrange("(n t p) d -> n p t d", p=P, t=TPC)
    x_ctx = g["ctx_x"].rearrange("(t p) d -> p t d", p=P)

    def at(i, ctx, lat, k):
        return k if i is None else ctx + i * lat + k

    with nc.Block() as block:
        @block.sync
        def _(sp):
            for s in range(2):
                for half in range(2):
                    for k in range(KD):
                        src = g["mod_rows"][s:s + 1, half * D + k * P:half * D + (k + 1) * P].rearrange("o p -> p o")
                        sp.dma_start(mcol[:, s, half * KD + k:half * KD + k + 1], src).then_inc(mcol_ld, 16)
            sp.dma_start(xr[:, 0:NT_C, :], x_ctx).then_inc(x_ld, 16)

            def chunk(i):
                sp.wait_ge(normed, START + NT_C + i * TPC)
                sp.sem_inc(g["alone"], 1)
                sp.dma_start(xr, x_lat[bass.ds(i, 1)].rearrange("n p t d -> (n p) t d")).then_inc(x_ld, 16)
                for t in range(TPC):
                    n = i * TPC + t
                    sp.dma_start(rope[:, t % 2, 0, :],
                                 g["cos_t"][bass.ds(n, 1)].rearrange("n p d -> (n p) d")).then_inc(rope_ld, 16)
                    sp.dma_start(rope[:, t % 2, 1, :],
                                 g["sin_t"][bass.ds(n, 1)].rearrange("n p d -> (n p) d")).then_inc(rope_ld, 16)
                    sp.wait_ge(rope_o, START + NT_C + 2 * (i * TPC + t) + 2)
                    sp.sem_inc(g["alone"], 1)
                    sp.wait_ge(q_ev, START + i * TPC + t + 1)
                    sp.sem_inc(g["alone"], 1)
                    sp.dma_start(g["qT_d"][bass.ds(n, 1)].rearrange("n p d -> (n p) d"), b["qTs"]).then_inc(q_st, 16)
            with sp.Fori(0, SEQ // CHUNK) as i:
                chunk(i)
            sp.wait_ge(q_st, START + 16 * T_LAT)

        def evac_plan(k):
            return "act" if k % 2 == 0 else "dve"

        @block.scalar
        def _(act):
            def chunk(i):
                nt = NT_C if i is None else TPC
                n = nt * P
                s = 1 if i is None else 0
                if i is None:
                    act.wait_ge(sc_ok, START + 1)
                for k in range(0, KD, 2):
                    act.wait_ge(tr_x, START + at(i, KD, KD, k + 1))
                    nc.scalar.activation(hT[:, k, 0:n], ps[:, 0, 0:n], ACT.Identity, bias=mcol[:, s, k:k + 1],
                                         scale=mcol[:, s, KD + k:KD + k + 1]).then_inc(hT_a, 1)
                if i is not None:
                    for c in range(C_RNN):
                        act.wait_ge(g_mm, START + i * C_RNN + c + 1)
                        act.wait_ge(g_st, START + (i * C_RNN + c) * 16)
                        nc.scalar.activation(gout[:, 0, :], ps[:, 3, :], ACT.Gelu_apprx_tanh).then_inc(g_ev, 1)
                        act.wait_ge(g_ev, START + i * C_RNN + c + 1)
                        act.dma_start(g["gate_d"][c][:, bass.ds(i * CHUNK, CHUNK)], gout[:, 0, :]).then_inc(g_st, 16)
                for t in range(nt):
                    act.wait_ge(rope_o, START + (t + 1 if i is None else NT_C + 2 * (i * TPC + t) + 2))
                    bank = 4 + 2 * (t % 2)
                    if i is None:
                        nc.scalar.activation(vt[:, t, :], ps[:, bank + 1, P:2 * P], ACT.Copy).then_inc(v_ev, 1)
                    else:
                        nc.scalar.activation(arena[:, bass.ds(V0 + (3 + t) * P + i * (TPC * P), P)],
                                             ps[:, bank + 1, P:2 * P], ACT.Copy).then_inc(v_ev, 1)
                        act.wait_ge(q_tr, START + i * TPC + t + 1)
                        act.wait_ge(q_st, START + (i * TPC + t) * 16)
                        nc.scalar.activation(b["qTs"], ps[:, 0, :], ACT.Copy, scale=HD ** -0.5).then_inc(q_ev, 1)
                    act.wait_ge(k_tr, START + at(i, NT_C, TPC, t + 1))
                    for z in range(2):
                        dst = kTz[64 * z:64 * z + 64, z, t * P:(t + 1) * P] if i is None else \
                            arena[64 * z:64 * z + 64, bass.ds(KT0 + z * K_ROW + K_LAT + t * P + i * CHUNK, P)]
                        nc.scalar.activation(dst, ps[64 * z:64 * z + 64, 1, 0:P], ACT.Copy).then_inc(k_ev, 1)
            act.wait_ge(pads, START + 5)
            chunk(None)
            with act.Fori(0, SEQ // CHUNK) as i:
                chunk(i)
            act.wait_ge(g_st, START + 16 * C_RNN * (SEQ // CHUNK))

        @block.gpsimd
        def _(pool):
            nc.gpsimd.memset(mh, -0.5).then_inc(pads, 1)
            nc.gpsimd.memset(kTz, 0.0).then_inc(pads, 1)
            nc.gpsimd.memset(vt[:, 2, :], 0.0).then_inc(pads, 1)
            nc.gpsimd.memset(vt[:, V_SLOTS - 1, :], 0.0).then_inc(pads, 1)
            nc.gpsimd.memset(uT, 0.0).then_inc(pads, 1)

            def chunk(i):
                nt = NT_C if i is None else TPC
                pool.wait_ge(pads, START + 5)
                pool.wait_ge(var_e, START + (1 if i is None else i + 2))
                nc.gpsimd.tensor_tensor(rs[:, 0:nt], ve[:, 0:nt], mh[:, 0:nt], ALU.pow).then_inc(rstd, 1)
            chunk(None)
            with pool.Fori(0, SEQ // CHUNK) as i:
                chunk(i)

        @block.vector
        def _(dve):
            dve.wait_ge(mcol_ld, START + 16 * 32)
            nc.vector.tensor_scalar(mcol[:, :, KD:2 * KD], mcol[:, :, KD:2 * KD], 1.0, None, ALU.add).then_inc(sc_ok, 1)
            dve.wait_ge(sc_ok, START + 1)
            dve.wait_ge(pads, START + 5)

            def norm(i):
                nt = NT_C if i is None else TPC
                dve.wait_ge(x_ld, START + (16 if i is None else i * 16 + 32))
                for t in range(nt):
                    for a in range(2):
                        nc.vector.bn_stats(st[:, t, a, :], xr[:, t, a * 512:(a + 1) * 512]).then_inc(stats, 1)
                dve.wait_ge(stats, START + at(i, 2 * NT_C, 2 * TPC, 2 * nt))
                dve.sem_inc(g["alone"], 1)
                for t in range(nt):
                    nc.vector.bn_aggr(mv[:, t, :], st[:, t, :, :]).then_inc(agg, 1)
                dve.wait_ge(agg, START + at(i, NT_C, TPC, nt))
                nc.vector.tensor_scalar(ve[:, 0:nt], mv[:, 0:nt, 1], EPS, None, ALU.add).then_inc(var_e, 1)
                dve.wait_ge(rstd, START + (1 if i is None else i + 2))
                dve.wait_ge(tr_x, START + at(i, KD, KD, 0))
                for t in range(nt):
                    nc.vector.tensor_scalar(xn[:, t, :], xr[:, t, :], mv[:, t, 0:1], rs[:, t:t + 1],
                                            ALU.subtract, ALU.mult).then_inc(normed, 1)

            def chunk(i):
                nt = NT_C if i is None else TPC
                n = nt * P
                s = 1 if i is None else 0
                norm(i)
                for k in range(1, KD, 2):
                    dve.wait_ge(tr_x, START + at(i, KD, KD, k + 1))
                    nc.vector.tensor_scalar(hT[:, k, 0:n], ps[:, 1, 0:n], mcol[:, s, KD + k:KD + k + 1],
                                            mcol[:, s, k:k + 1], ALU.mult, ALU.add).then_inc(hT_v, 1)
                for c in range(C_RNN):
                    dve.wait_ge(u_mm, START + at(i, C_RNN, C_RNN, c + 1))
                    dst = uT[:, c, U_CTX:U_CTX + CTX] if i is None else \
                        arena[:, bass.ds(UT0 + c * U_ROW + U_LAT + i * CHUNK, CHUNK)]
                    nc.vector.tensor_copy(dst, ps[:, 2, 0:n]).then_inc(u_ev, 1)
                for t in range(nt):
                    bank = 4 + 2 * (t % 2)
                    dve.wait_ge(qkv_mm, START + at(i, NT_C, TPC, t + 1))
                    if i is None:
                        if t:
                            dve.wait_ge(k_tr, START + t)
                        nc.vector.tensor_copy(qr[:, 512:640], ps[:, bank + 1, 0:P]).then_inc(rope_o, 1)
                        continue
                    j = i * TPC + t
                    dve.wait_ge(rope_ld, START + 32 * j + 32)
                    raw = ps_row[:, bank * 512:bank * 512 + 640].rearrange("p (h a f d) -> p h a f d", a=2, f=2, d=16)
                    rot = qr.rearrange("p (h a f d) -> p h a f d", a=2, f=2, d=16)
                    co = rope[:, t % 2, 0, :].rearrange("p (o a d) -> p o a d", o=1, a=2).to_broadcast([P, 10, 2, 16])
                    si = rope[:, t % 2, 1, :].rearrange("p (o a d) -> p o a d", o=1, a=2).to_broadcast([P, 10, 2, 16])
                    tav = ta.rearrange("p (h a d) -> p h a d", a=2, d=16)
                    tbv = tb.rearrange("p (h a d) -> p h a d", a=2, d=16)
                    for f, op in ((0, ALU.subtract), (1, ALU.add)):
                        dve.wait_ge(rope_o, START + NT_C + 2 * j + f)
                        nc.vector.tensor_tensor(tav, raw[:, :, :, f, :], co, ALU.mult).then_inc(rope_a, 1)
                        nc.vector.tensor_tensor(tbv, raw[:, :, :, 1 - f, :], si, ALU.mult).then_inc(rope_a, 1)
                        dve.wait_ge(rope_a, START + 4 * j + 2 * f + 2)
                        if f == 0:
                            dve.wait_ge(k_tr, START + NT_C + j)
                        nc.vector.tensor_tensor(rot[:, :, :, f, :], tav, tbv, op).then_inc(rope_o, 1)
            chunk(None)
            with dve.Fori(0, SEQ // CHUNK) as i:
                chunk(i)

        @block.tensor
        def _(pe):
            pe.wait_ge(g["const_ld"], 16)

            def transposed(i):
                nt = NT_C if i is None else TPC
                pe.wait_ge(normed, START + at(i, NT_C, TPC, nt))
                for k in range(KD):
                    ev, n = (hT_a, k // 2) if k % 2 == 0 else (hT_v, k // 2)
                    pe.wait_ge(ev, START + at(i, KD // 2, KD // 2, n))
                    if k == 0:
                        if i is not None:
                            pe.wait_ge(q_ev, START + i * TPC)
                    if k == 1:
                        pe.wait_ge(k_ev, START + at(i, 2 * NT_C, 2 * TPC, 0))
                    for t in range(nt):
                        mm = pe.transpose(ps[:, k % 2, t * P:(t + 1) * P], xn[:, t, k * P:(k + 1) * P], idn[:])
                    mm.then_inc(tr_x, 1)

            def qk_transposes(i, t):
                pe.wait_ge(rope_o, START + (t + 1 if i is None else NT_C + 2 * (i * TPC + t) + 2))
                if i is not None:
                    pe.wait_ge(q_ev, START + i * TPC + t)
                    for a in range(PAIRS):
                        mm = pe.transpose(ps[:, 0, a * P:(a + 1) * P], qr[:, a * P:(a + 1) * P], idn[:])
                    mm.then_inc(q_tr, 1)
                pe.wait_ge(k_ev, START + at(i, 2 * NT_C, 2 * TPC, 2 * t))
                pe.transpose(ps[:, 1, 0:P], qr[:, 512:640], idn[:]).then_inc(k_tr, 1)

            def chunk(i):
                nt = NT_C if i is None else TPC
                n = nt * P
                transposed(i)
                pe.wait_ge(hT_a, START + at(i, KD // 2, KD // 2, KD // 2))
                pe.wait_ge(hT_v, START + at(i, KD // 2, KD // 2, KD // 2))
                for c in range(C_RNN):
                    pe.wait_ge(u_ev, START + at(i, C_RNN, C_RNN, c))
                    for k in range(KD):
                        mm = pe.matmul(ps[:, 2, 0:n], win[:, k, c * P:(c + 1) * P], hT[:, k, 0:n],
                                       start=(k == 0), stop=(k == KD - 1))
                    mm.then_inc(u_mm, 1)
                    if i is not None:
                        pe.wait_ge(g_ev, START + i * C_RNN + c)
                        for k in range(KD):
                            mm = pe.matmul(ps[:, 3, 0:n], win[:, k, D_RNN + c * P:D_RNN + (c + 1) * P], hT[:, k, 0:n],
                                           start=(k == 0), stop=(k == KD - 1))
                        mm.then_inc(g_mm, 1)
                for t in range(nt):
                    bank = 4 + 2 * (t % 2)
                    m = max(t - 1, 0)
                    pe.wait_ge(v_ev, START + at(i, NT_C, TPC, m))
                    pe.wait_ge(rope_o, START + (m if i is None else NT_C + 2 * (i * TPC + m)))
                    for k in range(KD):
                        if i is not None:
                            pe.matmul(ps[:, bank, :], hT[:, k, t * P:(t + 1) * P], win[:, k, D:D + 512],
                                      start=(k == 0), stop=(k == KD - 1))
                        mm = pe.matmul(ps[:, bank + 1, 0:256], hT[:, k, t * P:(t + 1) * P], win[:, k, D + 512:D_IN],
                                       start=(k == 0), stop=(k == KD - 1))
                    mm.then_inc(qkv_mm, 1)
                    if t:
                        qk_transposes(i, t - 1)
                qk_transposes(i, nt - 1)
            pe.wait_ge(g["win_ld"], 16)
            chunk(None)
            with pe.Fori(0, SEQ // CHUNK) as i:
                chunk(i)


def phase_recurrence(nc, env):
    g = env
    sem, arena, ps, small = g["sem"], g["arena"], g["ps"], g["small"]
    names = ["x", "r0", "r1", "g0", "g1", "t0", "t1", "d0", "d1"]
    b = arena_slices(arena, B0, [(n, TIME) for n in names] + [("gate", SEQ), ("gw", 4 * P)])
    gw = b["gw"].rearrange("p (q m) -> p q m", q=4)
    par = small[:, 0:NPAR]
    lam_all = small[:, 16:16 + 2 * C_RNN]
    neg_s = small[:, 32:32 + 2 * C_RNN]
    tmp = [small[:, 48 + 8 * n:56 + 8 * n] for n in range(6)]
    s_cur = small[:, 112:116]

    lam_ld, par_ld, gw_ld, gate_ld, zero = sem("c_lam_ld"), sem("c_par_ld"), sem("c_gw_ld"), sem("c_gate_ld"), sem("c_zero")
    sp_v, sp_a, cur, conv = sem("c_sp_v"), sem("c_sp_a"), sem("c_cur"), sem("c_conv")
    g_mm, g_ev, tanh_d, exp_d, sqrt_d = sem("c_g_mm"), sem("c_g_ev"), sem("c_tanh"), sem("c_exp"), sem("c_sqrt")
    frac, drive, scan, y_done, y_st = sem("c_frac"), sem("c_drive"), sem("c_scan"), sem("c_y"), sem("c_y_st")
    segs = [(0, CTX)] + [(CTX + j * 512, 512) for j in range(4)]

    with nc.Block() as block:
        @block.sync
        def _(sp):
            sp.dma_start(lam_all, g["lam"]).then_inc(lam_ld, 16)
            sp.wait_ge(zero, START + 1)
            with sp.Fori(0, C_RNN) as i:
                sp.wait_ge(y_done, START + 2 * i)
                sp.sem_inc(g["alone"], 1)
                sp.dma_start(par, g["rg_par"].rearrange("(c p) n -> c p n", p=P)[bass.ds(i, 1)]
                             .rearrange("c p n -> (c p) n")).then_inc(par_ld, 16)
                for d in range(2):
                    for q, w in enumerate((g["rg_wa"], g["rg_wx"])):
                        for h in range(2):
                            src = w[d].rearrange("(c h) i j -> c h i j", h=2)[bass.ds(i, 1), h]\
                                .rearrange("c i j -> (c i) j")
                            sp.dma_start(gw[64 * h:64 * h + 64, 2 * d + q, 64 * h:64 * h + 64], src).then_inc(gw_ld, 16)
                sp.dma_start(b["gate"], g["gate_d"][bass.ds(i, 1)].rearrange("c p t -> (c p) t")).then_inc(gate_ld, 16)
                sp.wait_ge(y_done, START + 2 * i + 2)
                sp.sem_inc(g["alone"], 1)
                sp.dma_start(g["yT_d"][bass.ds(i, 1)].rearrange("c p t -> (c p) t"), b["gate"]).then_inc(y_st, 16)
                sp.wait_ge(y_st, START + 16 * i + 16)
                sp.sem_inc(g["alone"], 1)

        @block.vector
        def _(dve):
            nc.vector.memset(gw, 0.0).then_inc(zero, 1)
            count = [0]

            def link(ins):
                count[0] += 1
                ins.then_inc(sp_v, 1)
                dve.wait_ge(sp_v, START + count[0])
            dve.wait_ge(lam_ld, START + 16)
            link(nc.vector.tensor_scalar(tmp[0], lam_all, -1.0, None, ALU.mult))
            link(nc.vector.tensor_tensor(tmp[1], tmp[0], lam_all, ALU.min))
            link(nc.vector.tensor_scalar(tmp[0], tmp[0], 0.0, None, ALU.max))
            dve.wait_ge(sp_a, START + 1)
            link(nc.vector.tensor_scalar(tmp[3], tmp[2], 2.0, None, ALU.add))
            link(nc.vector.reciprocal(tmp[4], tmp[3]))
            link(nc.vector.tensor_tensor(tmp[3], tmp[2], tmp[4], ALU.mult))
            link(nc.vector.tensor_tensor(tmp[4], tmp[3], tmp[3], ALU.mult))
            link(nc.vector.tensor_scalar(tmp[5], tmp[4], 1.0 / 17, 1.0 / 15, ALU.mult, ALU.add))
            for q in (13, 11, 9, 7, 5, 3, 1):
                link(nc.vector.tensor_tensor(tmp[5], tmp[5], tmp[4], ALU.mult))
                link(nc.vector.tensor_scalar(tmp[5], tmp[5], 1.0 / q, None, ALU.add))
            link(nc.vector.tensor_tensor(tmp[5], tmp[5], tmp[3], ALU.mult))
            link(nc.vector.scalar_tensor_tensor(tmp[5], tmp[5], 2.0, tmp[0], ALU.mult, ALU.add))
            link(nc.vector.tensor_scalar(neg_s, tmp[5], -8.0, None, ALU.mult))
            with dve.Fori(0, C_RNN) as i:
                dve.wait_ge(par_ld, START + 16 * i + 16)
                for d in range(2):
                    dve.wait_ge(exp_d, START + 2 * i)
                    for sgn in range(2):
                        nc.vector.tensor_scalar(s_cur[:, 2 * d + sgn:2 * d + sgn + 1],
                                                small[:, bass.ds(32 + d * C_RNN + i, 1)],
                                                -1.0 if sgn == 0 else 1.0, None, ALU.mult).then_inc(cur, 1)
                dve.wait_ge(drive, START + 4 * i)
                for q in range(CONV_W):
                    dve.wait_ge(conv, START + 8 * i + 2 * q)
                    for n, (lo, ln, at) in enumerate(((0, CTX, U_CTX), (CTX, SEQ, U_LAT))):
                        src = arena[:, bass.ds(UT0 + i * U_ROW + at - 2 + q, ln)]
                        dst = b["x"][:, lo:lo + ln]
                        if q == 0:
                            nc.vector.tensor_scalar(dst, src, par[:, 0:1], par[:, 4:5], ALU.mult, ALU.add)\
                                .then_inc(conv, 1)
                        else:
                            nc.vector.scalar_tensor_tensor(dst, src, par[:, q:q + 1], dst, ALU.mult, ALU.add)\
                                .then_inc(conv, 1)
                for d in range(2):
                    T, Dn, G, R = b[f"t{d}"], b[f"d{d}"], b[f"g{d}"], b[f"r{d}"]
                    dve.wait_ge(y_done, START + 2 * i)
                    dve.wait_ge(exp_d, START + 2 * i + d + 1)
                    nc.vector.tensor_tensor(Dn, R, R, ALU.mult).then_inc(frac, 1)
                    dve.wait_ge(frac, START + 4 * i + 2 * d + 1)
                    nc.vector.scalar_tensor_tensor(T, Dn, 1.0, T, ALU.add, ALU.mult).then_inc(frac, 1)
                    dve.wait_ge(g_ev, START + 20 * i + 10 * d + 10)
                    nc.vector.tensor_tensor(G, G, b["x"], ALU.mult).then_inc(drive, 1)
                for d in range(2):
                    T, Dn, G, R = b[f"t{d}"], b[f"d{d}"], b[f"g{d}"], b[f"r{d}"]
                    dve.wait_ge(sqrt_d, START + 2 * i + d + 1)
                    nc.vector.tensor_tensor(G, G, T, ALU.mult).then_inc(drive, 1)
                    dve.wait_ge(drive, START + 4 * i + 3 + d)
                    if d == 0:
                        nc.vector.tensor_tensor_scan(Dn, R, G, 0.0, ALU.mult, ALU.add).then_inc(scan, 1)
                    else:
                        nc.vector.tensor_tensor_scan(Dn[:, CTX - 1::-1], R[:, CTX - 1::-1], G[:, CTX - 1::-1], 0.0,
                                                     ALU.mult, ALU.add).then_inc(scan, 1)
                        dve.wait_ge(scan, START + 3 * i + 2)
                        nc.vector.tensor_tensor_scan(Dn[:, TIME - 1:CTX - 1:-1], R[:, TIME - 1:CTX - 1:-1],
                                                     G[:, TIME - 1:CTX - 1:-1], Dn[:, 0:1],
                                                     ALU.mult, ALU.add).then_inc(scan, 1)
                dve.wait_ge(scan, START + 3 * i + 3)
                dve.wait_ge(gate_ld, START + 16 * i + 16)
                nc.vector.tensor_tensor(b["d0"][:, CTX:TIME], b["d0"][:, CTX:TIME], b["d1"][:, CTX:TIME], ALU.add)\
                    .then_inc(y_done, 1)
                dve.wait_ge(y_done, START + 2 * i + 1)
                nc.vector.tensor_tensor(b["gate"], b["d0"][:, CTX:TIME], b["gate"], ALU.mult).then_inc(y_done, 1)

        @block.scalar
        def _(act):
            act.wait_ge(sp_v, START + 3)
            nc.scalar.activation(tmp[2], tmp[1], ACT.Exp).then_inc(sp_a, 1)
            with act.Fori(0, C_RNN) as i:
                for d in range(2):
                    for q in range(2):
                        dst = b[f"{'rg'[q]}{d}"]
                        if q == 0:
                            act.wait_ge(scan, START + 3 * i)
                        for n, (lo, ln) in enumerate(segs):
                            idx = (2 * d + q) * 5 + n
                            act.wait_ge(g_mm, START + 20 * i + idx + 1)
                            nc.scalar.activation(dst[:, lo:lo + ln], ps[:, idx % 4, 0:ln], ACT.Sigmoid,
                                                 bias=par[:, 5 + 2 * q + d:6 + 2 * q + d]).then_inc(g_ev, 1)
                act.wait_ge(cur, START + 4 * i + 4)
                act.wait_ge(g_ev, START + 20 * i + 20)
                for d in range(2):
                    nc.scalar.activation(b[f"t{d}"], b[f"r{d}"], ACT.Tanh, scale=s_cur[:, 2 * d:2 * d + 1])\
                        .then_inc(tanh_d, 1)
                act.wait_ge(tanh_d, START + 2 * i + 2)
                for d in range(2):
                    nc.scalar.activation(b[f"r{d}"], b[f"r{d}"], ACT.Exp, scale=s_cur[:, 2 * d + 1:2 * d + 2])\
                        .then_inc(exp_d, 1)
                act.wait_ge(exp_d, START + 2 * i + 2)
                for d in range(2):
                    act.wait_ge(frac, START + 4 * i + 2 * d + 2)
                    nc.scalar.activation(b[f"t{d}"], b[f"t{d}"], ACT.Sqrt).then_inc(sqrt_d, 1)

        @block.tensor
        def _(pe):
            with pe.Fori(0, C_RNN) as i:
                pe.wait_ge(gw_ld, START + 128 * i + 128)
                pe.wait_ge(conv, START + 8 * i + 8)
                for dq in range(4):
                    for n, (lo, ln) in enumerate(segs):
                        idx = dq * 5 + n
                        pe.wait_ge(g_ev, START + 20 * i + max(idx - 3, 0))
                        pe.matmul(ps[:, idx % 4, 0:ln], gw[:, dq, :], b["x"][:, lo:lo + ln], start=True, stop=True)\
                            .then_inc(g_mm, 1)


def phase_attention(nc, env):
    g = env
    sem, arena, ps, ps_row, small, idn = g["sem"], g["arena"], g["ps"], g["ps_row"], g["small"], g["idn"]
    b = arena_slices(arena, B0, [("mask0", KEYS), ("mask1", KEYS), ("q0", 512), ("q1", 512), ("s0", KEYS), ("s1", KEYS),
                                 ("pT0", KEYS), ("pT1", KEYS), ("o", 512)])
    sinks = small[:, 0:NH]
    mx = small[:, 8:16]
    nm = small[:, 16:24]
    den = small[:, 24:32]
    es = small[:, 32:40]
    rd = small[:, 40:48]
    mask_ld, q_ld, s_mm, s_max, nm_d, p_d = sem("d_mask_ld"), sem("d_q_ld"), sem("d_s_mm"), sem("d_s_max"), sem("d_nm"), sem("d_p")
    p_tr, p_ev, pv_mm = sem("d_p_tr"), sem("d_p_ev"), sem("d_pv")
    o_free = sem("d_o_free")
    es_d, es_e, den_d, o_d, o_st = sem("d_es"), sem("d_es_e"), sem("d_den"), sem("d_o"), g["plain_sem"]("d_o_st")

    with nc.Block() as block:
        @block.sync
        def _(sp):
            sp.dma_start(sinks, g["sink"]).then_inc(mask_ld, 16)
            with sp.Fori(0, T_LAT // 2) as i:
                for j in range(2):
                    sp.wait_ge(s_mm, START + 16 * i)
                    sp.wait_ge(s_max, START + 16 * i)
                    sp.sem_inc(g["alone"], 1)
                    kind = ((2 * i + j + 15) >> 4) + ((2 * i + j + 1) >> 4)
                    sp.dma_start(b[f"mask{j}"], g["masks"][bass.ds(kind, 1)].rearrange("m p k -> (m p) k")).then_inc(q_ld, 16)
                    sp.dma_start(b[f"q{j}"], g["qT_d"][bass.ds(2 * i + j, 1)].rearrange("n p d -> (n p) d")).then_inc(q_ld, 16)
                    sp.wait_ge(q_ld, START + 64 * i + 32 * j + 32)
                    sp.sem_inc(g["alone"], 1)

        @block.gpsimd
        def _(pool):
            with pool.Fori(0, T_LAT) as i:
                pool.wait_ge(o_d, START + i + 1)
                pool.sem_inc(g["alone"], 1)
                pool.dma_start(g["attn_d"][bass.ds(i, 1)].rearrange("n p d -> (n p) d"), b["o"]).then_inc(o_st, 16)
                pool.wait_ge(o_st, 16 * i + 16)
                pool.sem_inc(o_free, 1)

        @block.tensor
        def _(pe):
            def scores(i, j, h):
                t = 2 * i + j
                z, a = h // PAIRS, h % PAIRS
                n = i * 16 + j * NH + h
                if h == 0:
                    pe.wait_ge(q_ld, START + 64 * i + 32 * j + 32)
                pe.wait_ge(s_max, START + i * 16 + max(j * NH + h - 1, 0))
                q = b[f"q{j}"][:, a * P:(a + 1) * P]
                s0 = (h % 2) * 1024
                pe.matmul(ps_row[:, s0:s0 + CTX], q, arena[:, KT0 + z * K_ROW:KT0 + z * K_ROW + CTX], start=True, stop=True)
                k0 = KT0 + z * K_ROW + K_LAT - P
                pe.matmul(ps_row[:, s0 + CTX:s0 + 512], q, arena[:, bass.ds(k0 + t * P, 256)], start=True, stop=True)
                pe.matmul(ps_row[:, s0 + 512:s0 + KEYS], q, arena[:, bass.ds(k0 + t * P + 256, P)],
                          start=True, stop=True).then_inc(s_mm, 1)

            def transposes(i, j, h):
                n = i * 16 + j * NH + h
                pe.wait_ge(p_d, START + n + 1)
                pe.wait_ge(p_ev, START + 2 * n)
                for q in range(KEYS // P):
                    mm = pe.transpose(ps_row[:, 2048 + q * P:2048 + (q + 1) * P], b[f"s{h % 2}"][:, q * P:(q + 1) * P], idn[:])
                mm.then_inc(p_tr, 1)

            def values(i, j, h):
                t = 2 * i + j
                n = i * 16 + j * NH + h
                z = h // PAIRS
                pe.wait_ge(p_ev, START + 2 * n + 2)
                if h == 0:
                    pe.wait_ge(o_d, START + 2 * i + j)
                for q in range(KEYS // P):
                    v = arena[:, V0 + q * P + z * HD:V0 + q * P + (z + 1) * HD] if q < 2 else \
                        arena[:, bass.ds(V0 + q * P + z * HD + t * P, HD)]
                    mm = pe.matmul(ps[:, 6, h * HD:(h + 1) * HD], b[f"pT{h % 2}"][:, q * P:(q + 1) * P], v,
                                   start=(q == 0), stop=(q == KEYS // P - 1))
                mm.then_inc(pv_mm, 1)
            with pe.Fori(0, T_LAT // 2) as i:
                for j in range(2):
                    scores(i, j, 0)
                    for h in range(NH):
                        if h + 1 < NH:
                            scores(i, j, h + 1)
                        transposes(i, j, h)
                        if h:
                            values(i, j, h - 1)
                    values(i, j, NH - 1)

        @block.vector
        def _(dve):
            dve.wait_ge(mask_ld, START + 16)

            def smax(i, j, h):
                t = 2 * i + j
                n = i * 16 + j * NH + h
                dve.wait_ge(s_mm, START + n + 1)
                if h == 0:
                    dve.wait_ge(q_ld, START + 64 * i + 32 * j + 32)
                dve.wait_ge(p_tr, START + i * 16 + max(j * NH + h - 1, 0))
                dve.sem_inc(g["alone"], 1)
                nc.vector.tensor_tensor_reduce(b[f"s{h % 2}"], ps_row[:, (h % 2) * 1024:(h % 2) * 1024 + KEYS],
                                               b[f"mask{j}"],
                                               1.0, NEG, ALU.add, ALU.max, mx[:, h:h + 1]).then_inc(s_max, 1)
                dve.wait_ge(s_max, START + n + 1)
                if h == 0:
                    dve.wait_ge(es_d, START + 2 * (2 * i + j))
                nc.vector.tensor_scalar(nm[:, h:h + 1], mx[:, h:h + 1], sinks[:, h:h + 1], -1.0, ALU.max, ALU.mult)\
                    .then_inc(nm_d, 1)

            def copy_pT(i, j, h):
                n = i * 16 + j * NH + h
                dve.wait_ge(p_tr, START + n + 1)
                dve.wait_ge(pv_mm, START + i * 16 + max(j * NH + h - 1, 0))
                nc.vector.tensor_copy(b[f"pT{h % 2}"][:, 512:KEYS], ps_row[:, 2048 + 512:2048 + KEYS]).then_inc(p_ev, 1)
            with dve.Fori(0, T_LAT // 2) as i:
                for j in range(2):
                    t = 2 * i + j
                    for h in range(NH):
                        smax(i, j, h)
                        if h:
                            copy_pT(i, j, h - 1)
                    copy_pT(i, j, NH - 1)
                    dve.wait_ge(nm_d, START + NH * t + NH)
                    nc.vector.tensor_tensor(es, sinks, nm, ALU.add).then_inc(es_d, 1)
                    dve.wait_ge(es_d, START + 2 * t + 2)
                    nc.vector.tensor_tensor(den, den, es, ALU.add).then_inc(den_d, 1)
                    dve.wait_ge(den_d, START + 2 * t + 1)
                    nc.vector.reciprocal(rd, den).then_inc(den_d, 1)
                    dve.wait_ge(den_d, START + 2 * t + 2)
                    dve.wait_ge(pv_mm, START + NH * t + NH)
                    dve.wait_ge(o_free, START + t)
                    nc.vector.tensor_tensor(b["o"].rearrange("p (h d) -> p h d", h=NH),
                                            ps[:, 6, :].rearrange("p (h d) -> p h d", h=NH),
                                            rd.rearrange("p (h o) -> p h o", o=1).to_broadcast([P, NH, HD]),
                                            ALU.mult).then_inc(o_d, 1)

        @block.scalar
        def _(act):
            def copy_pT(i, j, h):
                n = i * 16 + j * NH + h
                act.wait_ge(p_tr, START + n + 1)
                act.wait_ge(pv_mm, START + i * 16 + max(j * NH + h - 1, 0))
                nc.scalar.activation(b[f"pT{h % 2}"][:, 0:512], ps_row[:, 2048:2048 + 512], ACT.Copy).then_inc(p_ev, 1)
            with act.Fori(0, T_LAT // 2) as i:
                for j in range(2):
                    t = 2 * i + j
                    for h in range(NH):
                        n = i * 16 + j * NH + h
                        act.wait_ge(nm_d, START + n + 1)
                        if h == 0:
                            act.wait_ge(den_d, START + 2 * t)
                        nc.scalar.activation(b[f"s{h % 2}"], b[f"s{h % 2}"], ACT.Exp, bias=nm[:, h:h + 1],
                                             accum_out=den[:, h:h + 1]).then_inc(p_d, 1)
                        if h:
                            copy_pT(i, j, h - 1)
                    copy_pT(i, j, NH - 1)
                    act.wait_ge(es_d, START + 2 * t + 1)
                    act.wait_ge(p_d, START + NH * t + NH)
                    nc.scalar.activation(es, es, ACT.Exp).then_inc(es_d, 1)


def phase_output(nc, env):
    g = env
    sem, arena, ps, ps_row, small, idn = g["sem"], g["arena"], g["ps"], g["ps_row"], g["small"], g["idn"]
    b = arena_slices(arena, 0, [("logits", T_LAT * 36), ("wo", KD * D), ("g1", D), ("sc2", D), ("sh2", D), ("l1g", D), ("l1b", D),
                                ("wr", KD * 36), ("br", 36), ("gnc", KD), ("ones", 1), ("mh", 2), ("yT", 512), ("ysq", 512),
                                ("at", 512), ("asq", 512), ("aT", 512), ("xt", D), ("t0", D), ("t1", D), ("x1", D), ("x1n", D),
                                ("h2", D), ("h2T", D), ("w0", D)])
    wo = b["wo"].rearrange("p (k n) -> p k n", k=KD)
    wr = b["wr"].rearrange("p (k n) -> p k n", k=KD)
    ss = small[:, 0:2]
    ssv = small[:, 2:4]
    sr = small[:, 4:6]
    st = small[:, 8:20]
    mv = small[:, 20:22]
    ve = small[:, 22:23]
    rs = small[:, 23:24]
    w_ld, in_ld, x_st, h_st = sem("e_w_ld"), sem("e_in_ld"), sem("e_x_st"), sem("e_h_st")
    w_ok, sq, ssm, ss_d, pw, a_tr, a_ev = sem("e_w_ok"), sem("e_sq"), sem("e_ssm"), sem("e_ss"), sem("e_pw"), sem("e_a_tr"), sem("e_a_ev")
    o_mm, o_act, v, pool_d, h_tr, h_ev, r_mm, lg = (sem("e_o_mm"), sem("e_o_act"), sem("e_v"), sem("e_pool"), sem("e_h_tr"),
                                                    sem("e_h_ev"), sem("e_r_mm"), sem("e_lg"))
    p_ok = sem("e_p_ok")
    NV = 15

    def row(src):
        return src.to_broadcast([P, src.shape[1]])
    with nc.Block() as block:
        @block.sync
        def _(sp):
            sp.dma_start(wo, g["w_out"].rearrange("(k p) n -> p k n", p=P)).then_inc(w_ld, 16)
            for name, src in (("g1", g["mod_rows"][0:1, 2 * D:3 * D]), ("sh2", g["mod_rows"][0:1, 3 * D:4 * D]),
                              ("sc2", g["mod_rows"][0:1, 4 * D:5 * D]), ("l1g", g["ln1"][0:1, :]),
                              ("l1b", g["ln1"][1:2, :]), ("br", g["router_b"])):
                sp.dma_start(b[name], row(src)).then_inc(w_ld, 16)
            sp.dma_start(wr, g["router"].rearrange("(k p) n -> p k n", p=P)).then_inc(w_ld, 16)
            sp.dma_start(b["gnc"], g["gn"]).then_inc(w_ld, 16)
            with sp.Fori(0, T_LAT) as i:
                sp.wait_ge(o_act, START + i)
                sp.sem_inc(g["alone"], 1)
                sp.wait_ge(v, START + NV * i)
                sp.sem_inc(g["alone"], 1)
                sp.dma_start(b["yT"].rearrange("p (c t) -> p c t", c=C_RNN),
                             g["yT_d"][:, :, bass.ds(i * P, P)].rearrange("c p t -> p c t")).then_inc(in_ld, 16)
                sp.dma_start(b["at"], g["attn_d"][bass.ds(i, 1)].rearrange("n p d -> (n p) d")).then_inc(in_ld, 16)
                sp.dma_start(b["xt"], g["x"][bass.ds(i * P, P), :]).then_inc(in_ld, 16)
                sp.wait_ge(v, START + NV * i + 11)
                sp.wait_ge(in_ld, START + 48 * i + 48)
                sp.sem_inc(g["alone"], 1)
                sp.dma_start(g["x1_d"][bass.ds(i * P, P), :], b["x1"]).then_inc(x_st, 16)
                sp.wait_ge(v, START + NV * i + 15)
                sp.wait_ge(x_st, START + 16 * i + 16)
                sp.sem_inc(g["alone"], 1)
                sp.dma_start(g["h2_d"][bass.ds(i * P, P), :], b["h2"]).then_inc(h_st, 16)
                sp.wait_ge(h_st, START + 16 * i + 16)
                sp.sem_inc(g["alone"], 1)

        @block.gpsimd
        def _(pool):
            nc.gpsimd.memset(b["mh"], -0.5).then_inc(p_ok, 1)
            nc.gpsimd.memset(b["ones"], 1.0).then_inc(p_ok, 1)
            pool.wait_ge(p_ok, START + 2)
            with pool.Fori(0, T_LAT) as i:
                pool.wait_ge(v, START + NV * i + 1)
                pool.sem_inc(g["alone"], 1)
                nc.gpsimd.tensor_tensor(sr, ssv, b["mh"], ALU.pow).then_inc(pw, 1)
                for n in (7, 12):
                    pool.wait_ge(v, START + NV * i + n)
                    pool.sem_inc(g["alone"], 1)
                    nc.gpsimd.tensor_tensor(rs, ve, b["mh"][:, 0:1], ALU.pow).then_inc(pw, 1)

        @block.vector
        def _(dve):
            dve.wait_ge(w_ld, START + 16 * 9)
            for k in range(KD):
                nc.vector.tensor_scalar(wo[:, k, :], wo[:, k, :], b["gnc"][:, k:k + 1], None, ALU.mult).then_inc(w_ok, 1)
            nc.vector.tensor_scalar(b["sc2"], b["sc2"], 1.0, None, ALU.add).then_inc(w_ok, 1)
            dve.wait_ge(w_ok, START + KD + 1)
            with dve.Fori(0, T_LAT) as i:
                base = NV * i
                step = [0]

                def link(ins):
                    step[0] += 1
                    ins.then_inc(v, 1)
                    dve.wait_ge(v, START + base + step[0])
                dve.wait_ge(sq, START + 2 * i + 2)
                dve.wait_ge(ssm, START + i + 1)
                nc.vector.tensor_copy(ss[:, 0:1], ps[:, 7, 64:65]).then_inc(ss_d, 1)
                dve.wait_ge(ss_d, START + i + 1)
                link(nc.vector.tensor_scalar(ssv, ss, 1.0 / 512, EPS, ALU.mult, ALU.add))
                dve.wait_ge(pw, START + 3 * i + 1)
                dve.wait_ge(o_mm, START + i + 1)
                dve.wait_ge(o_act, START + i + 1)
                link(nc.vector.scalar_tensor_tensor(b["t1"], ps_row[:, 2048:3072], sr[:, 1:2], b["t0"], ALU.mult, ALU.add))
                link(nc.vector.tensor_tensor(b["t1"], b["t1"], b["g1"], ALU.mult))
                link(nc.vector.scalar_tensor_tensor(b["t1"], b["xt"], ALPHA, b["t1"], ALU.mult, ALU.add))
                link(nc.vector.bn_stats(st[:, 0:6], b["t1"][:, 0:512]))
                nc.vector.bn_stats(st[:, 6:12], b["t1"][:, 512:1024]).then_inc(lg, 1)
                dve.wait_ge(lg, START + 4 * i + 1)
                dve.sem_inc(g["alone"], 1)
                link(nc.vector.bn_aggr(mv, st.rearrange("p (a s) -> p a s", a=2)))
                link(nc.vector.tensor_scalar(ve, mv[:, 1:2], EPS, None, ALU.add))
                dve.wait_ge(pw, START + 3 * i + 2)
                link(nc.vector.tensor_scalar(b["t1"], b["t1"], mv[:, 0:1], rs, ALU.subtract, ALU.mult))
                link(nc.vector.tensor_tensor(b["t1"], b["t1"], b["l1g"], ALU.mult))
                dve.wait_ge(x_st, START + 16 * i)
                link(nc.vector.tensor_tensor(b["x1"], b["t1"], b["l1b"], ALU.add))
                nc.vector.bn_stats(st[:, 0:6], b["x1"][:, 0:512]).then_inc(lg, 1)
                nc.vector.bn_stats(st[:, 6:12], b["x1"][:, 512:1024]).then_inc(lg, 1)
                dve.wait_ge(lg, START + 4 * i + 3)
                dve.sem_inc(g["alone"], 1)
                link(nc.vector.bn_aggr(mv, st.rearrange("p (a s) -> p a s", a=2)))
                link(nc.vector.tensor_scalar(ve, mv[:, 1:2], EPS, None, ALU.add))
                dve.wait_ge(pw, START + 3 * i + 3)
                link(nc.vector.tensor_scalar(b["x1n"], b["x1"], mv[:, 0:1], rs, ALU.subtract, ALU.mult))
                link(nc.vector.tensor_tensor(b["x1n"], b["x1n"], b["sc2"], ALU.mult))
                dve.wait_ge(h_st, START + 16 * i)
                dve.wait_ge(h_tr, START + 2 * i)
                link(nc.vector.tensor_tensor(b["h2"], b["x1n"], b["sh2"], ALU.add))
                dve.wait_ge(r_mm, START + i + 1)
                nc.vector.tensor_tensor(arena[:, bass.ds(i * 36, 36)], ps[:, 7, 0:36], b["br"], ALU.add).then_inc(lg, 1)

        @block.scalar
        def _(act):
            with act.Fori(0, T_LAT) as i:
                act.wait_ge(in_ld, START + 48 * i + 48)
                act.wait_ge(ssm, START + i)
                nc.scalar.activation(b["ysq"], b["yT"], ACT.Square).then_inc(sq, 1)
                act.wait_ge(v, START + NV * i)
                nc.scalar.activation(b["asq"], b["at"], ACT.Square, accum_out=ss[:, 1:2]).then_inc(sq, 1)
                act.wait_ge(a_tr, START + i + 1)
                nc.scalar.activation(b["aT"], ps[:, 6, :], ACT.Copy).then_inc(a_ev, 1)
                act.wait_ge(o_mm, START + i + 1)
                act.wait_ge(pw, START + 3 * i + 1)
                nc.scalar.activation(b["t0"], ps_row[:, 1024:2048], ACT.Copy, scale=sr[:, 0:1]).then_inc(o_act, 1)
                for n in range(2):
                    act.wait_ge(h_tr, START + 2 * i + n + 1)
                    if n == 0:
                        act.wait_ge(r_mm, START + i)
                    nc.scalar.activation(b["h2T"][:, n * 512:(n + 1) * 512], ps[:, n, :], ACT.Copy).then_inc(h_ev, 1)

        @block.tensor
        def _(pe):
            pe.wait_ge(p_ok, START + 2)
            pe.wait_ge(w_ok, START + KD + 1)
            with pe.Fori(0, T_LAT) as i:
                pe.wait_ge(sq, START + 2 * i + 2)
                pe.wait_ge(lg, START + 4 * i)
                for c in range(C_RNN):
                    mm = pe.matmul(ps[:, 7, 64:65], b["ysq"][:, c * P:(c + 1) * P], b["ones"], start=(c == 0), stop=(c == C_RNN - 1))
                mm.then_inc(ssm, 1)
                for c in range(C_RNN):
                    mm = pe.transpose(ps[:, 6, c * P:(c + 1) * P], b["at"][:, c * P:(c + 1) * P], idn[:])
                mm.then_inc(a_tr, 1)
                for k in range(C_RNN):
                    for n in range(2):
                        pe.matmul(ps[:, 2 + n, :], b["yT"][:, k * P:(k + 1) * P], wo[:, k, n * 512:(n + 1) * 512],
                                  start=(k == 0), stop=(k == C_RNN - 1))
                pe.wait_ge(a_ev, START + i + 1)
                for k in range(C_RNN):
                    for n in range(2):
                        mm = pe.matmul(ps[:, 4 + n, :], b["aT"][:, k * P:(k + 1) * P], wo[:, C_RNN + k, n * 512:(n + 1) * 512],
                                       start=(k == 0), stop=(k == C_RNN - 1))
                mm.then_inc(o_mm, 1)
                pe.wait_ge(v, START + NV * i + 15)
                for n in range(2):
                    pe.wait_ge(h_ev, START + 2 * i)
                    for c in range(4):
                        mm = pe.transpose(ps[:, n, c * P:(c + 1) * P], b["h2"][:, (4 * n + c) * P:(4 * n + c + 1) * P], idn[:])
                    mm.then_inc(h_tr, 1)
                pe.wait_ge(h_ev, START + 2 * i + 2)
                pe.wait_ge(ss_d, START + i + 1)
                for k in range(KD):
                    mm = pe.matmul(ps[:, 7, 0:36], b["h2T"][:, k * P:(k + 1) * P], wr[:, k, :], start=(k == 0), stop=(k == KD - 1))
                mm.then_inc(r_mm, 1)


def phase_route(nc, env):
    g = env
    sem, arena, ps, ps_row, idn = g["sem"], g["arena"], g["ps"], g["ps_row"], g["idn"]
    T = T_LAT
    names = [("logits", T * 36), ("pad8", T * 8), ("gm8", T * 8), ("gi8", T * 8), ("gif", T), ("goh", T * NG),
             ("elm", T * NE), ("em8", T * 8), ("ei8", T * 8), ("eif", 2 * T), ("gex", T * NG), ("gsum", T), ("pg", T),
             ("dif", T), ("q", T), ("oh0", T * NE), ("oh1", T * NE), ("ohs", T * NE), ("base", (T + 1) * NE),
             ("rank", T * NE), ("sel", T * NE), ("slotf", 2 * T), ("nbi", NE), ("nb", NE), ("pend", NE), ("pst", NE),
             ("one32", NE), ("ones", P), ("tri", P), ("iota", 64), ("tok", T), ("ge", 64 * NE), ("has", NE), ("rk", NE), ("rend", NE), ("ebf", 64), ("nw", 64),
             ("st_i", P), ("st_f", P)]
    b = arena_slices(arena, 0, names)
    v3 = lambda name, t, n: b[name].rearrange("p (t n) -> p t n", t=t)
    slot_i, gates, tab, gidx = g["slot_i"], g["gates"], g["blk_tab"], g["gidx"]
    f_ld, v, act_d, mm, scat, tab_ld, tr = sem("f_ld"), sem("f_v"), sem("f_act"), sem("f_mm"), g["plain_sem"]("f_scat"), sem("f_tab_ld"), sem("f_tr")
    mark = {}

    with nc.Block() as block:
        @block.vector
        def _(dve):
            n = [0]

            def link(ins, name=None):
                n[0] += 1
                ins.then_inc(v, 1)
                dve.wait_ge(v, START + n[0])
                if name:
                    mark[name] = n[0]
            V = nc.vector
            lg = v3("logits", T, 36)
            link(V.memset(b["pad8"], NEG))
            link(V.memset(b["one32"], 1.0))
            link(V.memset(b["ones"], 1.0))
            link(V.memset(b["base"][:, 0:NE], 0.0))
            link(V.tensor_copy(v3("pad8", T, 8)[:, :, 0:NG], lg[:, :, 0:NG]))
            for t in range(T):
                link(V.max(v3("gm8", T, 8)[:, t, :], v3("pad8", T, 8)[:, t, :]))
                link(V.max_index(v3("gi8", T, 8)[:, t, :].bitcast(U32), v3("gm8", T, 8)[:, t, :], v3("pad8", T, 8)[:, t, :]))
            link(V.tensor_copy(b["gif"], v3("gi8", T, 8)[:, :, 0].bitcast(U32)))
            dve.wait_ge(f_ld, START + 48)
            io4 = b["iota"][:, 0:NG].rearrange("p (o n) -> p o n", o=1).to_broadcast([P, T, NG])
            link(V.tensor_tensor(v3("goh", T, NG), io4, b["gif"].rearrange("p (t o) -> p t o", o=1).to_broadcast([P, T, NG]),
                                 ALU.is_equal))
            link(V.tensor_scalar(b["goh"], b["goh"], 1.0, -NEG, ALU.subtract, ALU.mult))
            link(V.tensor_tensor(b["elm"].rearrange("p (t g e) -> p t g e", t=T, g=NG),
                                 lg[:, :, NG:36].rearrange("p t (g e) -> p t g e", g=NG),
                                 v3("goh", T, NG).rearrange("p t (g o) -> p t g o", o=1).to_broadcast([P, T, NG, EPG]), ALU.add))
            for t in range(T):
                link(V.max(v3("em8", T, 8)[:, t, :], v3("elm", T, NE)[:, t, :]))
                link(V.max_index(v3("ei8", T, 8)[:, t, :].bitcast(U32), v3("em8", T, 8)[:, t, :], v3("elm", T, NE)[:, t, :]))
            link(V.tensor_copy(b["eif"].rearrange("p (k t) -> p t k", k=2), v3("ei8", T, 8)[:, :, 0:2].bitcast(U32)))
            io32 = b["iota"][:, 0:NE].rearrange("p (o n) -> p o n", o=1).to_broadcast([P, T, NE])
            for k in range(2):
                idx = b["eif"][:, k * T:(k + 1) * T].rearrange("p (t o) -> p t o", o=1).to_broadcast([P, T, NE])
                link(V.tensor_tensor(v3(f"oh{k}", T, NE), io32, idx, ALU.is_equal))
            link(V.tensor_tensor(b["ohs"], b["oh0"], b["oh1"], ALU.add), "onehot")
            link(V.tensor_tensor(v3("gex", T, NG), lg[:, :, 0:NG], v3("gm8", T, 8)[:, :, 0:1].to_broadcast([P, T, NG]),
                                 ALU.subtract))
            link(V.tensor_tensor(b["dif"], v3("em8", T, 8)[:, :, 1], v3("em8", T, 8)[:, :, 0], ALU.subtract), "exps")
            dve.wait_ge(mm, START + 2)
            for t in range(T):
                link(V.tensor_tensor(b["base"][:, (t + 1) * NE:(t + 2) * NE], b["base"][:, t * NE:(t + 1) * NE],
                                     ps[:, 1, t * NE:(t + 1) * NE], ALU.add))
            cnt = b["base"][:, T * NE:(T + 1) * NE]
            link(V.tensor_tensor(b["rank"], ps[:, 0, :], b["base"][:, 0:T * NE], ALU.add))
            link(V.tensor_scalar(b["nbi"].bitcast(I32), cnt, float(P - 1), None, ALU.add))
            link(V.tensor_scalar(b["nbi"].bitcast(I32), b["nbi"].bitcast(I32), 7, None, ALU.arith_shift_right))
            link(V.tensor_copy(b["nb"], b["nbi"].bitcast(I32)))
            link(V.tensor_tensor_scan(b["pend"], b["one32"], b["nb"], 0.0, ALU.mult, ALU.add))
            link(V.tensor_tensor(b["pst"], b["pend"], b["nb"], ALU.subtract))
            link(V.tensor_scalar(b["pst"], b["pst"], float(P), None, ALU.mult))
            link(V.tensor_tensor(v3("rank", T, NE), v3("rank", T, NE),
                                 b["pst"].rearrange("p (o n) -> p o n", o=1).to_broadcast([P, T, NE]), ALU.add))
            for k in range(2):
                link(V.tensor_tensor(b["sel"], b["rank"], b[f"oh{k}"], ALU.mult))
                link(V.tensor_reduce(b["slotf"][:, k * T:(k + 1) * T], v3("sel", T, NE), AX_X, ALU.add))
            link(V.tensor_copy(slot_i[:], b["slotf"]), "slots")
            one = lambda ap: ap[0:1]

            def count_le(dst, n, limit):
                link(V.tensor_tensor(one(b["ge"])[:, 0:n * NE].rearrange("p (b e) -> p b e", b=n),
                                     one(b["iota"])[:, 0:n].rearrange("p (b o) -> p b o", o=1).to_broadcast([1, n, NE]),
                                     one(limit).rearrange("p (o e) -> p o e", o=1).to_broadcast([1, n, NE]), ALU.is_ge))
                if dst is not None:
                    link(V.tensor_reduce(dst, one(b["ge"])[:, 0:n * NE].rearrange("p (b e) -> p b e", b=n), AX_X, ALU.add))
            link(V.tensor_scalar(one(b["has"]), one(b["nb"]), 0.5, None, ALU.is_ge))
            link(V.tensor_tensor_scan(one(b["rk"]), one(b["one32"]), one(b["has"]), 0.0, ALU.mult, ALU.add))
            link(V.tensor_copy(tab[:, TAB_NR:TAB_NR + 1], one(b["rk"])[:, NE - 1:NE]))
            count_le(one(b["ebf"])[:, 0:NE], NE, b["rk"])
            link(V.tensor_scalar(tab[:, TAB_EXPERT:TAB_EXPERT + NE], one(b["ebf"])[:, 0:NE], float(NE - 1), None, ALU.min))
            link(V.tensor_scalar(one(b["rk"]), one(b["rk"]), -1.0, None, ALU.add))
            count_le(None, NE, b["rk"])
            gev = one(b["ge"])[:, 0:NE * NE].rearrange("p (b e) -> p b e", b=NE)
            link(V.tensor_tensor(gev, gev, one(b["nb"]).rearrange("p (o e) -> p o e", o=1).to_broadcast([1, NE, NE]), ALU.mult))
            link(V.tensor_reduce(one(b["rend"]), gev, AX_X, ALU.add))
            count_le(one(b["ebf"]), 64, b["rend"])
            link(V.tensor_scalar(tab[:, TAB_RANK:TAB_RANK + 64], one(b["ebf"]), float(NE - 1), None, ALU.min))
            link(V.tensor_scalar(tab[:, TAB_BUF:TAB_BUF + 64], tab[:, TAB_RANK:TAB_RANK + 64], 1, None, ALU.bitwise_and))
            nw = one(b["nw"])
            link(V.memset(nw, 1.0))
            link(V.tensor_tensor(nw[:, 1:64], one(b["ebf"])[:, 1:64], one(b["ebf"])[:, 0:63], ALU.not_equal))
            link(V.tensor_scalar(one(b["ebf"]), one(b["ebf"]), one(b["rk"])[:, NE - 1:NE], None, ALU.is_lt))
            link(V.tensor_tensor(tab[:, TAB_NEW:TAB_NEW + 64], nw, one(b["ebf"]), ALU.mult))
            for less in range(3):
                link(V.tensor_scalar(tab[:, TAB_NB + less:TAB_NB + less + 1], one(b["pend"])[:, NE - 1:NE], float(-less), None, ALU.add))
            link(V.tensor_scalar(tab[:, TAB_FREE:TAB_FREE + 1], one(b["pend"])[:, NE - 1:NE], -1.0, 64.0, ALU.mult, ALU.add))
            dve.wait_ge(act_d, START + 2)
            link(V.tensor_reduce(b["gsum"], v3("gex", T, NG), AX_X, ALU.add))
            link(V.reciprocal(b["pg"], b["gsum"]))
            link(V.tensor_scalar(b["q"], b["dif"], 1.0, None, ALU.add))
            link(V.reciprocal(b["q"], b["q"]))
            link(V.tensor_tensor(gates[:, 0:T], b["q"], b["pg"], ALU.mult))
            link(V.tensor_tensor(gates[:, T:2 * T], gates[:, 0:T], b["dif"], ALU.mult))
            dve.wait_ge(tab_ld, START + 16)
            link(V.tensor_copy(b["st_f"][0:64, :], b["st_i"][0:64, :].bitcast(I32)), "slot_tok")
            dve.wait_ge(tr, START + 1)
            link(V.tensor_copy(gidx[:, 0:64], ps[:, 2, 0:64]))

        @block.scalar
        def _(act):
            act.wait_ge(v, START + mark["exps"])
            nc.scalar.activation(b["gex"], b["gex"], ACT.Exp).then_inc(act_d, 1)
            nc.scalar.activation(b["dif"], b["dif"], ACT.Exp).then_inc(act_d, 1)

        @block.tensor
        def _(pe):
            pe.wait_ge(f_ld, START + 48)
            pe.wait_ge(v, START + mark["onehot"])
            pe.matmul(ps[:, 0, :], b["tri"], b["ohs"], start=True, stop=True).then_inc(mm, 1)
            pe.matmul(ps[:, 1, :], b["ones"], b["ohs"], start=True, stop=True).then_inc(mm, 1)
            pe.wait_ge(v, START + mark["slot_tok"])
            pe.transpose(ps[:, 2, 0:64], b["st_f"][0:64, :], idn[0:64, 0:64]).then_inc(tr, 1)

        @block.gpsimd
        def _(pool):
            pool.wait_ge(f_ld, START + 48)
            pool.wait_ge(v, START + mark["slots"])
            for k in range(2):
                for t in range(T):
                    pool.indirect_dma_start(g["slot_tok_d"], bass.IndirectOffsetOnAxis(slot_i[:, k * T + t:k * T + t + 1], 0),
                                            b["tok"][:, t:t + 1].bitcast(I32), None).then_inc(scat, 16)
            pool.wait_ge(scat, 16 * 2 * T)

        @block.sync
        def _(sp):
            sp.dma_start(b["tri"], g["tri"]).then_inc(f_ld, 16)
            sp.dma_start(b["iota"], g["iota"]).then_inc(f_ld, 16)
            sp.dma_start(b["tok"].bitcast(I32), g["tok_id"]).then_inc(f_ld, 16)
            sp.wait_ge(scat, 16 * 2 * T)
            sp.dma_start(b["st_i"][0:64, :].bitcast(I32), g["slot_tok_d"].rearrange("(a b) o -> a (b o)", a=64)).then_inc(tab_ld, 16)


def phase_experts(nc, env):
    g = env
    sem, arena, ps, ps_row, idn = g["sem"], g["arena"], g["ps"], g["ps_row"], g["idn"]
    tab, gidx = g["blk_tab"], g["gidx"]
    W13 = 2 * KD * D_EXP
    W2 = KE * D
    WSZ = W13 + W2
    PIECE = 2048
    N13, N2 = W13 // PIECE, W2 // PIECE
    b = arena_slices(arena, 0, [("whi", WSZ), ("wlo", WSZ), ("st", WSZ), ("x0", D), ("x1", D), ("xh", D // 2), ("xl", D // 2),
                                ("s", D_EXP), ("h", D_EXP), ("hh", D_EXP // 2), ("hl", D_EXP // 2), ("g2", D), ("y0", D),
                                ("zero", D)])
    whi, wlo, xh, xl, hh, hl = (b[n].bitcast(F16) for n in ("whi", "wlo", "xh", "xl", "hh", "hl"))
    ix = g["stack"].enter_context(nc.sbuf_tensor("ix", [P, 2], I32))
    st_ld = [sem("g_st_ld0"), sem("g_st_ld1"), sem("g_st_ld2"), sem("g_st_ld3"), sem("g_st_ld4"), sem("g_st_ld5")]
    hi13, lo13, hi2, lo2 = sem("g_hi13"), sem("g_lo13"), sem("g_hi2"), sem("g_lo2")
    g2_ld, x_ix, x_ld, x_tr, x_hi, x_lo = (sem("g_g2_ld"), sem("g_x_ix"), g["plain_sem"]("g_x_ld"), sem("g_x_tr"),
                                           sem("g_x_hi"), sem("g_x_lo"))
    up_mm, silu_d, h_d, h_tr, h_hi, h_lo = (sem("g_up_mm"), sem("g_silu"), sem("g_h"), sem("g_h_tr"), sem("g_h_hi"),
                                            sem("g_h_lo"))
    y_mm, y_ev, y_st = sem("g_y_mm"), sem("g_y_ev"), sem("g_y_st")
    zero_d, z_st = sem("g_zero"), sem("g_z_st")

    def blocks(eng):
        return eng.value_load(tab[0:1, TAB_NB:TAB_NB + 1], min_val=32, max_val=MAX_BLOCKS - 1)

    def rank_of(eng, n):
        return eng.value_load(tab[0:1, bass.ds(n + TAB_RANK, 1)], min_val=0, max_val=NE - 1)

    def buffer_of(eng, n):
        return eng.value_load(tab[0:1, bass.ds(n + TAB_BUF, 1)], min_val=0, max_val=1)

    def starts_rank(eng, n):
        return eng.value_load(tab[0:1, bass.ds(n + TAB_NEW, 1)], min_val=0, max_val=1)

    def part(buf, whole, at, size):
        return whole[:, bass.ds(buf * WSZ + at, size)] if not isinstance(buf, int) else \
            whole[:, buf * WSZ + at:buf * WSZ + at + size]

    with nc.Block() as block:
        @block.sync
        def _(sp):
            sp.dma_start(b["g2"], g["mod_rows"][0:1, 5 * D:6 * D].to_broadcast([P, D])).then_inc(g2_ld, 16)
            ranks = sp.value_load(tab[0:1, TAB_NR:TAB_NR + 1], min_val=2, max_val=NE)

            def pieces(r, e):
                for n in range(N13 + N2):
                    if n < N13:
                        src = g[("w1", "w3")[n // (N13 // 2)]][bass.ds(e, 1)].rearrange("e (k p) n -> p (e k) n", p=P)
                        k0, cols = n % (N13 // 2) * (PIECE // D_EXP), D_EXP
                    else:
                        src = g["w2"][bass.ds(e, 1)].rearrange("e (k p) n -> p (e k) n", p=P)
                        k0, cols = (n - N13) * (PIECE // D), D
                    if r is not None:
                        done = (lo13, N13 * (r - 1) + n + 1) if n < N13 else (lo2, N2 * (r - 1) + n - N13 + 1)
                        sp.wait_ge(done[0], START + done[1])
                        sp.sem_inc(g["alone"], 1)
                    sp.dma_start(b["st"][:, n * PIECE:(n + 1) * PIECE].rearrange("p (k n) -> p k n", n=cols),
                                 src[:, k0:k0 + PIECE // cols, :]).then_inc(st_ld[n], 16)
            pieces(None, sp.value_load(tab[0:1, TAB_EXPERT:TAB_EXPERT + 1], min_val=0, max_val=NE - 1))
            with sp.Fori(1, ranks) as r:
                pieces(r, sp.value_load(tab[0:1, bass.ds(r + TAB_EXPERT, 1)], min_val=0, max_val=NE - 1))
            used = blocks(sp)
            sp.wait_ge(zero_d, START + 1)
            with sp.Fori(used, 64) as n:
                sp.dma_start(g["y_d"][bass.ds(n * P, P), :], b["zero"]).then_inc(z_st, 16)
            sp.wait_ge(z_st, START + sp.value_load(tab[0:1, TAB_FREE:TAB_FREE + 1], min_val=1, max_val=32) * 16)
            sp.sem_inc(g["alone"], 1)

        @block.gpsimd
        def _(pool):
            nb = blocks(pool)

            def gather(i, j):
                pool.wait_ge(x_tr, START + 2 * i)
                pool.sem_inc(g["alone"], 1)
                nc.gpsimd.tensor_copy(ix[:, j:j + 1], gidx[:, bass.ds(2 * i + j, 1)]).then_inc(x_ix, 1)
                pool.wait_ge(x_ix, START + 2 * i + j + 1)
                pool.sem_inc(g["alone"], 1)
                pool.indirect_dma_start(b[f"x{j}"], None, g["h2_d"], bass.IndirectOffsetOnAxis(ix[:, j:j + 1], 0))\
                    .then_inc(x_ld, 16)
                pool.wait_ge(x_ld, 16 * (2 * i + j + 1))
                pool.sem_inc(g["alone"], 1)
            with pool.Fori(0, (nb >> 1) + 1) as i:
                gather(i, 0)
                gather(i, 1)

        @block.scalar
        def _(act):
            nb = blocks(act)

            def split13(r, buf, lo, hi):
                for n in range(lo, hi):
                    act.wait_ge(st_ld[n], START + 16 * r + 16)
                    nc.scalar.activation(part(buf, whi, n * PIECE, PIECE), b["st"][:, n * PIECE:(n + 1) * PIECE],
                                         ACT.Copy, scale=W_SCALE).then_inc(hi13, 1)

            def split2(r, buf):
                for n in range(N13, N13 + N2):
                    act.wait_ge(st_ld[n], START + 16 * r + 16)
                    nc.scalar.activation(part(buf, whi, n * PIECE, PIECE), b["st"][:, n * PIECE:(n + 1) * PIECE],
                                         ACT.Copy, scale=W_SCALE).then_inc(hi2, 1)

            def x_high(n):
                act.wait_ge(x_tr, START + n + 1)
                act.wait_ge(up_mm, START + 2 * n)
                nc.scalar.activation(xh, ps_row[:, 1024:2048], ACT.Copy, scale=X_SCALE).then_inc(x_hi, 1)

            def silu(n):
                act.wait_ge(up_mm, START + 2 * n + 1)
                act.wait_ge(h_d, START + n)
                nc.scalar.activation(b["s"], ps[:, 0, :], ACT.Silu, scale=1.0 / (W_SCALE * X_SCALE)).then_inc(silu_d, 1)

            def h_high(n):
                act.wait_ge(h_tr, START + n + 1)
                act.wait_ge(y_mm, START + n)
                nc.scalar.activation(hh, ps[:, 4, :], ACT.Copy).then_inc(h_hi, 1)

            def store_y(n):
                act.wait_ge(y_ev, START + n + 1)
                act.dma_start(g["y_d"][bass.ds(n * P, P), :], b["y0"]).then_inc(y_st, 16)

            def step(n, prev, stored):
                new = starts_rank(act, n)
                rank, buf = rank_of(act, n), buffer_of(act, n)
                with act.If(new == 1):
                    act.wait_ge(up_mm, START + 2 * n)
                    split13(rank + 1, 1 - buf, 0, N13 // 2)
                h_high(prev)
                silu(n)
                with act.If(new == 1):
                    split13(rank + 1, 1 - buf, N13 // 2, N13)
                x_high(n + 1)
                if stored:
                    store_y(n - 2)
                newp = starts_rank(act, prev)
                rankp, bufp = rank_of(act, prev), buffer_of(act, prev)
                with act.If(newp == 1):
                    act.wait_ge(y_mm, START + prev)
                    split2(rankp + 1, 1 - bufp)
            split13(0, 0, 0, N13)
            x_high(0)
            split2(0, 0)
            split13(1, 1, 0, N13 // 2)
            silu(0)
            split13(1, 1, N13 // 2, N13)
            x_high(1)
            step(1, 0, False)
            with act.Fori(2, nb) as n:
                step(n, n - 1, True)
            last = act.value_load(tab[0:1, TAB_NB1:TAB_NB1 + 1], min_val=31, max_val=MAX_BLOCKS - 2)
            store_y(act.value_load(tab[0:1, TAB_NB2:TAB_NB2 + 1], min_val=30, max_val=MAX_BLOCKS - 3))
            h_high(last)
            store_y(last)
            act.wait_ge(y_st, START + nb * 16)
            act.sem_inc(g["alone"], 1)

        @block.vector
        def _(dve):
            nb = blocks(dve)

            def low(dst, src, scale, high):
                return nc.vector.scalar_tensor_tensor(dst, src, scale, high, ALU.mult, ALU.subtract)

            def split13(r, buf, lo, hi):
                for n in range(lo, hi):
                    dve.wait_ge(hi13, START + N13 * r + n + 1)
                    dve.sem_inc(g["alone"], 1)
                    low(part(buf, wlo, n * PIECE, PIECE), b["st"][:, n * PIECE:(n + 1) * PIECE], W_SCALE,
                        part(buf, whi, n * PIECE, PIECE)).then_inc(lo13, 1)

            def split2(r, buf):
                for n in range(N13, N13 + N2):
                    dve.wait_ge(hi2, START + N2 * r + n - N13 + 1)
                    dve.sem_inc(g["alone"], 1)
                    low(part(buf, wlo, n * PIECE, PIECE), b["st"][:, n * PIECE:(n + 1) * PIECE], W_SCALE,
                        part(buf, whi, n * PIECE, PIECE)).then_inc(lo2, 1)

            def x_low(n):
                dve.wait_ge(x_hi, START + n + 1)
                low(xl, ps_row[:, 1024:2048], X_SCALE, xh).then_inc(x_lo, 1)

            def hidden(n):
                dve.wait_ge(silu_d, START + n + 1)
                dve.wait_ge(up_mm, START + 2 * n + 2)
                dve.wait_ge(h_tr, START + n)
                nc.vector.scalar_tensor_tensor(b["h"], ps[:, 1, :], 1.0 / (W_SCALE * X_SCALE), b["s"], ALU.mult, ALU.mult)\
                    .then_inc(h_d, 1)

            def h_low(n):
                dve.wait_ge(h_hi, START + n + 1)
                low(hl, ps[:, 4, :], 1.0, hh).then_inc(h_lo, 1)

            def scale_y(n):
                dve.wait_ge(y_mm, START + n + 1)
                dve.wait_ge(y_st, START + 16 * n)
                nc.vector.scalar_tensor_tensor(b["y0"], ps_row[:, 2560:3584], 1.0 / W_SCALE, b["g2"], ALU.mult, ALU.mult)\
                    .then_inc(y_ev, 1)

            def step(n, prev):
                new = starts_rank(dve, n)
                rank, buf = rank_of(dve, n), buffer_of(dve, n)
                with dve.If(new == 1):
                    split13(rank + 1, 1 - buf, 0, N13 // 2)
                h_low(prev)
                with dve.If(new == 1):
                    split13(rank + 1, 1 - buf, N13 // 2, N13)
                hidden(n)
                x_low(n + 1)
                newp = starts_rank(dve, prev)
                rankp, bufp = rank_of(dve, prev), buffer_of(dve, prev)
                with dve.If(newp == 1):
                    split2(rankp + 1, 1 - bufp)
                scale_y(prev)
            nc.vector.memset(b["zero"], 0.0).then_inc(zero_d, 1)
            dve.wait_ge(g2_ld, START + 16)
            split13(0, 0, 0, N13)
            x_low(0)
            split2(0, 0)
            split13(1, 1, 0, N13)
            hidden(0)
            x_low(1)
            step(1, 0)
            with dve.Fori(2, nb) as n:
                step(n, n - 1)
            last = dve.value_load(tab[0:1, TAB_NB1:TAB_NB1 + 1], min_val=31, max_val=MAX_BLOCKS - 2)
            h_low(last)
            scale_y(last)

        @block.tensor
        def _(pe):
            def transposes_x(j, n):
                pe.wait_ge(x_ld, 16 * n + 16)
                pe.wait_ge(x_lo, START + n)
                for k in range(KD):
                    mm = pe.transpose(ps_row[:, 1024 + k * P:1024 + (k + 1) * P], b[f"x{j}"][:, k * P:(k + 1) * P], idn[:])
                mm.then_inc(x_tr, 1)

            def product(out, high, low, buf, at, first, last):
                pe.matmul(out, high, part(buf, whi, at, 512), start=first, stop=False)
                pe.matmul(out, high, part(buf, wlo, at, 512), start=False, stop=False)
                return pe.matmul(out, low, part(buf, whi, at, 512), start=False, stop=last)

            def up(bank, off, buf):
                for k in range(KD):
                    mm = product(ps[:, bank, :], xh[:, k * P:(k + 1) * P], xl[:, k * P:(k + 1) * P], buf,
                                 off + k * D_EXP, k == 0, k == KD - 1)
                mm.then_inc(up_mm, 1)

            def down(n):
                rank, buf = rank_of(pe, n), buffer_of(pe, n)
                pe.wait_ge(h_lo, START + n + 1)
                pe.wait_ge(y_ev, START + n)
                pe.wait_ge(lo2, START + N2 * rank + N2)
                for k in range(KE):
                    for c in range(2):
                        mm = product(ps[:, 5 + c, :], hh[:, k * P:(k + 1) * P], hl[:, k * P:(k + 1) * P], buf,
                                     W13 + k * D + c * 512, k == 0, k == KE - 1)
                mm.then_inc(y_mm, 1)

            def transposes_h(n):
                pe.wait_ge(h_d, START + n + 1)
                pe.wait_ge(h_lo, START + n)
                for k in range(KE):
                    mm = pe.transpose(ps[:, 4, k * P:(k + 1) * P], b["h"][:, k * P:(k + 1) * P], idn[:])
                mm.then_inc(h_tr, 1)

            def step(n, prev, j):
                rank, buf = rank_of(pe, n), buffer_of(pe, n)
                pe.wait_ge(x_lo, START + n + 1)
                pe.wait_ge(silu_d, START + n)
                pe.wait_ge(lo13, START + N13 * rank + N13 // 2)
                up(0, 0, buf)
                if prev is not None:
                    transposes_h(prev)
                    pe.wait_ge(h_d, START + n)
                pe.wait_ge(lo13, START + N13 * rank + N13)
                up(1, KD * D_EXP, buf)
                transposes_x(1 - j, n + 1)
                if prev is not None:
                    down(prev)
            last = pe.value_load(tab[0:1, TAB_NB1:TAB_NB1 + 1], min_val=31, max_val=MAX_BLOCKS - 2)
            before = pe.value_load(tab[0:1, TAB_NB2:TAB_NB2 + 1], min_val=30, max_val=MAX_BLOCKS - 3)
            transposes_x(0, 0)
            step(0, None, 0)
            with pe.Fori(0, last >> 1) as i:
                step(2 * i + 1, 2 * i, 1)
                step(2 * i + 2, 2 * i + 1, 0)
            with pe.If((last & 1) == 1):
                step(last, before, 1)
            transposes_h(last)
            down(last)


def phase_combine(nc, env):
    g = env
    sem, arena = g["sem"], g["arena"]
    slot_i, gates = g["slot_i"], g["gates"]
    b = arena_slices(arena, 0, [("l2g", D), ("l2b", D), ("mh", 1), ("st", 12), ("mv", 2), ("ve", 1), ("rs", 1), ("nmr", 1)]
                     + [(f"{n}{j}", D) for n in ("ya", "yb", "x1", "o") for j in range(2)])
    ix = g["stack"].enter_context(nc.sbuf_tensor("ixc", [P, 4], I32))
    ld, ix_d, y_ld, x_ld, o_st, v, pw, a_x, a_n, fin, hold, mh_d = (
        sem("h_ld"), sem("h_ix"), g["plain_sem"]("h_y_ld"), sem("h_x_ld"), sem("h_o_st"), sem("h_v"), sem("h_pw"), sem("h_a_x"),
        sem("h_a_n"), sem("h_fin"), sem("h_hold"), sem("h_mh"))
    NV = 8
    with nc.Block() as block:
        @block.sync
        def _(sp):
            for n, name in enumerate(("l2g", "l2b")):
                sp.dma_start(b[name], g["ln2"][n:n + 1, :].to_broadcast([P, D])).then_inc(ld, 16)
            with sp.Fori(0, T_LAT // 2) as i:
                for j in range(2):
                    sp.wait_ge(v, START + NV * 2 * i)
                    sp.dma_start(b[f"x1{j}"], g["x1_d"][bass.ds((2 * i + j) * P, P), :]).then_inc(x_ld, 16)
                    sp.wait_ge(x_ld, START + 32 * i + 16 * j + 16)
                    sp.sem_inc(g["alone"], 1)

        @block.gpsimd
        def _(pool):
            nc.gpsimd.memset(b["mh"], -0.5).then_inc(mh_d, 1)
            pool.wait_ge(mh_d, START + 1)
            pool.wait_ge(ld, START + 32)

            def fetch(i, j):
                pool.wait_ge(v, START + NV * 2 * i)
                pool.sem_inc(g["alone"], 1)
                for k in range(2):
                    nc.gpsimd.tensor_copy(ix[:, 2 * j + k:2 * j + k + 1], slot_i[:, bass.ds(k * T_LAT + 2 * i + j, 1)]).then_inc(ix_d, 1)
                pool.wait_ge(ix_d, START + 4 * i + 2 * j + 2)
                pool.sem_inc(g["alone"], 1)
                for k in range(2):
                    pool.indirect_dma_start(b[f"{('ya', 'yb')[k]}{j}"], None, g["y_d"],
                                            bass.IndirectOffsetOnAxis(ix[:, 2 * j + k:2 * j + k + 1], 0)).then_inc(y_ld, 16)
                pool.wait_ge(y_ld, 64 * i + 32 * j + 32)
                pool.sem_inc(g["alone"], 1)
            with pool.Fori(0, T_LAT // 2) as i:
                for j in range(2):
                    fetch(i, j)
                for j in range(2):
                    pool.wait_ge(v, START + NV * (2 * i + j) + 5)
                    pool.sem_inc(g["alone"], 1)
                    nc.gpsimd.tensor_tensor(b["rs"], b["ve"], b["mh"], ALU.pow).then_inc(pw, 1)

        @block.scalar
        def _(act):
            with act.Fori(0, T_LAT // 2) as i:
                for j in range(2):
                    t = 2 * i + j
                    act.wait_ge(x_ld, START + 16 * t + 16)
                    nc.scalar.activation(b[f"x1{j}"], b[f"x1{j}"], ACT.Copy, scale=ALPHA).then_inc(a_x, 1)
                    act.wait_ge(fin, START + t + 1)
                    act.dma_start(g["out"][bass.ds(t * P, P), :], b[f"o{j}"]).then_inc(o_st, 16)
            act.wait_ge(o_st, START + 16 * T_LAT)

        @block.vector
        def _(dve):
            dve.wait_ge(ld, START + 32)
            with dve.Fori(0, T_LAT // 2) as i:
                for j in range(2):
                    t = 2 * i + j
                    n = [0]

                    def link(ins, sync=True):
                        n[0] += 1
                        ins.then_inc(v, 1)
                        if sync:
                            dve.wait_ge(v, START + NV * t + n[0])
                    y0, y1, x1, o = b[f"ya{j}"], b[f"yb{j}"], b[f"x1{j}"], b[f"o{j}"]
                    dve.wait_ge(a_x, START + t + 1)
                    dve.wait_ge(y_ld, 32 * t + 32)
                    link(nc.vector.scalar_tensor_tensor(x1, y0, gates[:, bass.ds(t, 1)], x1, ALU.mult, ALU.add))
                    link(nc.vector.scalar_tensor_tensor(x1, y1, gates[:, bass.ds(T_LAT + t, 1)], x1, ALU.mult, ALU.add))
                    link(nc.vector.bn_stats(b["st"][:, 0:6], x1[:, 0:512]))
                    link(nc.vector.bn_stats(b["st"][:, 6:12], x1[:, 512:1024]))
                    dve.sem_inc(g["alone"], 1)
                    nc.vector.bn_aggr(b["mv"], b["st"].rearrange("p (a s) -> p a s", a=2)).then_inc(a_n, 1)
                    dve.wait_ge(a_n, START + t + 1)
                    link(nc.vector.tensor_scalar(b["ve"], b["mv"][:, 1:2], EPS, None, ALU.add))
                    dve.wait_ge(pw, START + t + 1)
                    link(nc.vector.tensor_scalar(x1, x1, b["mv"][:, 0:1], b["rs"], ALU.subtract, ALU.mult))
                    link(nc.vector.tensor_tensor(x1, x1, b["l2g"], ALU.mult))
                    dve.wait_ge(o_st, START + 32 * i)
                    link(nc.vector.tensor_tensor(o, x1, b["l2b"], ALU.add))
                    dve.sem_inc(fin, 1)


def _constants():
    grid_w, axis = 64, HD // 2
    inv = (10000.0 ** (-np.arange(0, axis, 2, dtype=np.float32) / np.float32(axis))).astype(np.float32)
    pos = np.arange(SEQ)
    ang = np.stack([(pos // grid_w).astype(np.float32)[:, None] * inv, (pos % grid_w).astype(np.float32)[:, None] * inv], 1)
    cos_t = np.cos(ang).astype(np.float32).reshape(T_LAT, P, 2 * inv.size)
    sin_t = np.sin(ang).astype(np.float32).reshape(T_LAT, P, 2 * inv.size)
    q, k = np.arange(P)[:, None], np.arange(WIN)[None, :] - P
    masks = np.zeros((4, P, KEYS), np.float32)
    for m in range(3):
        ok = np.abs(k - q) <= P
        if m == 0:
            ok = ok & (k >= 0)
        if m == 2:
            ok = ok & (k < P)
        masks[m, :, CTX:] = np.where(ok, 0.0, NEG)
    tri = np.triu(np.ones((P, P), np.float32), 1)
    iota = np.tile(np.arange(64, dtype=np.float32), (P, 1))
    tok = (np.arange(T_LAT)[None, :] * P + np.arange(P)[:, None]).astype(np.int32)
    return {"cos_t": cos_t, "sin_t": sin_t, "ident": np.eye(P, dtype=np.float32), "masks": masks, "tri": tri,
            "iota": iota, "tok_id": tok}


def _layout(i):
    c = np.ascontiguousarray
    cs = np.stack([np.asarray(i["c"])[0], np.asarray(i["c_ctx"])], 1)
    a = {k: np.asarray(i[k]) for k in i}
    order = np.arange(NH).reshape(NKV, PAIRS).T.reshape(-1)
    cols = (2 * D_RNN + order[:, None] * HD + np.arange(HD)).reshape(-1)
    w_in = np.concatenate([a["w_in"][0][:, :2 * D_RNN], a["w_in"][0][:, cols], a["w_in"][0][:, 2 * D_RNN + D_ATTN:]], 1)
    return {
        "x": c(a["x"][0]), "c2": c(cs.reshape(KD, P, 2).transpose(1, 0, 2).reshape(P, 2 * KD)), "w_mod": c(a["w_mod"][0]),
        "b_mod": c(np.stack([a["b_mod"][0]] * 2)), "w_in": c(w_in),
        "rg_par": c(np.concatenate([a["conv_w"][0].T, a["conv_b"][0][:, None], a["rg_ba"][0].T, a["rg_bx"][0].T],
                                   1)),
        "lam": c(a["rg_lam"][0].reshape(2, C_RNN, P).transpose(2, 0, 1).reshape(P, 2 * C_RNN)),
        "rg_wa": c(a["rg_wa"][0]), "rg_wx": c(a["rg_wx"][0]), "ctx_x": c(a["ctx"][0]),
        "sink": c(np.stack([a["attn_sink"][0]] * P)), "w_out": c(a["w_out"][0]),
        "gn": c(np.concatenate([a["gn_rnn"][0], a["gn_attn"][0]]).reshape(KD, P).T),
        "ln1": c(np.stack([a["ln1_g"][0], a["ln1_b"][0]])),
        "router": c(np.concatenate([a["router_g"][0], a["router_e"][0]], 1)),
        "router_b": c(np.concatenate([a["router_gb"][0], a["router_eb"][0]])[None, :]),
        "w1": c(a["w1"][0]), "w3": c(a["w3"][0]), "w2": c(a["w2"][0]), "ln2": c(np.stack([a["ln2_g"][0], a["ln2_b"][0]])),
        **_constants(),
    }


_ARGS = ["x", "c2", "w_mod", "b_mod", "w_in", "rg_par", "lam", "rg_wa", "rg_wx", "ctx_x", "sink", "w_out", "gn", "ln1", "router",
         "router_b", "w1", "w3", "w2", "ln2", "cos_t", "sin_t", "ident", "masks", "tri", "iota", "tok_id"]


def kernel(**inputs):
    import concourse.bacc as bacc
    from concourse.bass_utils import run_bass_kernel_spmd

    arrays = _layout(inputs)
    nc = bacc.Bacc("TRN2", target_bir_lowering=False, num_devices=1)
    aps = {n: nc.dram_tensor(n, arrays[n].shape, mybir.dt.from_np(arrays[n].dtype), kind="ExternalInput").ap() for n in _ARGS}
    aps["out"] = nc.dram_tensor("out", (SEQ, D), F32, kind="ExternalOutput").ap()
    hybrid_layer(nc, **aps)
    r = run_bass_kernel_spmd(nc, [{n: arrays[n] for n in _ARGS}], core_ids=[0])
    return np.asarray(r.results[0]["out"]).reshape(1, SEQ, D)
```

```python
from contextlib import ExitStack

import numpy as np

import concourse.bass as bass
from concourse import mybir

F32 = mybir.dt.float32
F16 = mybir.dt.float16
I32 = mybir.dt.int32
U32 = mybir.dt.uint32
ALU = mybir.AluOpType
ACT = mybir.ActivationFunctionType
AX_X = mybir.AxisListType.X

P = 128
D = 1024
KD = D // P
SEQ = 2048
CTX = 256
T_LAT = SEQ // P
D_RNN = 512
C_RNN = D_RNN // P
D_ATTN = 512
HD = 64
NH = D_ATTN // HD
NKV = 2
PAIRS = NH // NKV
QKV = D_ATTN + 2 * NKV * HD
D_IN = 2 * D_RNN + QKV
TIME = CTX + SEQ
U_CTX = 2
U_LAT = U_CTX + CTX + 2
U_ROW = U_LAT + SEQ + 4
WIN = 3 * P
KEYS = CTX + WIN
K_LAT = CTX + P
K_ROW = K_LAT + SEQ + P
CONV_W = 4
NE = 32
NG = 4
EPG = NE // NG
D_EXP = 512
KE = D_EXP // P
MAX_BLOCKS = (2 * SEQ + NE * (P - 1)) // P + 1
NPAR = 9
ALPHA = 2 ** 0.25
START = 1
W_SCALE, X_SCALE = 64.0, 16.0
TAB_RANK, TAB_BUF, TAB_NEW, TAB_EXPERT = 0, 64, 128, 192
TAB_NB, TAB_NB1, TAB_NB2, TAB_NR, TAB_FREE = 224, 225, 226, 227, 228
TAB_SIZE = 264
EPS = 1e-6
NEG = -1e30
CHUNK = 512
TPC = CHUNK // P

SEMAPHORES = """
b_mcol_ld b_rope_ld b_x_ld b_g_st b_q_st b_pads b_sc b_stats b_agg b_var b_rstd b_normed b_tr_x b_hT_a b_hT_v
b_u_mm b_g_mm b_u_ev b_g_ev b_qkv_mm b_rope_a b_rope_b b_rope_o b_v_ev b_q_tr b_k_tr b_q_ev b_k_ev c_lam_ld
c_par_ld c_gw_ld c_gate_ld c_zero c_sp_v c_sp_a c_cur c_conv c_g_mm c_g_ev c_tanh c_exp c_sqrt c_frac c_drive
c_scan c_y c_y_st d_mask_ld d_q_ld d_s_mm d_s_max d_nm d_p d_p_tr d_p_ev d_pv d_o_free d_es d_es_e d_den d_o
e_w_ld e_w_ok e_w_hi e_w_lo e_p_ok e_in_ld0 e_in_ld1 e_xt_ld0 e_xt_ld1 e_x_st0 e_x_st1 e_h_st0 e_h_st1 e_sq
e_y_hi e_y_lo e_ssm e_ss e_ssv e_pw_s e_a_tr e_a_hi e_a_lo e_o_mm e_o_act e_v e_pw e_h_tr e_h_ev e_r_mm e_lg
f_ld f_v f_act f_mm f_tab_ld f_tr g_st_ld0 g_st_ld1 g_st_ld2 g_st_ld3 g_st_ld4 g_st_ld5 g_hi13 g_lo13 g_hi2
g_lo2 g_g2_ld g_x_ix g_x_tr g_x_hi g_x_lo g_up_mm g_silu g_h g_h_tr g_h_hi g_h_lo g_y_mm g_y_ev g_y_st g_zero
g_z_st h_ld h_ix h_v h_pw h_a_x h_mh h_x_ld0 h_x_ld1 h_o_st0 h_o_st1
""".split()


def arena_slices(arena, start, sizes):
    out = {}
    for name, size in sizes:
        out[name] = arena[:, start:start + size]
        start += size
    assert start <= arena.shape[1], start
    return out


def hybrid_layer(nc, x, c2, w_mod, b_mod, w_in, rg_par, lam, rg_wa, rg_wx, ctx_x, sink, w_out, gn, ln1, router, router_b,
                 w1, w3, w2, ln2, cos_t, sin_t, ident, masks, tri, iota, tok_id, out):
    with ExitStack() as stack:
        def plain_sem(name):
            return stack.enter_context(nc.semaphore(name))

        from_one = {name: plain_sem(name) for name in SEMAPHORES}

        def sem(name):
            return from_one[name]

        def sb(name, shape, dt=F32):
            return stack.enter_context(nc.sbuf_tensor(name, shape, dt))

        def dram(name, shape, dt=F32):
            return nc.dram_tensor(name, shape, dt, kind="Internal").ap()

        mod_rows = dram("mod_rows", [2, 6 * D])
        gate_d = dram("gate_d", [C_RNN, P, SEQ])
        qT_d = dram("qT_d", [T_LAT, P, PAIRS * P])
        yT_d = dram("yT_d", [C_RNN, P, SEQ])
        attn_d = dram("attn_d", [T_LAT, P, D_ATTN])
        x1_d = dram("x1_d", [SEQ, D])
        h2_d = dram("h2_d", [SEQ, D])
        slot_tok_d = dram("slot_tok_d", [64 * P, 1], I32)
        y_d = dram("y_d", [64 * P, D])

        idn = sb("idn", [P, P])
        small = sb("small", [P, 640])
        arena = sb("arena", [P, 50500])
        slot_i = sb("slot_i", [P, 2 * T_LAT], I32)
        gates = sb("gates", [P, 2 * T_LAT])
        blk_tab = sb("blk_tab", [1, TAB_SIZE], I32)
        gidx = sb("gidx", [P, 66], I32)
        ps = stack.enter_context(nc.psum_tensor("ps", [P, 8, 512], F32))
        ps_row = ps[:, :, :].rearrange("p b n -> p (b n)")

        const_ld = plain_sem("const_ld")
        win_ld = plain_sem("win_ld")
        alone = plain_sem("alone")
        env = dict(locals())
        phase_modulation(nc, env)
        phase_project(nc, env)
        phase_recurrence(nc, env)
        phase_attention(nc, env)
        phase_output(nc, env)
        phase_route(nc, env)
        phase_experts(nc, env)
        phase_combine(nc, env)


UT0 = 0
KT0 = UT0 + C_RNN * U_ROW
V0 = KT0 + 2 * K_ROW
V_SLOTS = 2 + 1 + T_LAT + 1
B0 = V0 + V_SLOTS * P
WIN0 = 50500 - KD * D_IN


def phase_modulation(nc, env):
    g = env
    sem, arena, ps, small = g["plain_sem"], g["arena"], g["ps"], g["small"]
    c_ld, silu_done = sem("a_c_ld"), sem("a_silu_done")
    wmod_ld = [sem(f"a_wmod_ld{j}") for j in range(3)]
    mod_mm, rows_done, rows_st = sem("a_mod_mm"), sem("a_rows_done"), sem("a_rows_st")
    a = arena_slices(arena, 0, [("w0", KD * 512), ("w1", KD * 512), ("w2", KD * 512), ("rows", 6 * D)])
    ring = [a[f"w{j}"].rearrange("p (k n) -> p k n", k=KD) for j in range(3)]
    c2s = small[:, 0:2 * KD]
    c2a = small[:, 2 * KD:4 * KD]
    zi = small[0:64, 128:256].bitcast(I32)
    wmod_v = g["w_mod"].rearrange("(k p) n -> p k n", p=P)
    with nc.Block() as block:
        @block.sync
        def _(sp):
            sp.dma_start(c2s, g["c2"]).then_inc(c_ld, 16)
            sp.dma_start(a["rows"][0:2, :], g["b_mod"]).then_inc(c_ld, 16)
            sp.dma_start(g["idn"][:], g["ident"]).then_inc(g["const_ld"], 16)
            for j in range(3):
                sp.dma_start(ring[j], wmod_v[:, :, j * 512:(j + 1) * 512]).then_inc(wmod_ld[j], 16)
            with sp.Fori(0, 3) as i:
                for j in range(3):
                    sp.wait_ge(mod_mm, i * 3 + j + 1)
                    sp.dma_start(ring[j], wmod_v[:, :, bass.ds(i * 1536 + (j + 3) * 512, 512)]).then_inc(wmod_ld[j], 16)
            win = arena[:, WIN0:].rearrange("p (k n) -> p k n", k=KD)
            sp.dma_start(win, g["w_in"].rearrange("(k p) n -> p k n", p=P)).then_inc(g["win_ld"], 16)
            sp.wait_ge(rows_done, 1)
            sp.dma_start(g["slot_tok_d"].rearrange("(a b) o -> a (b o)", a=64), zi).then_inc(rows_st, 16)
            sp.wait_ge(rows_done, 13)
            sp.dma_start(g["mod_rows"], a["rows"][0:2, :]).then_inc(rows_st, 16)
            sp.wait_ge(rows_st, 32)
            sp.wait_ge(c_ld, 32)
            sp.wait_ge(g["const_ld"], 16)

        @block.gpsimd
        def _(pool):
            for s in g["from_one"].values():
                pool.sem_inc(s, START)

        @block.scalar
        def _(act):
            act.wait_ge(c_ld, 32)
            nc.scalar.activation(c2a, c2s, ACT.Silu).then_inc(silu_done, 1)

        @block.tensor
        def _(pe):
            pe.wait_ge(silu_done, 1)
            with pe.Fori(0, 4) as i:
                for j in range(3):
                    pe.wait_ge(wmod_ld[j], i * 16 + 16)
                    pe.wait_ge(rows_done, i * 3 + 1)
                    for k in range(KD):
                        mm = pe.matmul(ps[0:2, j, :], c2a[:, 2 * k:2 * k + 2], ring[j][:, k, :],
                                       start=(k == 0), stop=(k == KD - 1))
                    mm.then_inc(mod_mm, 1)

        @block.vector
        def _(dve):
            nc.vector.memset(zi, 0).then_inc(rows_done, 1)
            dve.wait_ge(c_ld, 32)
            with dve.Fori(0, 4) as i:
                for j in range(3):
                    row = a["rows"][0:2, bass.ds(i * 1536 + j * 512, 512)]
                    dve.wait_ge(mod_mm, i * 3 + j + 1)
                    nc.vector.tensor_tensor(row, ps[0:2, j, :], row, ALU.add).then_inc(rows_done, 1)


def phase_project(nc, env):
    g = env
    sem, arena, ps, ps_row, small, idn = g["sem"], g["arena"], g["ps"], g["ps_row"], g["small"], g["idn"]
    uT = arena[:, UT0:KT0].rearrange("p (c t) -> p c t", c=C_RNN)
    kTz = arena[:, KT0:V0].rearrange("p (z t) -> p z t", z=2)
    vt = arena[:, V0:B0].rearrange("p (s d) -> p s d", s=V_SLOTS)
    b = arena_slices(arena, B0, [("xr", TPC * D), ("xn", TPC * D), ("hT", KD * CHUNK), ("gout", 2 * CHUNK),
                                 ("qr", 640), ("ta", 320), ("tb", 320), ("qTs", 512)])
    assert B0 + 2 * TPC * D + KD * CHUNK + 2 * CHUNK + 1792 <= WIN0, (B0, WIN0)
    win = arena[:, WIN0:].rearrange("p (k n) -> p k n", k=KD)
    xr = b["xr"].rearrange("p (t d) -> p t d", t=TPC)
    xn = b["xn"].rearrange("p (t d) -> p t d", t=TPC)
    hT = b["hT"].rearrange("p (k n) -> p k n", k=KD)
    gout = b["gout"].rearrange("p (a n) -> p a n", a=2)
    qr, ta, tb = b["qr"], b["ta"], b["tb"]
    mcol = small[:, 0:32].rearrange("p (s n) -> p s n", s=2)
    st = small[:, 32:32 + 12 * TPC].rearrange("p (t a s) -> p t a s", t=TPC, a=2)
    mv = small[:, 80:80 + 2 * TPC].rearrange("p (t s) -> p t s", t=TPC)
    ve = small[:, 96:96 + TPC]
    rs = small[:, 100:100 + TPC]
    mh = small[:, 104:104 + TPC]
    rope = g["stack"].enter_context(nc.sbuf_tensor("rope", [P, 2, 2, 32], F32))

    mcol_ld, rope_ld, x_ld, g_st, q_st = sem("b_mcol_ld"), sem("b_rope_ld"), sem("b_x_ld"), sem("b_g_st"), sem("b_q_st")
    pads, sc_ok, stats, agg, var_e, rstd = sem("b_pads"), sem("b_sc"), sem("b_stats"), sem("b_agg"), sem("b_var"), sem("b_rstd")
    normed, tr_x, hT_a, hT_v = sem("b_normed"), sem("b_tr_x"), sem("b_hT_a"), sem("b_hT_v")
    u_mm, g_mm, u_ev, g_ev = sem("b_u_mm"), sem("b_g_mm"), sem("b_u_ev"), sem("b_g_ev")
    qkv_mm, rope_a, rope_b, rope_o = sem("b_qkv_mm"), sem("b_rope_a"), sem("b_rope_b"), sem("b_rope_o")
    v_ev, q_tr, k_tr, q_ev, k_ev = sem("b_v_ev"), sem("b_q_tr"), sem("b_k_tr"), sem("b_q_ev"), sem("b_k_ev")

    NT_C = CTX // P
    x_lat = g["x"].rearrange("(n t p) d -> n p t d", p=P, t=TPC)
    x_ctx = g["ctx_x"].rearrange("(t p) d -> p t d", p=P)

    def at(i, ctx, lat, k):
        return k if i is None else ctx + i * lat + k

    with nc.Block() as block:
        @block.sync
        def _(sp):
            for s in range(2):
                for half in range(2):
                    for k in range(KD):
                        src = g["mod_rows"][s:s + 1, half * D + k * P:half * D + (k + 1) * P].rearrange("o p -> p o")
                        sp.dma_start(mcol[:, s, half * KD + k:half * KD + k + 1], src).then_inc(mcol_ld, 16)
            sp.dma_start(xr[:, 0:NT_C, :], x_ctx).then_inc(x_ld, 16)

            def chunk(i):
                sp.wait_ge(normed, START + NT_C + i * TPC)
                sp.sem_inc(g["alone"], 1)
                sp.dma_start(xr, x_lat[bass.ds(i, 1)].rearrange("n p t d -> (n p) t d")).then_inc(x_ld, 16)
                for t in range(TPC):
                    n = i * TPC + t
                    sp.dma_start(rope[:, t % 2, 0, :],
                                 g["cos_t"][bass.ds(n, 1)].rearrange("n p d -> (n p) d")).then_inc(rope_ld, 16)
                    sp.dma_start(rope[:, t % 2, 1, :],
                                 g["sin_t"][bass.ds(n, 1)].rearrange("n p d -> (n p) d")).then_inc(rope_ld, 16)
                    sp.wait_ge(rope_o, START + NT_C + 2 * (i * TPC + t) + 2)
                    sp.sem_inc(g["alone"], 1)
                    sp.wait_ge(q_ev, START + i * TPC + t + 1)
                    sp.sem_inc(g["alone"], 1)
                    sp.dma_start(g["qT_d"][bass.ds(n, 1)].rearrange("n p d -> (n p) d"), b["qTs"]).then_inc(q_st, 16)
            with sp.Fori(0, SEQ // CHUNK) as i:
                chunk(i)
            sp.wait_ge(q_st, START + 16 * T_LAT)

        def evac_plan(k):
            return "act" if k % 2 == 0 else "dve"

        @block.scalar
        def _(act):
            def chunk(i):
                nt = NT_C if i is None else TPC
                n = nt * P
                s = 1 if i is None else 0
                if i is None:
                    act.wait_ge(sc_ok, START + 1)
                for k in range(0, KD, 2):
                    act.wait_ge(tr_x, START + at(i, KD, KD, k + 1))
                    nc.scalar.activation(hT[:, k, 0:n], ps[:, 0, 0:n], ACT.Identity, bias=mcol[:, s, k:k + 1],
                                         scale=mcol[:, s, KD + k:KD + k + 1]).then_inc(hT_a, 1)
                if i is not None:
                    for c in range(C_RNN):
                        act.wait_ge(g_mm, START + i * C_RNN + c + 1)
                        act.wait_ge(g_st, START + (i * C_RNN + c) * 16)
                        nc.scalar.activation(gout[:, 0, :], ps[:, 3, :], ACT.Gelu_apprx_tanh).then_inc(g_ev, 1)
                        act.wait_ge(g_ev, START + i * C_RNN + c + 1)
                        act.dma_start(g["gate_d"][c][:, bass.ds(i * CHUNK, CHUNK)], gout[:, 0, :]).then_inc(g_st, 16)
                for t in range(nt):
                    act.wait_ge(rope_o, START + (t + 1 if i is None else NT_C + 2 * (i * TPC + t) + 2))
                    bank = 4 + 2 * (t % 2)
                    if i is None:
                        nc.scalar.activation(vt[:, t, :], ps[:, bank + 1, P:2 * P], ACT.Copy).then_inc(v_ev, 1)
                    else:
                        nc.scalar.activation(arena[:, bass.ds(V0 + (3 + t) * P + i * (TPC * P), P)],
                                             ps[:, bank + 1, P:2 * P], ACT.Copy).then_inc(v_ev, 1)
                        act.wait_ge(q_tr, START + i * TPC + t + 1)
                        act.wait_ge(q_st, START + (i * TPC + t) * 16)
                        nc.scalar.activation(b["qTs"], ps[:, 0, :], ACT.Copy, scale=HD ** -0.5).then_inc(q_ev, 1)
                    act.wait_ge(k_tr, START + at(i, NT_C, TPC, t + 1))
                    for z in range(2):
                        dst = kTz[64 * z:64 * z + 64, z, t * P:(t + 1) * P] if i is None else \
                            arena[64 * z:64 * z + 64, bass.ds(KT0 + z * K_ROW + K_LAT + t * P + i * CHUNK, P)]
                        nc.scalar.activation(dst, ps[64 * z:64 * z + 64, 1, 0:P], ACT.Copy).then_inc(k_ev, 1)
            act.wait_ge(pads, START + 5)
            chunk(None)
            with act.Fori(0, SEQ // CHUNK) as i:
                chunk(i)
            act.wait_ge(g_st, START + 16 * C_RNN * (SEQ // CHUNK))

        @block.gpsimd
        def _(pool):
            nc.gpsimd.memset(mh, -0.5).then_inc(pads, 1)
            nc.gpsimd.memset(kTz, 0.0).then_inc(pads, 1)
            nc.gpsimd.memset(vt[:, 2, :], 0.0).then_inc(pads, 1)
            nc.gpsimd.memset(vt[:, V_SLOTS - 1, :], 0.0).then_inc(pads, 1)
            nc.gpsimd.memset(uT, 0.0).then_inc(pads, 1)

            def chunk(i):
                nt = NT_C if i is None else TPC
                pool.wait_ge(pads, START + 5)
                pool.wait_ge(var_e, START + (1 if i is None else i + 2))
                nc.gpsimd.tensor_tensor(rs[:, 0:nt], ve[:, 0:nt], mh[:, 0:nt], ALU.pow).then_inc(rstd, 1)
            chunk(None)
            with pool.Fori(0, SEQ // CHUNK) as i:
                chunk(i)

        @block.vector
        def _(dve):
            dve.wait_ge(mcol_ld, START + 16 * 32)
            nc.vector.tensor_scalar(mcol[:, :, KD:2 * KD], mcol[:, :, KD:2 * KD], 1.0, None, ALU.add).then_inc(sc_ok, 1)
            dve.wait_ge(sc_ok, START + 1)
            dve.wait_ge(pads, START + 5)

            def norm(i):
                nt = NT_C if i is None else TPC
                dve.wait_ge(x_ld, START + (16 if i is None else i * 16 + 32))
                for t in range(nt):
                    for a in range(2):
                        nc.vector.bn_stats(st[:, t, a, :], xr[:, t, a * 512:(a + 1) * 512]).then_inc(stats, 1)
                dve.wait_ge(stats, START + at(i, 2 * NT_C, 2 * TPC, 2 * nt))
                dve.sem_inc(g["alone"], 1)
                for t in range(nt):
                    nc.vector.bn_aggr(mv[:, t, :], st[:, t, :, :]).then_inc(agg, 1)
                dve.wait_ge(agg, START + at(i, NT_C, TPC, nt))
                nc.vector.tensor_scalar(ve[:, 0:nt], mv[:, 0:nt, 1], EPS, None, ALU.add).then_inc(var_e, 1)
                dve.wait_ge(rstd, START + (1 if i is None else i + 2))
                dve.wait_ge(tr_x, START + at(i, KD, KD, 0))
                for t in range(nt):
                    nc.vector.tensor_scalar(xn[:, t, :], xr[:, t, :], mv[:, t, 0:1], rs[:, t:t + 1],
                                            ALU.subtract, ALU.mult).then_inc(normed, 1)

            def chunk(i):
                nt = NT_C if i is None else TPC
                n = nt * P
                s = 1 if i is None else 0
                norm(i)
                for k in range(1, KD, 2):
                    dve.wait_ge(tr_x, START + at(i, KD, KD, k + 1))
                    nc.vector.tensor_scalar(hT[:, k, 0:n], ps[:, 1, 0:n], mcol[:, s, KD + k:KD + k + 1],
                                            mcol[:, s, k:k + 1], ALU.mult, ALU.add).then_inc(hT_v, 1)
                for c in range(C_RNN):
                    dve.wait_ge(u_mm, START + at(i, C_RNN, C_RNN, c + 1))
                    dst = uT[:, c, U_CTX:U_CTX + CTX] if i is None else \
                        arena[:, bass.ds(UT0 + c * U_ROW + U_LAT + i * CHUNK, CHUNK)]
                    nc.vector.tensor_copy(dst, ps[:, 2, 0:n]).then_inc(u_ev, 1)
                for t in range(nt):
                    bank = 4 + 2 * (t % 2)
                    dve.wait_ge(qkv_mm, START + at(i, NT_C, TPC, t + 1))
                    if i is None:
                        if t:
                            dve.wait_ge(k_tr, START + t)
                        nc.vector.tensor_copy(qr[:, 512:640], ps[:, bank + 1, 0:P]).then_inc(rope_o, 1)
                        continue
                    j = i * TPC + t
                    dve.wait_ge(rope_ld, START + 32 * j + 32)
                    raw = ps_row[:, bank * 512:bank * 512 + 640].rearrange("p (h a f d) -> p h a f d", a=2, f=2, d=16)
                    rot = qr.rearrange("p (h a f d) -> p h a f d", a=2, f=2, d=16)
                    co = rope[:, t % 2, 0, :].rearrange("p (o a d) -> p o a d", o=1, a=2).to_broadcast([P, 10, 2, 16])
                    si = rope[:, t % 2, 1, :].rearrange("p (o a d) -> p o a d", o=1, a=2).to_broadcast([P, 10, 2, 16])
                    tav = ta.rearrange("p (h a d) -> p h a d", a=2, d=16)
                    tbv = tb.rearrange("p (h a d) -> p h a d", a=2, d=16)
                    for f, op in ((0, ALU.subtract), (1, ALU.add)):
                        dve.wait_ge(rope_o, START + NT_C + 2 * j + f)
                        nc.vector.tensor_tensor(tav, raw[:, :, :, f, :], co, ALU.mult).then_inc(rope_a, 1)
                        nc.vector.tensor_tensor(tbv, raw[:, :, :, 1 - f, :], si, ALU.mult).then_inc(rope_a, 1)
                        dve.wait_ge(rope_a, START + 4 * j + 2 * f + 2)
                        if f == 0:
                            dve.wait_ge(k_tr, START + NT_C + j)
                        nc.vector.tensor_tensor(rot[:, :, :, f, :], tav, tbv, op).then_inc(rope_o, 1)
            chunk(None)
            with dve.Fori(0, SEQ // CHUNK) as i:
                chunk(i)

        @block.tensor
        def _(pe):
            pe.wait_ge(g["const_ld"], 16)

            def transposed(i):
                nt = NT_C if i is None else TPC
                pe.wait_ge(normed, START + at(i, NT_C, TPC, nt))
                for k in range(KD):
                    ev, n = (hT_a, k // 2) if k % 2 == 0 else (hT_v, k // 2)
                    pe.wait_ge(ev, START + at(i, KD // 2, KD // 2, n))
                    if k == 0:
                        if i is not None:
                            pe.wait_ge(q_ev, START + i * TPC)
                    if k == 1:
                        pe.wait_ge(k_ev, START + at(i, 2 * NT_C, 2 * TPC, 0))
                    for t in range(nt):
                        mm = pe.transpose(ps[:, k % 2, t * P:(t + 1) * P], xn[:, t, k * P:(k + 1) * P], idn[:])
                    mm.then_inc(tr_x, 1)

            def qk_transposes(i, t):
                pe.wait_ge(rope_o, START + (t + 1 if i is None else NT_C + 2 * (i * TPC + t) + 2))
                if i is not None:
                    pe.wait_ge(q_ev, START + i * TPC + t)
                    for a in range(PAIRS):
                        mm = pe.transpose(ps[:, 0, a * P:(a + 1) * P], qr[:, a * P:(a + 1) * P], idn[:])
                    mm.then_inc(q_tr, 1)
                pe.wait_ge(k_ev, START + at(i, 2 * NT_C, 2 * TPC, 2 * t))
                pe.transpose(ps[:, 1, 0:P], qr[:, 512:640], idn[:]).then_inc(k_tr, 1)

            def chunk(i):
                nt = NT_C if i is None else TPC
                n = nt * P
                transposed(i)
                pe.wait_ge(hT_a, START + at(i, KD // 2, KD // 2, KD // 2))
                pe.wait_ge(hT_v, START + at(i, KD // 2, KD // 2, KD // 2))
                for c in range(C_RNN):
                    pe.wait_ge(u_ev, START + at(i, C_RNN, C_RNN, c))
                    for k in range(KD):
                        mm = pe.matmul(ps[:, 2, 0:n], win[:, k, c * P:(c + 1) * P], hT[:, k, 0:n],
                                       start=(k == 0), stop=(k == KD - 1))
                    mm.then_inc(u_mm, 1)
                    if i is not None:
                        pe.wait_ge(g_ev, START + i * C_RNN + c)
                        for k in range(KD):
                            mm = pe.matmul(ps[:, 3, 0:n], win[:, k, D_RNN + c * P:D_RNN + (c + 1) * P], hT[:, k, 0:n],
                                           start=(k == 0), stop=(k == KD - 1))
                        mm.then_inc(g_mm, 1)
                for t in range(nt):
                    bank = 4 + 2 * (t % 2)
                    m = max(t - 1, 0)
                    pe.wait_ge(v_ev, START + at(i, NT_C, TPC, m))
                    pe.wait_ge(rope_o, START + (m if i is None else NT_C + 2 * (i * TPC + m)))
                    for k in range(KD):
                        if i is not None:
                            pe.matmul(ps[:, bank, :], hT[:, k, t * P:(t + 1) * P], win[:, k, D:D + 512],
                                      start=(k == 0), stop=(k == KD - 1))
                        mm = pe.matmul(ps[:, bank + 1, 0:256], hT[:, k, t * P:(t + 1) * P], win[:, k, D + 512:D_IN],
                                       start=(k == 0), stop=(k == KD - 1))
                    mm.then_inc(qkv_mm, 1)
                    if t:
                        qk_transposes(i, t - 1)
                qk_transposes(i, nt - 1)
            pe.wait_ge(g["win_ld"], 16)
            chunk(None)
            with pe.Fori(0, SEQ // CHUNK) as i:
                chunk(i)


def phase_recurrence(nc, env):
    g = env
    sem, arena, ps, small = g["sem"], g["arena"], g["ps"], g["small"]
    names = ["x", "r0", "r1", "g0", "g1", "t0", "t1", "d0", "d1"]
    b = arena_slices(arena, B0, [(n, TIME) for n in names] + [("gate", SEQ), ("gw", 4 * P)])
    gw = b["gw"].rearrange("p (q m) -> p q m", q=4)
    par = small[:, 0:NPAR]
    lam_all = small[:, 16:16 + 2 * C_RNN]
    neg_s = small[:, 32:32 + 2 * C_RNN]
    tmp = [small[:, 48 + 8 * n:56 + 8 * n] for n in range(6)]
    s_cur = small[:, 112:116]

    lam_ld, par_ld, gw_ld, gate_ld, zero = sem("c_lam_ld"), sem("c_par_ld"), sem("c_gw_ld"), sem("c_gate_ld"), sem("c_zero")
    sp_v, sp_a, cur, conv = sem("c_sp_v"), sem("c_sp_a"), sem("c_cur"), sem("c_conv")
    g_mm, g_ev, tanh_d, exp_d, sqrt_d = sem("c_g_mm"), sem("c_g_ev"), sem("c_tanh"), sem("c_exp"), sem("c_sqrt")
    frac, drive, scan, y_done, y_st = sem("c_frac"), sem("c_drive"), sem("c_scan"), sem("c_y"), sem("c_y_st")
    segs = [(0, CTX)] + [(CTX + j * 512, 512) for j in range(4)]

    with nc.Block() as block:
        @block.sync
        def _(sp):
            sp.dma_start(lam_all, g["lam"]).then_inc(lam_ld, 16)
            sp.wait_ge(zero, START + 1)
            with sp.Fori(0, C_RNN) as i:
                sp.wait_ge(y_done, START + 2 * i)
                sp.sem_inc(g["alone"], 1)
                sp.dma_start(par, g["rg_par"].rearrange("(c p) n -> c p n", p=P)[bass.ds(i, 1)]
                             .rearrange("c p n -> (c p) n")).then_inc(par_ld, 16)
                for d in range(2):
                    for q, w in enumerate((g["rg_wa"], g["rg_wx"])):
                        for h in range(2):
                            src = w[d].rearrange("(c h) i j -> c h i j", h=2)[bass.ds(i, 1), h]\
                                .rearrange("c i j -> (c i) j")
                            sp.dma_start(gw[64 * h:64 * h + 64, 2 * d + q, 64 * h:64 * h + 64], src).then_inc(gw_ld, 16)
                sp.dma_start(b["gate"], g["gate_d"][bass.ds(i, 1)].rearrange("c p t -> (c p) t")).then_inc(gate_ld, 16)
                sp.wait_ge(y_done, START + 2 * i + 2)
                sp.sem_inc(g["alone"], 1)
                sp.dma_start(g["yT_d"][bass.ds(i, 1)].rearrange("c p t -> (c p) t"), b["gate"]).then_inc(y_st, 16)
                sp.wait_ge(y_st, START + 16 * i + 16)
                sp.sem_inc(g["alone"], 1)

        @block.vector
        def _(dve):
            nc.vector.memset(gw, 0.0).then_inc(zero, 1)
            count = [0]

            def link(ins):
                count[0] += 1
                ins.then_inc(sp_v, 1)
                dve.wait_ge(sp_v, START + count[0])
            dve.wait_ge(lam_ld, START + 16)
            link(nc.vector.tensor_scalar(tmp[0], lam_all, -1.0, None, ALU.mult))
            link(nc.vector.tensor_tensor(tmp[1], tmp[0], lam_all, ALU.min))
            link(nc.vector.tensor_scalar(tmp[0], tmp[0], 0.0, None, ALU.max))
            dve.wait_ge(sp_a, START + 1)
            link(nc.vector.tensor_scalar(tmp[3], tmp[2], 2.0, None, ALU.add))
            link(nc.vector.reciprocal(tmp[4], tmp[3]))
            link(nc.vector.tensor_tensor(tmp[3], tmp[2], tmp[4], ALU.mult))
            link(nc.vector.tensor_tensor(tmp[4], tmp[3], tmp[3], ALU.mult))
            link(nc.vector.tensor_scalar(tmp[5], tmp[4], 1.0 / 17, 1.0 / 15, ALU.mult, ALU.add))
            for q in (13, 11, 9, 7, 5, 3, 1):
                link(nc.vector.tensor_tensor(tmp[5], tmp[5], tmp[4], ALU.mult))
                link(nc.vector.tensor_scalar(tmp[5], tmp[5], 1.0 / q, None, ALU.add))
            link(nc.vector.tensor_tensor(tmp[5], tmp[5], tmp[3], ALU.mult))
            link(nc.vector.scalar_tensor_tensor(tmp[5], tmp[5], 2.0, tmp[0], ALU.mult, ALU.add))
            link(nc.vector.tensor_scalar(neg_s, tmp[5], -8.0, None, ALU.mult))
            with dve.Fori(0, C_RNN) as i:
                dve.wait_ge(par_ld, START + 16 * i + 16)
                for d in range(2):
                    dve.wait_ge(exp_d, START + 2 * i)
                    for sgn in range(2):
                        nc.vector.tensor_scalar(s_cur[:, 2 * d + sgn:2 * d + sgn + 1],
                                                small[:, bass.ds(32 + d * C_RNN + i, 1)],
                                                -1.0 if sgn == 0 else 1.0, None, ALU.mult).then_inc(cur, 1)
                dve.wait_ge(drive, START + 4 * i)
                for q in range(CONV_W):
                    dve.wait_ge(conv, START + 8 * i + 2 * q)
                    for n, (lo, ln, at) in enumerate(((0, CTX, U_CTX), (CTX, SEQ, U_LAT))):
                        src = arena[:, bass.ds(UT0 + i * U_ROW + at - 2 + q, ln)]
                        dst = b["x"][:, lo:lo + ln]
                        if q == 0:
                            nc.vector.tensor_scalar(dst, src, par[:, 0:1], par[:, 4:5], ALU.mult, ALU.add)\
                                .then_inc(conv, 1)
                        else:
                            nc.vector.scalar_tensor_tensor(dst, src, par[:, q:q + 1], dst, ALU.mult, ALU.add)\
                                .then_inc(conv, 1)
                for d in range(2):
                    T, Dn, G, R = b[f"t{d}"], b[f"d{d}"], b[f"g{d}"], b[f"r{d}"]
                    dve.wait_ge(y_done, START + 2 * i)
                    dve.wait_ge(exp_d, START + 2 * i + d + 1)
                    nc.vector.tensor_tensor(Dn, R, R, ALU.mult).then_inc(frac, 1)
                    dve.wait_ge(frac, START + 4 * i + 2 * d + 1)
                    nc.vector.scalar_tensor_tensor(T, Dn, 1.0, T, ALU.add, ALU.mult).then_inc(frac, 1)
                    dve.wait_ge(g_ev, START + 20 * i + 10 * d + 10)
                    nc.vector.tensor_tensor(G, G, b["x"], ALU.mult).then_inc(drive, 1)
                for d in range(2):
                    T, Dn, G, R = b[f"t{d}"], b[f"d{d}"], b[f"g{d}"], b[f"r{d}"]
                    dve.wait_ge(sqrt_d, START + 2 * i + d + 1)
                    nc.vector.tensor_tensor(G, G, T, ALU.mult).then_inc(drive, 1)
                    dve.wait_ge(drive, START + 4 * i + 3 + d)
                    if d == 0:
                        nc.vector.tensor_tensor_scan(Dn, R, G, 0.0, ALU.mult, ALU.add).then_inc(scan, 1)
                    else:
                        nc.vector.tensor_tensor_scan(Dn[:, CTX - 1::-1], R[:, CTX - 1::-1], G[:, CTX - 1::-1], 0.0,
                                                     ALU.mult, ALU.add).then_inc(scan, 1)
                        dve.wait_ge(scan, START + 3 * i + 2)
                        nc.vector.tensor_tensor_scan(Dn[:, TIME - 1:CTX - 1:-1], R[:, TIME - 1:CTX - 1:-1],
                                                     G[:, TIME - 1:CTX - 1:-1], Dn[:, 0:1],
                                                     ALU.mult, ALU.add).then_inc(scan, 1)
                dve.wait_ge(scan, START + 3 * i + 3)
                dve.wait_ge(gate_ld, START + 16 * i + 16)
                nc.vector.tensor_tensor(b["d0"][:, CTX:TIME], b["d0"][:, CTX:TIME], b["d1"][:, CTX:TIME], ALU.add)\
                    .then_inc(y_done, 1)
                dve.wait_ge(y_done, START + 2 * i + 1)
                nc.vector.tensor_tensor(b["gate"], b["d0"][:, CTX:TIME], b["gate"], ALU.mult).then_inc(y_done, 1)

        @block.scalar
        def _(act):
            act.wait_ge(sp_v, START + 3)
            nc.scalar.activation(tmp[2], tmp[1], ACT.Exp).then_inc(sp_a, 1)
            with act.Fori(0, C_RNN) as i:
                for d in range(2):
                    for q in range(2):
                        dst = b[f"{'rg'[q]}{d}"]
                        if q == 0:
                            act.wait_ge(scan, START + 3 * i)
                        for n, (lo, ln) in enumerate(segs):
                            idx = (2 * d + q) * 5 + n
                            act.wait_ge(g_mm, START + 20 * i + idx + 1)
                            nc.scalar.activation(dst[:, lo:lo + ln], ps[:, idx % 4, 0:ln], ACT.Sigmoid,
                                                 bias=par[:, 5 + 2 * q + d:6 + 2 * q + d]).then_inc(g_ev, 1)
                act.wait_ge(cur, START + 4 * i + 4)
                act.wait_ge(g_ev, START + 20 * i + 20)
                for d in range(2):
                    nc.scalar.activation(b[f"t{d}"], b[f"r{d}"], ACT.Tanh, scale=s_cur[:, 2 * d:2 * d + 1])\
                        .then_inc(tanh_d, 1)
                act.wait_ge(tanh_d, START + 2 * i + 2)
                for d in range(2):
                    nc.scalar.activation(b[f"r{d}"], b[f"r{d}"], ACT.Exp, scale=s_cur[:, 2 * d + 1:2 * d + 2])\
                        .then_inc(exp_d, 1)
                act.wait_ge(exp_d, START + 2 * i + 2)
                for d in range(2):
                    act.wait_ge(frac, START + 4 * i + 2 * d + 2)
                    nc.scalar.activation(b[f"t{d}"], b[f"t{d}"], ACT.Sqrt).then_inc(sqrt_d, 1)

        @block.tensor
        def _(pe):
            with pe.Fori(0, C_RNN) as i:
                pe.wait_ge(gw_ld, START + 128 * i + 128)
                pe.wait_ge(conv, START + 8 * i + 8)
                for dq in range(4):
                    for n, (lo, ln) in enumerate(segs):
                        idx = dq * 5 + n
                        pe.wait_ge(g_ev, START + 20 * i + max(idx - 3, 0))
                        pe.matmul(ps[:, idx % 4, 0:ln], gw[:, dq, :], b["x"][:, lo:lo + ln], start=True, stop=True)\
                            .then_inc(g_mm, 1)


def phase_attention(nc, env):
    g = env
    sem, arena, ps, ps_row, small, idn = g["sem"], g["arena"], g["ps"], g["ps_row"], g["small"], g["idn"]
    b = arena_slices(arena, B0, [("mask0", KEYS), ("mask1", KEYS), ("q0", 512), ("q1", 512), ("s0", KEYS), ("s1", KEYS),
                                 ("pT0", KEYS), ("pT1", KEYS), ("o", 512)])
    sinks = small[:, 0:NH]
    mx = small[:, 8:16]
    nm = small[:, 16:24]
    den = small[:, 24:32]
    es = small[:, 32:40]
    rd = small[:, 40:48]
    mask_ld, q_ld, s_mm, s_max, nm_d, p_d = sem("d_mask_ld"), sem("d_q_ld"), sem("d_s_mm"), sem("d_s_max"), sem("d_nm"), sem("d_p")
    p_tr, p_ev, pv_mm = sem("d_p_tr"), sem("d_p_ev"), sem("d_pv")
    o_free = sem("d_o_free")
    es_d, es_e, den_d, o_d, o_st = sem("d_es"), sem("d_es_e"), sem("d_den"), sem("d_o"), g["plain_sem"]("d_o_st")

    with nc.Block() as block:
        @block.sync
        def _(sp):
            sp.dma_start(sinks, g["sink"]).then_inc(mask_ld, 16)
            with sp.Fori(0, T_LAT // 2) as i:
                for j in range(2):
                    sp.wait_ge(s_mm, START + 16 * i)
                    sp.wait_ge(s_max, START + 16 * i)
                    sp.sem_inc(g["alone"], 1)
                    kind = ((2 * i + j + 15) >> 4) + ((2 * i + j + 1) >> 4)
                    sp.dma_start(b[f"mask{j}"], g["masks"][bass.ds(kind, 1)].rearrange("m p k -> (m p) k")).then_inc(q_ld, 16)
                    sp.dma_start(b[f"q{j}"], g["qT_d"][bass.ds(2 * i + j, 1)].rearrange("n p d -> (n p) d")).then_inc(q_ld, 16)
                    sp.wait_ge(q_ld, START + 64 * i + 32 * j + 32)
                    sp.sem_inc(g["alone"], 1)

        @block.gpsimd
        def _(pool):
            with pool.Fori(0, T_LAT) as i:
                pool.wait_ge(o_d, START + i + 1)
                pool.sem_inc(g["alone"], 1)
                pool.dma_start(g["attn_d"][bass.ds(i, 1)].rearrange("n p d -> (n p) d"), b["o"]).then_inc(o_st, 16)
                pool.wait_ge(o_st, 16 * i + 16)
                pool.sem_inc(o_free, 1)

        @block.tensor
        def _(pe):
            def scores(i, j, h):
                t = 2 * i + j
                z, a = h // PAIRS, h % PAIRS
                n = i * 16 + j * NH + h
                if h == 0:
                    pe.wait_ge(q_ld, START + 64 * i + 32 * j + 32)
                pe.wait_ge(s_max, START + i * 16 + max(j * NH + h - 1, 0))
                q = b[f"q{j}"][:, a * P:(a + 1) * P]
                s0 = (h % 2) * 1024
                pe.matmul(ps_row[:, s0:s0 + CTX], q, arena[:, KT0 + z * K_ROW:KT0 + z * K_ROW + CTX], start=True, stop=True)
                k0 = KT0 + z * K_ROW + K_LAT - P
                pe.matmul(ps_row[:, s0 + CTX:s0 + 512], q, arena[:, bass.ds(k0 + t * P, 256)], start=True, stop=True)
                pe.matmul(ps_row[:, s0 + 512:s0 + KEYS], q, arena[:, bass.ds(k0 + t * P + 256, P)],
                          start=True, stop=True).then_inc(s_mm, 1)

            def transposes(i, j, h):
                n = i * 16 + j * NH + h
                pe.wait_ge(p_d, START + n + 1)
                pe.wait_ge(p_ev, START + 2 * n)
                for q in range(KEYS // P):
                    mm = pe.transpose(ps_row[:, 2048 + q * P:2048 + (q + 1) * P], b[f"s{h % 2}"][:, q * P:(q + 1) * P], idn[:])
                mm.then_inc(p_tr, 1)

            def values(i, j, h):
                t = 2 * i + j
                n = i * 16 + j * NH + h
                z = h // PAIRS
                pe.wait_ge(p_ev, START + 2 * n + 2)
                if h == 0:
                    pe.wait_ge(o_d, START + 2 * i + j)
                for q in range(KEYS // P):
                    v = arena[:, V0 + q * P + z * HD:V0 + q * P + (z + 1) * HD] if q < 2 else \
                        arena[:, bass.ds(V0 + q * P + z * HD + t * P, HD)]
                    mm = pe.matmul(ps[:, 6, h * HD:(h + 1) * HD], b[f"pT{h % 2}"][:, q * P:(q + 1) * P], v,
                                   start=(q == 0), stop=(q == KEYS // P - 1))
                mm.then_inc(pv_mm, 1)
            with pe.Fori(0, T_LAT // 2) as i:
                for j in range(2):
                    scores(i, j, 0)
                    for h in range(NH):
                        if h + 1 < NH:
                            scores(i, j, h + 1)
                        transposes(i, j, h)
                        if h:
                            values(i, j, h - 1)
                    values(i, j, NH - 1)

        @block.vector
        def _(dve):
            dve.wait_ge(mask_ld, START + 16)

            def smax(i, j, h):
                t = 2 * i + j
                n = i * 16 + j * NH + h
                dve.wait_ge(s_mm, START + n + 1)
                if h == 0:
                    dve.wait_ge(q_ld, START + 64 * i + 32 * j + 32)
                dve.wait_ge(p_tr, START + i * 16 + max(j * NH + h - 1, 0))
                dve.sem_inc(g["alone"], 1)
                nc.vector.tensor_tensor_reduce(b[f"s{h % 2}"], ps_row[:, (h % 2) * 1024:(h % 2) * 1024 + KEYS],
                                               b[f"mask{j}"],
                                               1.0, NEG, ALU.add, ALU.max, mx[:, h:h + 1]).then_inc(s_max, 1)
                dve.wait_ge(s_max, START + n + 1)
                if h == 0:
                    dve.wait_ge(es_d, START + 2 * (2 * i + j))
                nc.vector.tensor_scalar(nm[:, h:h + 1], mx[:, h:h + 1], sinks[:, h:h + 1], -1.0, ALU.max, ALU.mult)\
                    .then_inc(nm_d, 1)

            def copy_pT(i, j, h):
                n = i * 16 + j * NH + h
                dve.wait_ge(p_tr, START + n + 1)
                dve.wait_ge(pv_mm, START + i * 16 + max(j * NH + h - 1, 0))
                nc.vector.tensor_copy(b[f"pT{h % 2}"][:, 512:KEYS], ps_row[:, 2048 + 512:2048 + KEYS]).then_inc(p_ev, 1)
            with dve.Fori(0, T_LAT // 2) as i:
                for j in range(2):
                    t = 2 * i + j
                    for h in range(NH):
                        smax(i, j, h)
                        if h:
                            copy_pT(i, j, h - 1)
                    copy_pT(i, j, NH - 1)
                    dve.wait_ge(nm_d, START + NH * t + NH)
                    nc.vector.tensor_tensor(es, sinks, nm, ALU.add).then_inc(es_d, 1)
                    dve.wait_ge(es_d, START + 2 * t + 2)
                    nc.vector.tensor_tensor(den, den, es, ALU.add).then_inc(den_d, 1)
                    dve.wait_ge(den_d, START + 2 * t + 1)
                    nc.vector.reciprocal(rd, den).then_inc(den_d, 1)
                    dve.wait_ge(den_d, START + 2 * t + 2)
                    dve.wait_ge(pv_mm, START + NH * t + NH)
                    dve.wait_ge(o_free, START + t)
                    nc.vector.tensor_tensor(b["o"].rearrange("p (h d) -> p h d", h=NH),
                                            ps[:, 6, :].rearrange("p (h d) -> p h d", h=NH),
                                            rd.rearrange("p (h o) -> p h o", o=1).to_broadcast([P, NH, HD]),
                                            ALU.mult).then_inc(o_d, 1)

        @block.scalar
        def _(act):
            def copy_pT(i, j, h):
                n = i * 16 + j * NH + h
                act.wait_ge(p_tr, START + n + 1)
                act.wait_ge(pv_mm, START + i * 16 + max(j * NH + h - 1, 0))
                nc.scalar.activation(b[f"pT{h % 2}"][:, 0:512], ps_row[:, 2048:2048 + 512], ACT.Copy).then_inc(p_ev, 1)
            with act.Fori(0, T_LAT // 2) as i:
                for j in range(2):
                    t = 2 * i + j
                    for h in range(NH):
                        n = i * 16 + j * NH + h
                        act.wait_ge(nm_d, START + n + 1)
                        if h == 0:
                            act.wait_ge(den_d, START + 2 * t)
                        nc.scalar.activation(b[f"s{h % 2}"], b[f"s{h % 2}"], ACT.Exp, bias=nm[:, h:h + 1],
                                             accum_out=den[:, h:h + 1]).then_inc(p_d, 1)
                        if h:
                            copy_pT(i, j, h - 1)
                    copy_pT(i, j, NH - 1)
                    act.wait_ge(es_d, START + 2 * t + 1)
                    act.wait_ge(p_d, START + NH * t + NH)
                    nc.scalar.activation(es, es, ACT.Exp).then_inc(es_d, 1)


def phase_output(nc, env):
    g = env
    sem, arena, ps, ps_row, small, idn = g["sem"], g["arena"], g["ps"], g["ps_row"], g["small"], g["idn"]
    b = arena_slices(arena, 0, [("logits", T_LAT * 36), ("wo", KD * D), ("whi", KD * D // 2), ("wlo", KD * D // 2), ("g1", D),
                                ("sc2", D), ("sh2", D), ("l1g", D), ("l1b", D), ("wr", KD * 36), ("br", 36), ("gnc", KD),
                                ("ones", 1), ("mh", 2), ("ysq", 512), ("asq", 512)]
                     + [(n, 256) for n in ("yhi", "ylo", "ahi", "alo")]
                     + [(f"{n}{j}", s) for n, s in (("yT", 512), ("at", 512), ("xt", D), ("x1", D), ("h2", D)) for j in range(2)]
                     + [("t0", D), ("t1", D), ("x1n", D), ("h2T", D)])
    wo = b["wo"].rearrange("p (k n) -> p k n", k=KD)
    whi, wlo = (b[n].bitcast(F16).rearrange("p (k n) -> p k n", k=KD) for n in ("whi", "wlo"))
    yhi, ylo, ahi, alo = (b[n].bitcast(F16) for n in ("yhi", "ylo", "ahi", "alo"))
    wr = b["wr"].rearrange("p (k n) -> p k n", k=KD)
    ss = [small[:, 8 * j:8 * j + 2] for j in range(2)]
    ssv = [small[:, 8 * j + 2:8 * j + 4] for j in range(2)]
    sr = [small[:, 8 * j + 4:8 * j + 6] for j in range(2)]
    st = small[:, 16:28]
    mv = small[:, 28:30]
    ve = small[:, 30:31]
    rs = small[:, 31:32]
    w_ld, w_ok, w_hi, w_lo, p_ok = sem("e_w_ld"), sem("e_w_ok"), sem("e_w_hi"), sem("e_w_lo"), sem("e_p_ok")
    in_ld, xt_ld = [sem("e_in_ld0"), sem("e_in_ld1")], [sem("e_xt_ld0"), sem("e_xt_ld1")]
    x_st, h_st = [sem("e_x_st0"), sem("e_x_st1")], [sem("e_h_st0"), sem("e_h_st1")]
    sq, y_hi, y_lo, ssm, ss_d, ssv_d, pw_s = (sem("e_sq"), sem("e_y_hi"), sem("e_y_lo"), sem("e_ssm"), sem("e_ss"), sem("e_ssv"),
                                              sem("e_pw_s"))
    a_tr, a_hi, a_lo = sem("e_a_tr"), sem("e_a_hi"), sem("e_a_lo")
    o_mm, o_act, v, pw = sem("e_o_mm"), sem("e_o_act"), sem("e_v"), sem("e_pw")
    h_tr, h_ev, r_mm, lg = sem("e_h_tr"), sem("e_h_ev"), sem("e_r_mm"), sem("e_lg")
    scale = W_SCALE * X_SCALE
    NV = 14

    def row(src):
        return src.to_broadcast([P, src.shape[1]])

    def tiles(eng, prepare, project, normalise, route):
        def step(t, j, first=False, second=False, last=False):
            project(t, j)
            if not first:
                normalise(t - 1, 1 - j)
            if not last:
                prepare(t + 1, 1 - j)
            if not first and not second:
                route(t - 2, j)
        prepare(0, 0)
        step(0, 0, first=True)
        step(1, 1, second=True)
        with eng.Fori(1, T_LAT // 2 - 1) as i:
            step(2 * i, 0)
            step(2 * i + 1, 1)
        step(T_LAT - 2, 0)
        step(T_LAT - 1, 1, last=True)
        normalise(T_LAT - 1, 1)
        route(T_LAT - 2, 0)
        route(T_LAT - 1, 1)

    def none(t, j):
        pass

    def half(t):
        return t // 2 if isinstance(t, int) else t >> 1
    with nc.Block() as block:
        @block.sync
        def _(sp):
            sp.dma_start(wo, g["w_out"].rearrange("(k p) n -> p k n", p=P)).then_inc(w_ld, 16)
            for name, src in (("g1", g["mod_rows"][0:1, 2 * D:3 * D]), ("sh2", g["mod_rows"][0:1, 3 * D:4 * D]),
                              ("sc2", g["mod_rows"][0:1, 4 * D:5 * D]), ("l1g", g["ln1"][0:1, :]),
                              ("l1b", g["ln1"][1:2, :]), ("br", g["router_b"])):
                sp.dma_start(b[name], row(src)).then_inc(w_ld, 16)
            sp.dma_start(wr, g["router"].rearrange("(k p) n -> p k n", p=P)).then_inc(w_ld, 16)
            sp.dma_start(b["gnc"], g["gn"]).then_inc(w_ld, 16)

            def load_in(t, j):
                sp.dma_start(b[f"yT{j}"].rearrange("p (c t) -> p c t", c=C_RNN),
                             g["yT_d"][:, :, bass.ds(t * P, P)].rearrange("c p t -> p c t")).then_inc(in_ld[j], 16)
                sp.dma_start(b[f"at{j}"], g["attn_d"][bass.ds(t, 1)].rearrange("n p d -> (n p) d")).then_inc(in_ld[j], 16)

            def load_x(t, j):
                sp.dma_start(b[f"xt{j}"], g["x"][bass.ds(t * P, P), :]).then_inc(xt_ld[j], 16)

            def stores(t, j):
                sp.wait_ge(v, START + NV * t + 8)
                sp.sem_inc(g["alone"], 1)
                sp.dma_start(g["x1_d"][bass.ds(t * P, P), :], b[f"x1{j}"]).then_inc(x_st[j], 16)
                sp.wait_ge(v, START + NV * t + 14)
                sp.sem_inc(g["alone"], 1)
                sp.dma_start(g["h2_d"][bass.ds(t * P, P), :], b[f"h2{j}"]).then_inc(h_st[j], 16)

            for j in range(2):
                load_in(j, j)
                load_x(j, j)
            with sp.Fori(0, T_LAT // 2 - 1) as i:
                for j in range(2):
                    t = 2 * i + j
                    sp.wait_ge(y_lo, START + t + 1)
                    sp.sem_inc(g["alone"], 1)
                    sp.wait_ge(a_lo, START + t + 1)
                    sp.sem_inc(g["alone"], 1)
                    sp.wait_ge(sq, START + 2 * t + 2)
                    sp.sem_inc(g["alone"], 1)
                    load_in(t + 2, j)
                    stores(t, j)
                    load_x(t + 2, j)
            for j in range(2):
                stores(T_LAT - 2 + j, j)
            for j in range(2):
                sp.wait_ge(x_st[j], START + 16 * (T_LAT // 2))
                sp.wait_ge(h_st[j], START + 16 * (T_LAT // 2))

        @block.gpsimd
        def _(pool):
            nc.gpsimd.memset(b["mh"], -0.5).then_inc(p_ok, 1)
            nc.gpsimd.memset(b["ones"], 1.0).then_inc(p_ok, 1)
            pool.wait_ge(p_ok, START + 2)

            def prepare(t, j):
                pool.wait_ge(ssv_d, START + t + 1)
                pool.sem_inc(g["alone"], 1)
                nc.gpsimd.tensor_tensor(sr[j], ssv[j], b["mh"], ALU.pow).then_inc(pw_s, 1)

            def normalise(t, j):
                for n in (6, 12):
                    pool.wait_ge(v, START + NV * t + n)
                    pool.sem_inc(g["alone"], 1)
                    nc.gpsimd.tensor_tensor(rs, ve, b["mh"][:, 0:1], ALU.pow).then_inc(pw, 1)
            tiles(pool, prepare, none, normalise, none)

        @block.vector
        def _(dve):
            dve.wait_ge(w_ld, START + 16 * 9)
            for k in range(KD):
                nc.vector.scalar_tensor_tensor(wo[:, k, :], wo[:, k, :], b["gnc"][:, k:k + 1], b["g1"], ALU.mult, ALU.mult)\
                    .then_inc(w_ok, 1)
            nc.vector.tensor_scalar(b["sc2"], b["sc2"], 1.0, None, ALU.add).then_inc(w_ok, 1)
            dve.wait_ge(w_ok, START + KD + 1)
            for k in range(KD):
                dve.wait_ge(w_hi, START + k + 1)
                nc.vector.scalar_tensor_tensor(wlo[:, k, :], wo[:, k, :], W_SCALE, whi[:, k, :], ALU.mult, ALU.subtract)\
                    .then_inc(w_lo, 1)

            def prepare(t, j):
                dve.wait_ge(y_hi, START + t + 1)
                dve.wait_ge(o_mm, START + t)
                nc.vector.scalar_tensor_tensor(ylo, b[f"yT{j}"], X_SCALE, yhi, ALU.mult, ALU.subtract).then_inc(y_lo, 1)
                dve.wait_ge(a_hi, START + t + 1)
                nc.vector.scalar_tensor_tensor(alo, ps[:, 6, :], X_SCALE, ahi, ALU.mult, ALU.subtract).then_inc(a_lo, 1)
                dve.wait_ge(ss_d, START + t + 1)
                dve.wait_ge(sq, START + 2 * t + 2)
                nc.vector.tensor_scalar(ssv[j], ss[j], scale * scale / 512, scale * scale * EPS, ALU.mult, ALU.add)\
                    .then_inc(ssv_d, 1)

            def normalise(t, j):
                base = NV * t
                step = [0]

                def link(ins):
                    step[0] += 1
                    ins.then_inc(v, 1)
                    dve.wait_ge(v, START + base + step[0])
                t1, x1, x1n, h2 = b["t1"], b[f"x1{j}"], b["x1n"], b[f"h2{j}"]
                dve.wait_ge(o_act, START + t + 1)
                link(nc.vector.scalar_tensor_tensor(t1, ps_row[:, 2048:3072], sr[j][:, 1:2], b["t0"], ALU.mult, ALU.add))
                dve.wait_ge(xt_ld[j], START + 16 * half(t) + 16)
                link(nc.vector.scalar_tensor_tensor(t1, b[f"xt{j}"], ALPHA, t1, ALU.mult, ALU.add))
                nc.vector.bn_stats(st[:, 0:6], t1[:, 0:512]).then_inc(v, 1)
                step[0] += 1
                link(nc.vector.bn_stats(st[:, 6:12], t1[:, 512:1024]))
                dve.sem_inc(g["alone"], 1)
                link(nc.vector.bn_aggr(mv, st.rearrange("p (a s) -> p a s", a=2)))
                link(nc.vector.tensor_scalar(ve, mv[:, 1:2], EPS, None, ALU.add))
                link(nc.vector.scalar_tensor_tensor(t1, t1, mv[:, 0:1], b["l1g"], ALU.subtract, ALU.mult))
                dve.wait_ge(pw, START + 2 * t + 1)
                dve.wait_ge(x_st[j], START + 16 * half(t))
                link(nc.vector.scalar_tensor_tensor(x1, t1, rs, b["l1b"], ALU.mult, ALU.add))
                nc.vector.bn_stats(st[:, 0:6], x1[:, 0:512]).then_inc(v, 1)
                step[0] += 1
                link(nc.vector.bn_stats(st[:, 6:12], x1[:, 512:1024]))
                dve.sem_inc(g["alone"], 1)
                link(nc.vector.bn_aggr(mv, st.rearrange("p (a s) -> p a s", a=2)))
                link(nc.vector.tensor_scalar(ve, mv[:, 1:2], EPS, None, ALU.add))
                link(nc.vector.scalar_tensor_tensor(x1n, x1, mv[:, 0:1], b["sc2"], ALU.subtract, ALU.mult))
                dve.wait_ge(pw, START + 2 * t + 2)
                dve.wait_ge(h_st[j], START + 16 * half(t))
                if not isinstance(t, int) or t > 1:
                    dve.wait_ge(h_tr, START + 2 * t - 2)
                link(nc.vector.scalar_tensor_tensor(h2, x1n, rs, b["sh2"], ALU.mult, ALU.add))

            def route(t, j):
                dve.wait_ge(r_mm, START + t + 1)
                nc.vector.tensor_tensor(arena[:, bass.ds(t * 36, 36)], ps[:, 7, 0:36], b["br"], ALU.add).then_inc(lg, 1)
            tiles(dve, prepare, none, normalise, route)

        @block.scalar
        def _(act):
            for k in range(KD):
                act.wait_ge(w_ok, START + k + 1)
                nc.scalar.activation(whi[:, k, :], wo[:, k, :], ACT.Copy, scale=W_SCALE).then_inc(w_hi, 1)

            def prepare(t, j):
                act.wait_ge(in_ld[j], START + 32 * half(t) + 32)
                act.wait_ge(ssm, START + t)
                nc.scalar.activation(b["ysq"], b[f"yT{j}"], ACT.Square).then_inc(sq, 1)
                act.wait_ge(ssv_d, START + t)
                nc.scalar.activation(b["asq"], b[f"at{j}"], ACT.Square, accum_out=ss[j][:, 1:2]).then_inc(sq, 1)
                act.wait_ge(o_mm, START + t)
                nc.scalar.activation(yhi, b[f"yT{j}"], ACT.Copy, scale=X_SCALE).then_inc(y_hi, 1)
                act.wait_ge(a_tr, START + t + 1)
                nc.scalar.activation(ahi, ps[:, 6, :], ACT.Copy, scale=X_SCALE).then_inc(a_hi, 1)
                act.wait_ge(ssm, START + t + 1)
                nc.scalar.activation(ss[j][:, 0:1], ps[:, 0, 0:1], ACT.Copy).then_inc(ss_d, 1)

            def normalise(t, j):
                act.wait_ge(o_mm, START + t + 1)
                act.wait_ge(pw_s, START + t + 1)
                if not isinstance(t, int) or t > 0:
                    act.wait_ge(v, START + NV * t - NV + 1)
                nc.scalar.activation(b["t0"], ps_row[:, 1024:2048], ACT.Copy, scale=sr[j][:, 0:1]).then_inc(o_act, 1)

            def route(t, j):
                for n in range(2):
                    act.wait_ge(h_tr, START + 2 * t + n + 1)
                    if n == 0:
                        act.wait_ge(r_mm, START + t)
                    nc.scalar.activation(b["h2T"][:, n * 512:(n + 1) * 512], ps[:, n, :], ACT.Copy).then_inc(h_ev, 1)
            tiles(act, prepare, none, normalise, route)

        @block.tensor
        def _(pe):
            pe.wait_ge(p_ok, START + 2)
            pe.wait_ge(w_lo, START + KD)

            def prepare(t, j):
                pe.wait_ge(in_ld[j], START + 32 * half(t) + 32)
                pe.wait_ge(a_lo, START + t)
                for c in range(C_RNN):
                    mm = pe.transpose(ps[:, 6, c * P:(c + 1) * P], b[f"at{j}"][:, c * P:(c + 1) * P], idn[:])
                mm.then_inc(a_tr, 1)
                pe.wait_ge(sq, START + 2 * t + 1)
                if not isinstance(t, int) or t > 3:
                    pe.wait_ge(h_ev, START + 2 * t - 6)
                for c in range(C_RNN):
                    mm = pe.matmul(ps[:, 0, 0:1], b["ysq"][:, c * P:(c + 1) * P], b["ones"], start=(c == 0), stop=(c == C_RNN - 1))
                mm.then_inc(ssm, 1)

            def project(t, j):
                for bank, high, low, k0, ready in ((2, yhi, ylo, 0, y_lo), (4, ahi, alo, C_RNN, a_lo)):
                    pe.wait_ge(ready, START + t + 1)
                    if bank == 2:
                        pe.wait_ge(o_act, START + t)
                    elif not isinstance(t, int) or t > 0:
                        pe.wait_ge(v, START + NV * t - NV + 1)
                    for k in range(C_RNN):
                        for n in range(2):
                            o, cols = ps[:, bank + n, :], slice(n * 512, (n + 1) * 512)
                            lhs_hi, lhs_lo = high[:, k * P:(k + 1) * P], low[:, k * P:(k + 1) * P]
                            pe.matmul(o, lhs_hi, whi[:, k0 + k, cols], start=(k == 0), stop=False)
                            pe.matmul(o, lhs_hi, wlo[:, k0 + k, cols], start=False, stop=False)
                            mm = pe.matmul(o, lhs_lo, whi[:, k0 + k, cols], start=False, stop=(k == C_RNN - 1))
                mm.then_inc(o_mm, 1)

            def route(t, j):
                pe.wait_ge(v, START + NV * t + 14)
                pe.wait_ge(ss_d, START + t + 4 if not isinstance(t, int) else START + min(t + 4, T_LAT))
                pe.wait_ge(h_ev, START + 2 * t)
                for n in range(2):
                    for c in range(4):
                        mm = pe.transpose(ps[:, n, c * P:(c + 1) * P], b[f"h2{j}"][:, (4 * n + c) * P:(4 * n + c + 1) * P], idn[:])
                    mm.then_inc(h_tr, 1)
                pe.wait_ge(h_ev, START + 2 * t + 2)
                pe.wait_ge(lg, START + t)
                for k in range(KD):
                    mm = pe.matmul(ps[:, 7, 0:36], b["h2T"][:, k * P:(k + 1) * P], wr[:, k, :], start=(k == 0), stop=(k == KD - 1))
                mm.then_inc(r_mm, 1)
            tiles(pe, prepare, project, none, route)


def phase_route(nc, env):
    g = env
    sem, arena, ps, ps_row, idn = g["sem"], g["arena"], g["ps"], g["ps_row"], g["idn"]
    T = T_LAT
    names = [("logits", T * 36), ("pad8", T * 8), ("gm8", T * 8), ("gi8", T * 8), ("gif", T), ("goh", T * NG),
             ("elm", T * NE), ("em8", T * 8), ("ei8", T * 8), ("eif", 2 * T), ("gex", T * NG), ("gsum", T), ("pg", T),
             ("dif", T), ("q", T), ("oh0", T * NE), ("oh1", T * NE), ("ohs", T * NE), ("base", (T + 1) * NE),
             ("rank", T * NE), ("sel", T * NE), ("slotf", 2 * T), ("nbi", NE), ("nb", NE), ("pend", NE), ("pst", NE),
             ("one32", NE), ("ones", P), ("tri", P), ("iota", 64), ("tok", T), ("ge", 64 * NE), ("has", NE), ("rk", NE), ("rend", NE), ("ebf", 64), ("nw", 64),
             ("st_i", P), ("st_f", P)]
    b = arena_slices(arena, 0, names)
    v3 = lambda name, t, n: b[name].rearrange("p (t n) -> p t n", t=t)
    slot_i, gates, tab, gidx = g["slot_i"], g["gates"], g["blk_tab"], g["gidx"]
    f_ld, v, act_d, mm, scat, tab_ld, tr = sem("f_ld"), sem("f_v"), sem("f_act"), sem("f_mm"), g["plain_sem"]("f_scat"), sem("f_tab_ld"), sem("f_tr")
    mark = {}

    with nc.Block() as block:
        @block.vector
        def _(dve):
            n = [0]

            def link(ins, name=None):
                n[0] += 1
                ins.then_inc(v, 1)
                dve.wait_ge(v, START + n[0])
                if name:
                    mark[name] = n[0]
            V = nc.vector
            lg = v3("logits", T, 36)
            link(V.memset(b["pad8"], NEG))
            link(V.memset(b["one32"], 1.0))
            link(V.memset(b["ones"], 1.0))
            link(V.memset(b["base"][:, 0:NE], 0.0))
            link(V.tensor_copy(v3("pad8", T, 8)[:, :, 0:NG], lg[:, :, 0:NG]))
            for t in range(T):
                link(V.max(v3("gm8", T, 8)[:, t, :], v3("pad8", T, 8)[:, t, :]))
                link(V.max_index(v3("gi8", T, 8)[:, t, :].bitcast(U32), v3("gm8", T, 8)[:, t, :], v3("pad8", T, 8)[:, t, :]))
            link(V.tensor_copy(b["gif"], v3("gi8", T, 8)[:, :, 0].bitcast(U32)))
            dve.wait_ge(f_ld, START + 48)
            io4 = b["iota"][:, 0:NG].rearrange("p (o n) -> p o n", o=1).to_broadcast([P, T, NG])
            link(V.tensor_tensor(v3("goh", T, NG), io4, b["gif"].rearrange("p (t o) -> p t o", o=1).to_broadcast([P, T, NG]),
                                 ALU.is_equal))
            link(V.tensor_scalar(b["goh"], b["goh"], 1.0, -NEG, ALU.subtract, ALU.mult))
            link(V.tensor_tensor(b["elm"].rearrange("p (t g e) -> p t g e", t=T, g=NG),
                                 lg[:, :, NG:36].rearrange("p t (g e) -> p t g e", g=NG),
                                 v3("goh", T, NG).rearrange("p t (g o) -> p t g o", o=1).to_broadcast([P, T, NG, EPG]), ALU.add))
            for t in range(T):
                link(V.max(v3("em8", T, 8)[:, t, :], v3("elm", T, NE)[:, t, :]))
                link(V.max_index(v3("ei8", T, 8)[:, t, :].bitcast(U32), v3("em8", T, 8)[:, t, :], v3("elm", T, NE)[:, t, :]))
            link(V.tensor_copy(b["eif"].rearrange("p (k t) -> p t k", k=2), v3("ei8", T, 8)[:, :, 0:2].bitcast(U32)))
            io32 = b["iota"][:, 0:NE].rearrange("p (o n) -> p o n", o=1).to_broadcast([P, T, NE])
            for k in range(2):
                idx = b["eif"][:, k * T:(k + 1) * T].rearrange("p (t o) -> p t o", o=1).to_broadcast([P, T, NE])
                link(V.tensor_tensor(v3(f"oh{k}", T, NE), io32, idx, ALU.is_equal))
            link(V.tensor_tensor(b["ohs"], b["oh0"], b["oh1"], ALU.add), "onehot")
            link(V.tensor_tensor(v3("gex", T, NG), lg[:, :, 0:NG], v3("gm8", T, 8)[:, :, 0:1].to_broadcast([P, T, NG]),
                                 ALU.subtract))
            link(V.tensor_tensor(b["dif"], v3("em8", T, 8)[:, :, 1], v3("em8", T, 8)[:, :, 0], ALU.subtract), "exps")
            dve.wait_ge(mm, START + 2)
            for t in range(T):
                link(V.tensor_tensor(b["base"][:, (t + 1) * NE:(t + 2) * NE], b["base"][:, t * NE:(t + 1) * NE],
                                     ps[:, 1, t * NE:(t + 1) * NE], ALU.add))
            cnt = b["base"][:, T * NE:(T + 1) * NE]
            link(V.tensor_tensor(b["rank"], ps[:, 0, :], b["base"][:, 0:T * NE], ALU.add))
            link(V.tensor_scalar(b["nbi"].bitcast(I32), cnt, float(P - 1), None, ALU.add))
            link(V.tensor_scalar(b["nbi"].bitcast(I32), b["nbi"].bitcast(I32), 7, None, ALU.arith_shift_right))
            link(V.tensor_copy(b["nb"], b["nbi"].bitcast(I32)))
            link(V.tensor_tensor_scan(b["pend"], b["one32"], b["nb"], 0.0, ALU.mult, ALU.add))
            link(V.tensor_tensor(b["pst"], b["pend"], b["nb"], ALU.subtract))
            link(V.tensor_scalar(b["pst"], b["pst"], float(P), None, ALU.mult))
            link(V.tensor_tensor(v3("rank", T, NE), v3("rank", T, NE),
                                 b["pst"].rearrange("p (o n) -> p o n", o=1).to_broadcast([P, T, NE]), ALU.add))
            for k in range(2):
                link(V.tensor_tensor(b["sel"], b["rank"], b[f"oh{k}"], ALU.mult))
                link(V.tensor_reduce(b["slotf"][:, k * T:(k + 1) * T], v3("sel", T, NE), AX_X, ALU.add))
            link(V.tensor_copy(slot_i[:], b["slotf"]), "slots")
            one = lambda ap: ap[0:1]

            def count_le(dst, n, limit):
                link(V.tensor_tensor(one(b["ge"])[:, 0:n * NE].rearrange("p (b e) -> p b e", b=n),
                                     one(b["iota"])[:, 0:n].rearrange("p (b o) -> p b o", o=1).to_broadcast([1, n, NE]),
                                     one(limit).rearrange("p (o e) -> p o e", o=1).to_broadcast([1, n, NE]), ALU.is_ge))
                if dst is not None:
                    link(V.tensor_reduce(dst, one(b["ge"])[:, 0:n * NE].rearrange("p (b e) -> p b e", b=n), AX_X, ALU.add))
            link(V.tensor_scalar(one(b["has"]), one(b["nb"]), 0.5, None, ALU.is_ge))
            link(V.tensor_tensor_scan(one(b["rk"]), one(b["one32"]), one(b["has"]), 0.0, ALU.mult, ALU.add))
            link(V.tensor_copy(tab[:, TAB_NR:TAB_NR + 1], one(b["rk"])[:, NE - 1:NE]))
            count_le(one(b["ebf"])[:, 0:NE], NE, b["rk"])
            link(V.tensor_scalar(tab[:, TAB_EXPERT:TAB_EXPERT + NE], one(b["ebf"])[:, 0:NE], float(NE - 1), None, ALU.min))
            link(V.tensor_scalar(one(b["rk"]), one(b["rk"]), -1.0, None, ALU.add))
            count_le(None, NE, b["rk"])
            gev = one(b["ge"])[:, 0:NE * NE].rearrange("p (b e) -> p b e", b=NE)
            link(V.tensor_tensor(gev, gev, one(b["nb"]).rearrange("p (o e) -> p o e", o=1).to_broadcast([1, NE, NE]), ALU.mult))
            link(V.tensor_reduce(one(b["rend"]), gev, AX_X, ALU.add))
            count_le(one(b["ebf"]), 64, b["rend"])
            link(V.tensor_scalar(tab[:, TAB_RANK:TAB_RANK + 64], one(b["ebf"]), float(NE - 1), None, ALU.min))
            link(V.tensor_scalar(tab[:, TAB_BUF:TAB_BUF + 64], tab[:, TAB_RANK:TAB_RANK + 64], 1, None, ALU.bitwise_and))
            nw = one(b["nw"])
            link(V.memset(nw, 1.0))
            link(V.tensor_tensor(nw[:, 1:64], one(b["ebf"])[:, 1:64], one(b["ebf"])[:, 0:63], ALU.not_equal))
            link(V.tensor_scalar(one(b["ebf"]), one(b["ebf"]), one(b["rk"])[:, NE - 1:NE], None, ALU.is_lt))
            link(V.tensor_tensor(tab[:, TAB_NEW:TAB_NEW + 64], nw, one(b["ebf"]), ALU.mult))
            for less in range(3):
                link(V.tensor_scalar(tab[:, TAB_NB + less:TAB_NB + less + 1], one(b["pend"])[:, NE - 1:NE], float(-less), None, ALU.add))
            link(V.tensor_scalar(tab[:, TAB_FREE:TAB_FREE + 1], one(b["pend"])[:, NE - 1:NE], -1.0, 64.0, ALU.mult, ALU.add))
            dve.wait_ge(act_d, START + 2)
            link(V.tensor_reduce(b["gsum"], v3("gex", T, NG), AX_X, ALU.add))
            link(V.reciprocal(b["pg"], b["gsum"]))
            link(V.tensor_scalar(b["q"], b["dif"], 1.0, None, ALU.add))
            link(V.reciprocal(b["q"], b["q"]))
            link(V.tensor_tensor(gates[:, 0:T], b["q"], b["pg"], ALU.mult))
            link(V.tensor_tensor(gates[:, T:2 * T], gates[:, 0:T], b["dif"], ALU.mult))
            dve.wait_ge(tab_ld, START + 16)
            link(V.tensor_copy(b["st_f"][0:64, :], b["st_i"][0:64, :].bitcast(I32)), "slot_tok")
            dve.wait_ge(tr, START + 1)
            link(V.tensor_copy(gidx[:, 0:64], ps[:, 2, 0:64]))

        @block.scalar
        def _(act):
            act.wait_ge(v, START + mark["exps"])
            nc.scalar.activation(b["gex"], b["gex"], ACT.Exp).then_inc(act_d, 1)
            nc.scalar.activation(b["dif"], b["dif"], ACT.Exp).then_inc(act_d, 1)

        @block.tensor
        def _(pe):
            pe.wait_ge(f_ld, START + 48)
            pe.wait_ge(v, START + mark["onehot"])
            pe.matmul(ps[:, 0, :], b["tri"], b["ohs"], start=True, stop=True).then_inc(mm, 1)
            pe.matmul(ps[:, 1, :], b["ones"], b["ohs"], start=True, stop=True).then_inc(mm, 1)
            pe.wait_ge(v, START + mark["slot_tok"])
            pe.transpose(ps[:, 2, 0:64], b["st_f"][0:64, :], idn[0:64, 0:64]).then_inc(tr, 1)

        @block.gpsimd
        def _(pool):
            pool.wait_ge(f_ld, START + 48)
            pool.wait_ge(v, START + mark["slots"])
            for k in range(2):
                for t in range(T):
                    pool.indirect_dma_start(g["slot_tok_d"], bass.IndirectOffsetOnAxis(slot_i[:, k * T + t:k * T + t + 1], 0),
                                            b["tok"][:, t:t + 1].bitcast(I32), None).then_inc(scat, 16)
            pool.wait_ge(scat, 16 * 2 * T)

        @block.sync
        def _(sp):
            sp.dma_start(b["tri"], g["tri"]).then_inc(f_ld, 16)
            sp.dma_start(b["iota"], g["iota"]).then_inc(f_ld, 16)
            sp.dma_start(b["tok"].bitcast(I32), g["tok_id"]).then_inc(f_ld, 16)
            sp.wait_ge(scat, 16 * 2 * T)
            sp.dma_start(b["st_i"][0:64, :].bitcast(I32), g["slot_tok_d"].rearrange("(a b) o -> a (b o)", a=64)).then_inc(tab_ld, 16)


def phase_experts(nc, env):
    g = env
    sem, arena, ps, ps_row, idn = g["sem"], g["arena"], g["ps"], g["ps_row"], g["idn"]
    tab, gidx = g["blk_tab"], g["gidx"]
    W13 = 2 * KD * D_EXP
    W2 = KE * D
    WSZ = W13 + W2
    PIECE = 2048
    N13, N2 = W13 // PIECE, W2 // PIECE
    b = arena_slices(arena, 0, [("whi", WSZ), ("wlo", WSZ), ("st", WSZ), ("x0", D), ("x1", D), ("xh", D // 2), ("xl", D // 2),
                                ("s", D_EXP), ("h", D_EXP), ("hh", D_EXP // 2), ("hl", D_EXP // 2), ("g2", D), ("y0", D),
                                ("zero", D)])
    whi, wlo, xh, xl, hh, hl = (b[n].bitcast(F16) for n in ("whi", "wlo", "xh", "xl", "hh", "hl"))
    ix = g["stack"].enter_context(nc.sbuf_tensor("ix", [P, 2], I32))
    st_ld = [sem("g_st_ld0"), sem("g_st_ld1"), sem("g_st_ld2"), sem("g_st_ld3"), sem("g_st_ld4"), sem("g_st_ld5")]
    hi13, lo13, hi2, lo2 = sem("g_hi13"), sem("g_lo13"), sem("g_hi2"), sem("g_lo2")
    g2_ld, x_ix, x_ld, x_tr, x_hi, x_lo = (sem("g_g2_ld"), sem("g_x_ix"), g["plain_sem"]("g_x_ld"), sem("g_x_tr"),
                                           sem("g_x_hi"), sem("g_x_lo"))
    up_mm, silu_d, h_d, h_tr, h_hi, h_lo = (sem("g_up_mm"), sem("g_silu"), sem("g_h"), sem("g_h_tr"), sem("g_h_hi"),
                                            sem("g_h_lo"))
    y_mm, y_ev, y_st = sem("g_y_mm"), sem("g_y_ev"), sem("g_y_st")
    zero_d, z_st = sem("g_zero"), sem("g_z_st")

    def blocks(eng):
        return eng.value_load(tab[0:1, TAB_NB:TAB_NB + 1], min_val=32, max_val=MAX_BLOCKS - 1)

    def rank_of(eng, n):
        return eng.value_load(tab[0:1, bass.ds(n + TAB_RANK, 1)], min_val=0, max_val=NE - 1)

    def buffer_of(eng, n):
        return eng.value_load(tab[0:1, bass.ds(n + TAB_BUF, 1)], min_val=0, max_val=1)

    def starts_rank(eng, n):
        return eng.value_load(tab[0:1, bass.ds(n + TAB_NEW, 1)], min_val=0, max_val=1)

    def part(buf, whole, at, size):
        return whole[:, bass.ds(buf * WSZ + at, size)] if not isinstance(buf, int) else \
            whole[:, buf * WSZ + at:buf * WSZ + at + size]

    with nc.Block() as block:
        @block.sync
        def _(sp):
            sp.dma_start(b["g2"], g["mod_rows"][0:1, 5 * D:6 * D].to_broadcast([P, D])).then_inc(g2_ld, 16)
            ranks = sp.value_load(tab[0:1, TAB_NR:TAB_NR + 1], min_val=2, max_val=NE)

            def pieces(r, e):
                for n in range(N13 + N2):
                    if n < N13:
                        src = g[("w1", "w3")[n // (N13 // 2)]][bass.ds(e, 1)].rearrange("e (k p) n -> p (e k) n", p=P)
                        k0, cols = n % (N13 // 2) * (PIECE // D_EXP), D_EXP
                    else:
                        src = g["w2"][bass.ds(e, 1)].rearrange("e (k p) n -> p (e k) n", p=P)
                        k0, cols = (n - N13) * (PIECE // D), D
                    if r is not None:
                        done = (lo13, N13 * (r - 1) + n + 1) if n < N13 else (lo2, N2 * (r - 1) + n - N13 + 1)
                        sp.wait_ge(done[0], START + done[1])
                        sp.sem_inc(g["alone"], 1)
                    sp.dma_start(b["st"][:, n * PIECE:(n + 1) * PIECE].rearrange("p (k n) -> p k n", n=cols),
                                 src[:, k0:k0 + PIECE // cols, :]).then_inc(st_ld[n], 16)
            pieces(None, sp.value_load(tab[0:1, TAB_EXPERT:TAB_EXPERT + 1], min_val=0, max_val=NE - 1))
            with sp.Fori(1, ranks) as r:
                pieces(r, sp.value_load(tab[0:1, bass.ds(r + TAB_EXPERT, 1)], min_val=0, max_val=NE - 1))
            used = blocks(sp)
            sp.wait_ge(zero_d, START + 1)
            with sp.Fori(used, 64) as n:
                sp.dma_start(g["y_d"][bass.ds(n * P, P), :], b["zero"]).then_inc(z_st, 16)
            sp.wait_ge(z_st, START + sp.value_load(tab[0:1, TAB_FREE:TAB_FREE + 1], min_val=1, max_val=32) * 16)
            sp.sem_inc(g["alone"], 1)

        @block.gpsimd
        def _(pool):
            nb = blocks(pool)

            def gather(i, j):
                pool.wait_ge(x_tr, START + 2 * i)
                pool.sem_inc(g["alone"], 1)
                nc.gpsimd.tensor_copy(ix[:, j:j + 1], gidx[:, bass.ds(2 * i + j, 1)]).then_inc(x_ix, 1)
                pool.wait_ge(x_ix, START + 2 * i + j + 1)
                pool.sem_inc(g["alone"], 1)
                pool.indirect_dma_start(b[f"x{j}"], None, g["h2_d"], bass.IndirectOffsetOnAxis(ix[:, j:j + 1], 0))\
                    .then_inc(x_ld, 16)
                pool.wait_ge(x_ld, 16 * (2 * i + j + 1))
                pool.sem_inc(g["alone"], 1)
            with pool.Fori(0, (nb >> 1) + 1) as i:
                gather(i, 0)
                gather(i, 1)

        @block.scalar
        def _(act):
            nb = blocks(act)

            def split13(r, buf, lo, hi):
                for n in range(lo, hi):
                    act.wait_ge(st_ld[n], START + 16 * r + 16)
                    nc.scalar.activation(part(buf, whi, n * PIECE, PIECE), b["st"][:, n * PIECE:(n + 1) * PIECE],
                                         ACT.Copy, scale=W_SCALE).then_inc(hi13, 1)

            def split2(r, buf):
                for n in range(N13, N13 + N2):
                    act.wait_ge(st_ld[n], START + 16 * r + 16)
                    nc.scalar.activation(part(buf, whi, n * PIECE, PIECE), b["st"][:, n * PIECE:(n + 1) * PIECE],
                                         ACT.Copy, scale=W_SCALE).then_inc(hi2, 1)

            def x_high(n):
                act.wait_ge(x_tr, START + n + 1)
                act.wait_ge(up_mm, START + 2 * n)
                nc.scalar.activation(xh, ps_row[:, 1024:2048], ACT.Copy, scale=X_SCALE).then_inc(x_hi, 1)

            def silu(n):
                act.wait_ge(up_mm, START + 2 * n + 1)
                act.wait_ge(h_d, START + n)
                nc.scalar.activation(b["s"], ps[:, 0, :], ACT.Silu, scale=1.0 / (W_SCALE * X_SCALE)).then_inc(silu_d, 1)

            def h_high(n):
                act.wait_ge(h_tr, START + n + 1)
                act.wait_ge(y_mm, START + n)
                nc.scalar.activation(hh, ps[:, 4, :], ACT.Copy).then_inc(h_hi, 1)

            def store_y(n):
                act.wait_ge(y_ev, START + n + 1)
                act.dma_start(g["y_d"][bass.ds(n * P, P), :], b["y0"]).then_inc(y_st, 16)

            def step(n, prev, stored):
                new = starts_rank(act, n)
                rank, buf = rank_of(act, n), buffer_of(act, n)
                with act.If(new == 1):
                    act.wait_ge(up_mm, START + 2 * n)
                    split13(rank + 1, 1 - buf, 0, N13 // 2)
                h_high(prev)
                silu(n)
                with act.If(new == 1):
                    split13(rank + 1, 1 - buf, N13 // 2, N13)
                x_high(n + 1)
                if stored:
                    store_y(n - 2)
                newp = starts_rank(act, prev)
                rankp, bufp = rank_of(act, prev), buffer_of(act, prev)
                with act.If(newp == 1):
                    act.wait_ge(y_mm, START + prev)
                    split2(rankp + 1, 1 - bufp)
            split13(0, 0, 0, N13)
            x_high(0)
            split2(0, 0)
            split13(1, 1, 0, N13 // 2)
            silu(0)
            split13(1, 1, N13 // 2, N13)
            x_high(1)
            step(1, 0, False)
            with act.Fori(2, nb) as n:
                step(n, n - 1, True)
            last = act.value_load(tab[0:1, TAB_NB1:TAB_NB1 + 1], min_val=31, max_val=MAX_BLOCKS - 2)
            store_y(act.value_load(tab[0:1, TAB_NB2:TAB_NB2 + 1], min_val=30, max_val=MAX_BLOCKS - 3))
            h_high(last)
            store_y(last)
            act.wait_ge(y_st, START + nb * 16)
            act.sem_inc(g["alone"], 1)

        @block.vector
        def _(dve):
            nb = blocks(dve)

            def low(dst, src, scale, high):
                return nc.vector.scalar_tensor_tensor(dst, src, scale, high, ALU.mult, ALU.subtract)

            def split13(r, buf, lo, hi):
                for n in range(lo, hi):
                    dve.wait_ge(hi13, START + N13 * r + n + 1)
                    dve.sem_inc(g["alone"], 1)
                    low(part(buf, wlo, n * PIECE, PIECE), b["st"][:, n * PIECE:(n + 1) * PIECE], W_SCALE,
                        part(buf, whi, n * PIECE, PIECE)).then_inc(lo13, 1)

            def split2(r, buf):
                for n in range(N13, N13 + N2):
                    dve.wait_ge(hi2, START + N2 * r + n - N13 + 1)
                    dve.sem_inc(g["alone"], 1)
                    low(part(buf, wlo, n * PIECE, PIECE), b["st"][:, n * PIECE:(n + 1) * PIECE], W_SCALE,
                        part(buf, whi, n * PIECE, PIECE)).then_inc(lo2, 1)

            def x_low(n):
                dve.wait_ge(x_hi, START + n + 1)
                low(xl, ps_row[:, 1024:2048], X_SCALE, xh).then_inc(x_lo, 1)

            def hidden(n):
                dve.wait_ge(silu_d, START + n + 1)
                dve.wait_ge(up_mm, START + 2 * n + 2)
                dve.wait_ge(h_tr, START + n)
                nc.vector.scalar_tensor_tensor(b["h"], ps[:, 1, :], 1.0 / (W_SCALE * X_SCALE), b["s"], ALU.mult, ALU.mult)\
                    .then_inc(h_d, 1)

            def h_low(n):
                dve.wait_ge(h_hi, START + n + 1)
                low(hl, ps[:, 4, :], 1.0, hh).then_inc(h_lo, 1)

            def scale_y(n):
                dve.wait_ge(y_mm, START + n + 1)
                dve.wait_ge(y_st, START + 16 * n)
                nc.vector.scalar_tensor_tensor(b["y0"], ps_row[:, 2560:3584], 1.0 / W_SCALE, b["g2"], ALU.mult, ALU.mult)\
                    .then_inc(y_ev, 1)

            def step(n, prev):
                new = starts_rank(dve, n)
                rank, buf = rank_of(dve, n), buffer_of(dve, n)
                with dve.If(new == 1):
                    split13(rank + 1, 1 - buf, 0, N13 // 2)
                h_low(prev)
                with dve.If(new == 1):
                    split13(rank + 1, 1 - buf, N13 // 2, N13)
                hidden(n)
                x_low(n + 1)
                newp = starts_rank(dve, prev)
                rankp, bufp = rank_of(dve, prev), buffer_of(dve, prev)
                with dve.If(newp == 1):
                    split2(rankp + 1, 1 - bufp)
                scale_y(prev)
            nc.vector.memset(b["zero"], 0.0).then_inc(zero_d, 1)
            dve.wait_ge(g2_ld, START + 16)
            split13(0, 0, 0, N13)
            x_low(0)
            split2(0, 0)
            split13(1, 1, 0, N13)
            hidden(0)
            x_low(1)
            step(1, 0)
            with dve.Fori(2, nb) as n:
                step(n, n - 1)
            last = dve.value_load(tab[0:1, TAB_NB1:TAB_NB1 + 1], min_val=31, max_val=MAX_BLOCKS - 2)
            h_low(last)
            scale_y(last)

        @block.tensor
        def _(pe):
            def transposes_x(j, n):
                pe.wait_ge(x_ld, 16 * n + 16)
                pe.wait_ge(x_lo, START + n)
                for k in range(KD):
                    mm = pe.transpose(ps_row[:, 1024 + k * P:1024 + (k + 1) * P], b[f"x{j}"][:, k * P:(k + 1) * P], idn[:])
                mm.then_inc(x_tr, 1)

            def product(out, high, low, buf, at, first, last):
                pe.matmul(out, high, part(buf, whi, at, 512), start=first, stop=False)
                pe.matmul(out, high, part(buf, wlo, at, 512), start=False, stop=False)
                return pe.matmul(out, low, part(buf, whi, at, 512), start=False, stop=last)

            def up(bank, off, buf):
                for k in range(KD):
                    mm = product(ps[:, bank, :], xh[:, k * P:(k + 1) * P], xl[:, k * P:(k + 1) * P], buf,
                                 off + k * D_EXP, k == 0, k == KD - 1)
                mm.then_inc(up_mm, 1)

            def down(n):
                rank, buf = rank_of(pe, n), buffer_of(pe, n)
                pe.wait_ge(h_lo, START + n + 1)
                pe.wait_ge(y_ev, START + n)
                pe.wait_ge(lo2, START + N2 * rank + N2)
                for k in range(KE):
                    for c in range(2):
                        mm = product(ps[:, 5 + c, :], hh[:, k * P:(k + 1) * P], hl[:, k * P:(k + 1) * P], buf,
                                     W13 + k * D + c * 512, k == 0, k == KE - 1)
                mm.then_inc(y_mm, 1)

            def transposes_h(n):
                pe.wait_ge(h_d, START + n + 1)
                pe.wait_ge(h_lo, START + n)
                for k in range(KE):
                    mm = pe.transpose(ps[:, 4, k * P:(k + 1) * P], b["h"][:, k * P:(k + 1) * P], idn[:])
                mm.then_inc(h_tr, 1)

            def step(n, prev, j):
                rank, buf = rank_of(pe, n), buffer_of(pe, n)
                pe.wait_ge(x_lo, START + n + 1)
                pe.wait_ge(silu_d, START + n)
                pe.wait_ge(lo13, START + N13 * rank + N13 // 2)
                up(0, 0, buf)
                if prev is not None:
                    transposes_h(prev)
                    pe.wait_ge(h_d, START + n)
                pe.wait_ge(lo13, START + N13 * rank + N13)
                up(1, KD * D_EXP, buf)
                transposes_x(1 - j, n + 1)
                if prev is not None:
                    down(prev)
            last = pe.value_load(tab[0:1, TAB_NB1:TAB_NB1 + 1], min_val=31, max_val=MAX_BLOCKS - 2)
            before = pe.value_load(tab[0:1, TAB_NB2:TAB_NB2 + 1], min_val=30, max_val=MAX_BLOCKS - 3)
            transposes_x(0, 0)
            step(0, None, 0)
            with pe.Fori(0, last >> 1) as i:
                step(2 * i + 1, 2 * i, 1)
                step(2 * i + 2, 2 * i + 1, 0)
            with pe.If((last & 1) == 1):
                step(last, before, 1)
            transposes_h(last)
            down(last)


def phase_combine(nc, env):
    g = env
    sem, plain_sem, arena = g["sem"], g["plain_sem"], g["arena"]
    slot_i, gates = g["slot_i"], g["gates"]
    b = arena_slices(arena, 0, [("l2g", D), ("l2b", D), ("mh", 1), ("st", 12), ("mv", 2), ("ve", 1), ("rs", 1)]
                     + [(f"{n}{j}", D) for n in ("ya", "yb", "x1", "xa", "o") for j in range(2)])
    ix = g["stack"].enter_context(nc.sbuf_tensor("ixc", [P, 4], I32))
    ld, ix_d, v, pw, a_x, mh_d = sem("h_ld"), sem("h_ix"), sem("h_v"), sem("h_pw"), sem("h_a_x"), sem("h_mh")
    y_ld = [plain_sem("h_y_ld0"), plain_sem("h_y_ld1")]
    x_ld, o_st = [sem("h_x_ld0"), sem("h_x_ld1")], [sem("h_o_st0"), sem("h_o_st1")]
    NV = 8
    LAST = T_LAT // 2 - 1
    with nc.Block() as block:
        @block.sync
        def _(sp):
            for n, name in enumerate(("l2g", "l2b")):
                sp.dma_start(b[name], g["ln2"][n:n + 1, :].to_broadcast([P, D])).then_inc(ld, 16)
            for j in range(2):
                sp.dma_start(b[f"x1{j}"], g["x1_d"][j * P:(j + 1) * P, :]).then_inc(x_ld[j], 16)
            with sp.Fori(0, LAST) as i:
                for j in range(2):
                    sp.wait_ge(a_x, START + 2 * i + j + 1)
                    sp.sem_inc(g["alone"], 1)
                    sp.dma_start(b[f"x1{j}"], g["x1_d"][bass.ds((2 * i + j + 2) * P, P), :]).then_inc(x_ld[j], 16)

        @block.gpsimd
        def _(pool):
            nc.gpsimd.memset(b["mh"], -0.5).then_inc(mh_d, 1)

            def fetch(i, j):
                for k in range(2):
                    nc.gpsimd.tensor_copy(ix[:, 2 * j + k:2 * j + k + 1], slot_i[:, bass.ds(k * T_LAT + 2 * i + j, 1)]).then_inc(ix_d, 1)
                pool.wait_ge(ix_d, START + 4 * i + 2 * j + 2)
                pool.sem_inc(g["alone"], 1)
                for k in range(2):
                    pool.indirect_dma_start(b[f"{('ya', 'yb')[k]}{j}"], None, g["y_d"],
                                            bass.IndirectOffsetOnAxis(ix[:, 2 * j + k:2 * j + k + 1], 0)).then_inc(y_ld[j], 16)

            def rstd(i, j):
                pool.wait_ge(v, START + NV * (2 * i + j) + 6)
                pool.sem_inc(g["alone"], 1)
                nc.gpsimd.tensor_tensor(b["rs"], b["ve"], b["mh"], ALU.pow).then_inc(pw, 1)
            for j in range(2):
                fetch(0, j)
            pool.wait_ge(mh_d, START + 1)
            with pool.Fori(0, LAST) as i:
                for j in range(2):
                    rstd(i, j)
                    fetch(i + 1, j)
            for j in range(2):
                rstd(LAST, j)

        @block.scalar
        def _(act):
            def store(i, j):
                act.wait_ge(v, START + NV * (2 * i + j + 1))
                act.dma_start(g["out"][bass.ds((2 * i + j) * P, P), :], b[f"o{j}"]).then_inc(o_st[j], 16)
            for j in range(2):
                act.wait_ge(x_ld[j], START + 16)
                nc.scalar.activation(b[f"xa{j}"], b[f"x1{j}"], ACT.Copy, scale=ALPHA).then_inc(a_x, 1)
            with act.Fori(0, LAST) as i:
                for j in range(2):
                    store(i, j)
                    act.wait_ge(x_ld[j], START + 16 * i + 32)
                    nc.scalar.activation(b[f"xa{j}"], b[f"x1{j}"], ACT.Copy, scale=ALPHA).then_inc(a_x, 1)
            for j in range(2):
                store(LAST, j)
            for j in range(2):
                act.wait_ge(o_st[j], START + 16 * (T_LAT // 2))

        @block.vector
        def _(dve):
            dve.wait_ge(ld, START + 32)
            with dve.Fori(0, T_LAT // 2) as i:
                for j in range(2):
                    t = 2 * i + j
                    n = [0]

                    def link(ins):
                        n[0] += 1
                        ins.then_inc(v, 1)
                        dve.wait_ge(v, START + NV * t + n[0])
                    y0, y1, xa, o = b[f"ya{j}"], b[f"yb{j}"], b[f"xa{j}"], b[f"o{j}"]
                    dve.wait_ge(a_x, START + t + 1)
                    dve.wait_ge(y_ld[j], 32 * i + 32)
                    link(nc.vector.scalar_tensor_tensor(xa, y0, gates[:, bass.ds(t, 1)], xa, ALU.mult, ALU.add))
                    link(nc.vector.scalar_tensor_tensor(xa, y1, gates[:, bass.ds(T_LAT + t, 1)], xa, ALU.mult, ALU.add))
                    nc.vector.bn_stats(b["st"][:, 0:6], xa[:, 0:512]).then_inc(v, 1)
                    n[0] += 1
                    link(nc.vector.bn_stats(b["st"][:, 6:12], xa[:, 512:1024]))
                    dve.sem_inc(g["alone"], 1)
                    link(nc.vector.bn_aggr(b["mv"], b["st"].rearrange("p (a s) -> p a s", a=2)))
                    link(nc.vector.tensor_scalar(b["ve"], b["mv"][:, 1:2], EPS, None, ALU.add))
                    link(nc.vector.scalar_tensor_tensor(xa, xa, b["mv"][:, 0:1], b["l2g"], ALU.subtract, ALU.mult))
                    dve.wait_ge(pw, START + t + 1)
                    dve.wait_ge(o_st[j], START + 16 * i)
                    link(nc.vector.scalar_tensor_tensor(o, xa, b["rs"], b["l2b"], ALU.mult, ALU.add))


def _constants():
    grid_w, axis = 64, HD // 2
    inv = (10000.0 ** (-np.arange(0, axis, 2, dtype=np.float32) / np.float32(axis))).astype(np.float32)
    pos = np.arange(SEQ)
    ang = np.stack([(pos // grid_w).astype(np.float32)[:, None] * inv, (pos % grid_w).astype(np.float32)[:, None] * inv], 1)
    cos_t = np.cos(ang).astype(np.float32).reshape(T_LAT, P, 2 * inv.size)
    sin_t = np.sin(ang).astype(np.float32).reshape(T_LAT, P, 2 * inv.size)
    q, k = np.arange(P)[:, None], np.arange(WIN)[None, :] - P
    masks = np.zeros((4, P, KEYS), np.float32)
    for m in range(3):
        ok = np.abs(k - q) <= P
        if m == 0:
            ok = ok & (k >= 0)
        if m == 2:
            ok = ok & (k < P)
        masks[m, :, CTX:] = np.where(ok, 0.0, NEG)
    tri = np.triu(np.ones((P, P), np.float32), 1)
    iota = np.tile(np.arange(64, dtype=np.float32), (P, 1))
    tok = (np.arange(T_LAT)[None, :] * P + np.arange(P)[:, None]).astype(np.int32)
    return {"cos_t": cos_t, "sin_t": sin_t, "ident": np.eye(P, dtype=np.float32), "masks": masks, "tri": tri,
            "iota": iota, "tok_id": tok}


def _layout(i):
    c = np.ascontiguousarray
    cs = np.stack([np.asarray(i["c"])[0], np.asarray(i["c_ctx"])], 1)
    a = {k: np.asarray(i[k]) for k in i}
    order = np.arange(NH).reshape(NKV, PAIRS).T.reshape(-1)
    cols = (2 * D_RNN + order[:, None] * HD + np.arange(HD)).reshape(-1)
    w_in = np.concatenate([a["w_in"][0][:, :2 * D_RNN], a["w_in"][0][:, cols], a["w_in"][0][:, 2 * D_RNN + D_ATTN:]], 1)
    return {
        "x": c(a["x"][0]), "c2": c(cs.reshape(KD, P, 2).transpose(1, 0, 2).reshape(P, 2 * KD)), "w_mod": c(a["w_mod"][0]),
        "b_mod": c(np.stack([a["b_mod"][0]] * 2)), "w_in": c(w_in),
        "rg_par": c(np.concatenate([a["conv_w"][0].T, a["conv_b"][0][:, None], a["rg_ba"][0].T, a["rg_bx"][0].T],
                                   1)),
        "lam": c(a["rg_lam"][0].reshape(2, C_RNN, P).transpose(2, 0, 1).reshape(P, 2 * C_RNN)),
        "rg_wa": c(a["rg_wa"][0]), "rg_wx": c(a["rg_wx"][0]), "ctx_x": c(a["ctx"][0]),
        "sink": c(np.stack([a["attn_sink"][0]] * P)), "w_out": c(a["w_out"][0]),
        "gn": c(np.concatenate([a["gn_rnn"][0], a["gn_attn"][0]]).reshape(KD, P).T),
        "ln1": c(np.stack([a["ln1_g"][0], a["ln1_b"][0]])),
        "router": c(np.concatenate([a["router_g"][0], a["router_e"][0]], 1)),
        "router_b": c(np.concatenate([a["router_gb"][0], a["router_eb"][0]])[None, :]),
        "w1": c(a["w1"][0]), "w3": c(a["w3"][0]), "w2": c(a["w2"][0]), "ln2": c(np.stack([a["ln2_g"][0], a["ln2_b"][0]])),
        **_constants(),
    }


_ARGS = ["x", "c2", "w_mod", "b_mod", "w_in", "rg_par", "lam", "rg_wa", "rg_wx", "ctx_x", "sink", "w_out", "gn", "ln1", "router",
         "router_b", "w1", "w3", "w2", "ln2", "cos_t", "sin_t", "ident", "masks", "tri", "iota", "tok_id"]


def kernel(**inputs):
    import concourse.bacc as bacc
    from concourse.bass_utils import run_bass_kernel_spmd

    arrays = _layout(inputs)
    nc = bacc.Bacc("TRN2", target_bir_lowering=False, num_devices=1)
    aps = {n: nc.dram_tensor(n, arrays[n].shape, mybir.dt.from_np(arrays[n].dtype), kind="ExternalInput").ap() for n in _ARGS}
    aps["out"] = nc.dram_tensor("out", (SEQ, D), F32, kind="ExternalOutput").ap()
    hybrid_layer(nc, **aps)
    r = run_bass_kernel_spmd(nc, [{n: arrays[n] for n in _ARGS}], core_ids=[0])
    return np.asarray(r.results[0]["out"]).reshape(1, SEQ, D)
```

```python
from contextlib import ExitStack

import numpy as np

import concourse.bass as bass
from concourse import mybir

F32 = mybir.dt.float32
F16 = mybir.dt.float16
I32 = mybir.dt.int32
U32 = mybir.dt.uint32
ALU = mybir.AluOpType
ACT = mybir.ActivationFunctionType
AX_X = mybir.AxisListType.X

P = 128
D = 1024
KD = D // P
SEQ = 2048
CTX = 256
T_LAT = SEQ // P
D_RNN = 512
C_RNN = D_RNN // P
D_ATTN = 512
HD = 64
NH = D_ATTN // HD
NKV = 2
GROUP = NH // NKV
QKV = D_ATTN + 2 * NKV * HD
D_IN = 2 * D_RNN + QKV
TIME = CTX + SEQ
U_CTX = 2
U_LAT = U_CTX + CTX + 2
U_ROW = U_LAT + SEQ + 4
WIN = 3 * P
KEYS = CTX + WIN
K_LAT = CTX + P
K_ROW = K_LAT + SEQ + P
CONV_W = 4
NE = 32
NG = 4
EPG = NE // NG
D_EXP = 512
KE = D_EXP // P
MAX_BLOCKS = (2 * SEQ + NE * (P - 1)) // P + 1
NPAR = 9
ALPHA = 2 ** 0.25
START = 1
W_SCALE, X_SCALE, P_SCALE = 64.0, 16.0, 1024.0
TAB_RANK, TAB_BUF, TAB_NEW, TAB_EXPERT = 0, 64, 128, 192
TAB_NB, TAB_NB1, TAB_NB2, TAB_NR, TAB_FREE, TAB_NR1 = 224, 225, 226, 227, 228, 229
TAB_SIZE = 264
EPS = 1e-6
NEG = -1e30
CHUNK = 256
TPC = CHUNK // P

SEMAPHORES = """
b_tab_ld b_mcol_tr b_x_ld0 b_x_ld1 b_g_st0 b_g_st1 b_q_st0 b_q_st1 b_pads b_sc b_stats b_var b_rstd b_normed
b_tr_x b_x_hi b_x_tmp b_x_lo b_u_mm b_g_mm b_u_ev b_g_ev b_qkv_mm b_rope_a b_rope_o b_q_hi b_k_hi b_v_hi
b_q_lo b_k_lo b_v_lo b_q_tr b_k_tr b_q_ev b_k_ev b_idh c_lam_ld c_gate_ld c_zero c_par_ld0 c_par_ld1 c_sp_v
c_sp_a c_cur c_conv c_g_mm c_g_ev c_func c_frac c_drive c_scan c_y c_y_st d_mask_ld d_s_mm d_s_max d_nm d_p
d_q_ld0 d_q_ld1 d_o_st0 d_o_st1 d_p_tr d_p_hi d_p_lo d_pv d_es d_es_e d_den d_o d_w_ld d_w_gate e_w_ok e_w_hi
e_w_lo e_p_ok e_in_ld0 e_in_ld1 e_xt_ld0 e_xt_ld1 e_x_st0 e_x_st1 e_h_st0 e_h_st1 e_sq e_hi e_lo e_ssm e_ss
e_ssv e_pw_s e_a_tr e_o_mm e_o_act e_v e_pw e_h_tr e_h_ev e_r_mm e_lg f_ld f_v f_act f_mm f_tr g_st_ld0
g_st_ld1 g_st_ld2 g_st_ld3 g_st_ld4 g_st_ld5 g_hi13 g_lo13 g_hi2 g_lo2 g_g2_ld g_x_ix g_x_tr g_x_hi g_x_lo
g_up_mm g_silu g_h g_h_tr g_h_hi g_h_lo g_y_mm g_y_ev g_y_st g_zero g_z_st h_ld h_ix h_v h_pw h_a_x h_mh
h_x_ld0 h_x_ld1 h_o_st0 h_o_st1
""".split()


def arena_slices(arena, start, sizes):
    out = {}
    for name, size in sizes:
        out[name] = arena[:, start:start + size]
        start += size
    assert start <= arena.shape[1], start
    return out


def hybrid_layer(nc, x, c2, w_mod, b_mod, w_in, rg_par, lam, rg_wa, rg_wx, ctx_x, sink, w_out, gn, ln1, router, router_b,
                 w1, w3, w2, ln2, cos_t, sin_t, ident, masks, tri, iota, tok_id, out):
    with ExitStack() as stack:
        def plain_sem(name):
            return stack.enter_context(nc.semaphore(name))

        from_one = {name: plain_sem(name) for name in SEMAPHORES}

        def sem(name):
            return from_one[name]

        def sb(name, shape, dt=F32):
            return stack.enter_context(nc.sbuf_tensor(name, shape, dt))

        def dram(name, shape, dt=F32):
            return nc.dram_tensor(name, shape, dt, kind="Internal").ap()

        mod_rows = dram("mod_rows", [2, 6 * D])
        gate_d = dram("gate_d", [C_RNN, P, SEQ])
        qT_d = dram("qT_d", [T_LAT, P, NH * P // 2])
        yT_d = dram("yT_d", [C_RNN, P, SEQ])
        attn_d = dram("attn_d", [T_LAT, P, D_ATTN])
        x1_d = dram("x1_d", [SEQ, D])
        h2_d = dram("h2_d", [SEQ, D])
        slot_tok_d = dram("slot_tok_d", [64 * P, 1], I32)
        y_d = dram("y_d", [64 * P, D])

        idn = sb("idn", [P, P])
        small = sb("small", [P, 640])
        arena = sb("arena", [P, 50500])
        slot_i = sb("slot_i", [P, 2 * T_LAT], I32)
        gates = sb("gates", [P, 2 * T_LAT])
        blk_tab = sb("blk_tab", [1, TAB_SIZE], I32)
        gidx = sb("gidx", [P, 66], I32)
        ps = stack.enter_context(nc.psum_tensor("ps", [P, 8, 512], F32))
        ps_row = ps[:, :, :].rearrange("p b n -> p (b n)")

        const_ld = plain_sem("const_ld")
        alone = plain_sem("alone")
        env = dict(locals())
        phase_modulation(nc, env)
        phase_project(nc, env)
        phase_recurrence(nc, env)
        phase_attention(nc, env)
        phase_output(nc, env)
        phase_route(nc, env)
        phase_experts(nc, env)
        phase_combine(nc, env)


X0 = 0
UT0 = X0 + U_ROW
KT0 = UT0 + C_RNN * U_ROW
V0 = KT0 + 2 * K_ROW
V_SLOTS = 2 + 1 + T_LAT + 1
B0 = V0 + V_SLOTS * P
WIN0 = 50500 - KD * D_IN
RAW0 = WIN0 - KD * D_IN


def split_w_in(arena):
    parts = arena[:, WIN0:].bitcast(F16).rearrange("p (s k n) -> p s k n", s=2, k=KD)
    return parts[:, 0], parts[:, 1]


def split_v(arena):
    flat = arena[:, V0:B0].bitcast(F16)
    return flat[:, 0:V_SLOTS * P], flat[:, V_SLOTS * P:]


OUT_W0 = 27000


def output_weights(arena):
    return arena_slices(arena, OUT_W0, [("wo", KD * D), ("g1", D), ("gnc", KD), ("sc2", D), ("sh2", D), ("l1g", D), ("l1b", D),
                                        ("wr", KD * 36), ("br", 36), ("whi", KD * D // 2), ("wlo", KD * D // 2)])


def phase_modulation(nc, env):
    g = env
    sem, arena, ps, small = g["plain_sem"], g["arena"], g["ps"], g["small"]
    c_ld, silu_done = sem("a_c_ld"), sem("a_silu_done")
    wmod_ld = [sem(f"a_wmod_ld{j}") for j in range(3)]
    mod_mm, rows_done, rows_st = sem("a_mod_mm"), sem("a_rows_done"), sem("a_rows_st")
    a = arena_slices(arena, 0, [("w0", KD * 512), ("w1", KD * 512), ("w2", KD * 512), ("rows", 6 * D)])
    ring = [a[f"w{j}"].rearrange("p (k n) -> p k n", k=KD) for j in range(3)]
    c2s = small[:, 0:2 * KD]
    c2a = small[:, 2 * KD:4 * KD]
    zi = small[0:64, 128:256].bitcast(I32)
    wmod_v = g["w_mod"].rearrange("(k p) n -> p k n", p=P)
    raw = arena[:, RAW0:WIN0].rearrange("p (k n) -> p k n", k=KD)
    whi = split_w_in(arena)[0]
    flat = arena[:, WIN0:].bitcast(F16)
    win_ld, win_hi = sem("a_win_ld"), sem("a_win_hi")
    with nc.Block() as block:
        @block.sync
        def _(sp):
            sp.dma_start(c2s, g["c2"]).then_inc(c_ld, 16)
            sp.dma_start(a["rows"][0:2, :], g["b_mod"]).then_inc(c_ld, 16)
            sp.dma_start(g["idn"][:], g["ident"]).then_inc(g["const_ld"], 16)
            for j in range(3):
                sp.dma_start(ring[j], wmod_v[:, :, j * 512:(j + 1) * 512]).then_inc(wmod_ld[j], 16)
            sp.dma_start(raw, g["w_in"].rearrange("(k p) n -> p k n", p=P)).then_inc(win_ld, 16)
            with sp.Fori(0, 3) as i:
                for j in range(3):
                    sp.wait_ge(mod_mm, i * 3 + j + 1)
                    sp.dma_start(ring[j], wmod_v[:, :, bass.ds(i * 1536 + (j + 3) * 512, 512)]).then_inc(wmod_ld[j], 16)
            sp.wait_ge(rows_done, 1)
            sp.dma_start(g["slot_tok_d"].rearrange("(a b) o -> a (b o)", a=64), zi).then_inc(rows_st, 16)
            sp.wait_ge(rows_done, 13)
            sp.dma_start(g["mod_rows"], a["rows"][0:2, :]).then_inc(rows_st, 16)
            sp.wait_ge(rows_st, 32)
            sp.wait_ge(c_ld, 32)
            sp.wait_ge(g["const_ld"], 16)

        @block.gpsimd
        def _(pool):
            for s in g["from_one"].values():
                pool.sem_inc(s, START)

        @block.scalar
        def _(act):
            act.wait_ge(c_ld, 32)
            nc.scalar.activation(c2a, c2s, ACT.Silu).then_inc(silu_done, 1)
            act.wait_ge(win_ld, 16)
            for k in range(KD):
                nc.scalar.activation(whi[:, k, :], raw[:, k, :], ACT.Copy, scale=W_SCALE).then_inc(win_hi, 1)

        @block.tensor
        def _(pe):
            pe.wait_ge(silu_done, 1)
            with pe.Fori(0, 4) as i:
                for j in range(3):
                    pe.wait_ge(wmod_ld[j], i * 16 + 16)
                    pe.wait_ge(rows_done, i * 3 + 1)
                    for k in range(KD):
                        mm = pe.matmul(ps[0:2, j, :], c2a[:, 2 * k:2 * k + 2], ring[j][:, k, :],
                                       start=(k == 0), stop=(k == KD - 1))
                    mm.then_inc(mod_mm, 1)

        @block.vector
        def _(dve):
            nc.vector.memset(zi, 0).then_inc(rows_done, 1)
            dve.wait_ge(c_ld, 32)
            with dve.Fori(0, 4) as i:
                for j in range(3):
                    row = a["rows"][0:2, bass.ds(i * 1536 + j * 512, 512)]
                    dve.wait_ge(mod_mm, i * 3 + j + 1)
                    nc.vector.tensor_tensor(row, ps[0:2, j, :], row, ALU.add).then_inc(rows_done, 1)
                for n in range(2):
                    k = 2 * i + n
                    dve.wait_ge(win_hi, k + 1)
                    dve.sem_inc(g["alone"], 1)
                    high, low = (flat[:, bass.ds(k * D_IN + s * KD * D_IN, D_IN)] for s in range(2))
                    nc.vector.scalar_tensor_tensor(low, arena[:, bass.ds(RAW0 + k * D_IN, D_IN)], W_SCALE, high,
                                                   ALU.mult, ALU.subtract)


def phase_project(nc, env):
    g = env
    sem, arena, ps, ps_row, small, idn = g["sem"], g["arena"], g["ps"], g["ps_row"], g["small"], g["idn"]
    uT = arena[:, UT0:KT0].rearrange("p (c t) -> p c t", c=C_RNN)
    kT = arena[:, KT0:V0].bitcast(F16).rearrange("p (z t) -> p z t", z=2 * NKV)
    vhi, vlo = split_v(arena)
    HT = KD * CHUNK // 2
    assert CTX == CHUNK
    b = arena_slices(arena, B0, [(f"x{j}", TPC * D) for j in range(2)] + [(f"h{n}{j}", HT) for n in ("hi", "lo") for j in range(2)]
                     + [("tmp", 2 * CHUNK), ("g0", C_RNN * CHUNK), ("g1", C_RNN * CHUNK), ("cos", T_LAT * 32), ("sin", T_LAT * 32),
                        ("qr0", 640), ("qr1", 640), ("ta", 320), ("tb", 320), ("qs0", 512), ("qs1", 512), ("ks0", 256), ("ks1", 256),
                        ("qTs0", 512), ("qTs1", 512)])
    COS0 = B0 + 2 * TPC * D + 4 * HT + 2 * CHUNK + 2 * C_RNN * CHUNK
    SIN0 = COS0 + T_LAT * 32
    assert SIN0 + T_LAT * 32 + 2 * 640 + 2 * 320 + 2 * 768 + 2 * 512 <= WIN0
    whi, wlo = split_w_in(arena)
    x = [b[f"x{j}"].rearrange("p (t d) -> p t d", t=TPC) for j in range(2)]
    hi, lo = ([b[f"h{n}{j}"].bitcast(F16).rearrange("p (k n) -> p k n", k=KD) for j in range(2)] for n in ("hi", "lo"))
    gout = [b[f"g{j}"].rearrange("p (c n) -> p c n", c=C_RNN) for j in range(2)]
    tmp = b["tmp"].rearrange("p (a n) -> p a n", a=2)
    mcol = small[:, 0:32].rearrange("p (s n) -> p s n", s=2)
    st = small[:, 32:32 + 12 * TPC].rearrange("p (t a s) -> p t a s", t=TPC, a=2)
    mv = small[:, 80:80 + 2 * TPC].rearrange("p (t s) -> p t s", t=TPC)
    ve = small[:, 96:96 + TPC]
    rs = small[:, 100:100 + TPC]
    mh = small[:, 104:104 + TPC]

    tab_ld, mcol_tr = sem("b_tab_ld"), sem("b_mcol_tr")
    mrow = small[0:4 * KD, 256:256 + P]
    mcol_ps = ps[:, 2, 0:4 * KD].rearrange("p (s n) -> p s n", s=2)
    x_ld, g_st, q_st = [sem("b_x_ld0"), sem("b_x_ld1")], [sem("b_g_st0"), sem("b_g_st1")], [sem("b_q_st0"), sem("b_q_st1")]
    pads, sc_ok, stats, var_e, rstd = sem("b_pads"), sem("b_sc"), sem("b_stats"), sem("b_var"), sem("b_rstd")
    normed, tr_x, x_hi, x_tmp, x_lo = sem("b_normed"), sem("b_tr_x"), sem("b_x_hi"), sem("b_x_tmp"), sem("b_x_lo")
    u_mm, g_mm, u_ev, g_ev = sem("b_u_mm"), sem("b_g_mm"), sem("b_u_ev"), sem("b_g_ev")
    qkv_mm, rope_a, rope_o = sem("b_qkv_mm"), sem("b_rope_a"), sem("b_rope_o")
    q_hi, k_hi, v_hi, q_lo, k_lo, v_lo = sem("b_q_hi"), sem("b_k_hi"), sem("b_v_hi"), sem("b_q_lo"), sem("b_k_lo"), sem("b_v_lo")
    q_tr, k_tr, q_ev, k_ev, idh_ok = sem("b_q_tr"), sem("b_k_tr"), sem("b_q_ev"), sem("b_k_ev"), sem("b_idh")
    idh = g["stack"].enter_context(nc.sbuf_tensor("idh", [P, P], F16))
    qs = [b[f"qs{t}"].bitcast(F16).rearrange("p (h part d) -> p h part d", h=NH, part=2) for t in range(TPC)]
    ks = [b[f"ks{t}"].bitcast(F16).rearrange("p (z part r d) -> p z part r d", z=NKV, part=2, r=2) for t in range(TPC)]
    HEAD_SCALE = X_SCALE / (W_SCALE * X_SCALE)

    LAST = SEQ // CHUNK
    undo = 1.0 / (W_SCALE * X_SCALE)
    x_lat = g["x"].rearrange("(n t p) d -> n p t d", p=P, t=TPC)
    x_ctx = g["ctx_x"].rearrange("(t p) d -> p t d", p=P)

    def known(s, low):
        return not isinstance(s, int) or s >= low

    def twice(qr, z):
        return qr[:, 512 + z * HD:512 + (z + 1) * HD].rearrange("p (r d) -> p r d", r=1).to_broadcast([P, 2, HD])

    def half(s):
        return s // 2 if isinstance(s, int) else s >> 1

    def steps(eng, body):
        body(0, 0)
        with eng.Fori(0, LAST // 2 - 1) as i:
            body(2 * i + 1, 1)
            body(2 * i + 2, 0)
        body(LAST - 1, 1)
        body(LAST, 0)

    with nc.Block() as block:
        @block.sync
        def _(sp):
            sp.dma_start(x[0], x_ctx).then_inc(x_ld[0], 16)
            sp.dma_start(x[1], x_lat[0]).then_inc(x_ld[1], 16)
            for m in range(2):
                sp.dma_start(mrow[2 * KD * m:2 * KD * (m + 1), :],
                             g["mod_rows"][m:m + 1, 0:2 * D].rearrange("o (r p) -> (o r) p", p=P)).then_inc(tab_ld, 16)
            sp.dma_start(b["cos"].rearrange("p (n d) -> p n d", d=32), g["cos_t"].rearrange("n p d -> p n d")).then_inc(tab_ld, 16)
            sp.dma_start(b["sin"].rearrange("p (n d) -> p n d", d=32), g["sin_t"].rearrange("n p d -> p n d")).then_inc(tab_ld, 16)

            def body(s, j):
                if not (isinstance(s, int) and s >= LAST - 1):
                    sp.wait_ge(tr_x, START + KD * s + KD)
                    sp.sem_inc(g["alone"], 1)
                    sp.dma_start(x[j], x_lat[bass.ds(s + 1, 1)].rearrange("n p t d -> (n p) t d")).then_inc(x_ld[j], 16)
                if not known(s, 1):
                    return
                for t in range(TPC):
                    n = (s - 1) * TPC + t
                    sp.wait_ge(q_ev, START + n + 1)
                    sp.sem_inc(g["alone"], 1)
                    sp.dma_start(g["qT_d"][bass.ds(n, 1)].rearrange("n p d -> (n p) d"), b[f"qTs{t}"]).then_inc(q_st[t], 16)
                sp.wait_ge(g_ev, START + C_RNN * s)
                sp.sem_inc(g["alone"], 1)
                sp.dma_start(g["gate_d"][:, :, bass.ds((s - 1) * CHUNK, CHUNK)].rearrange("c p t -> p c t"), gout[j])\
                    .then_inc(g_st[j], 16)
            steps(sp, body)
            for j in range(2):
                sp.wait_ge(q_st[j], START + 16 * LAST)
                sp.wait_ge(g_st[j], START + 16 * (LAST // 2))

        @block.scalar
        def _(act):
            def high(s, j, k):
                m = 0 if known(s, 1) else 1
                act.wait_ge(tr_x, START + KD * s + k + 1)
                nc.scalar.activation(hi[j][:, k, :], ps[:, k % 2, 0:CHUNK], ACT.Identity, bias=mcol[:, m, k:k + 1],
                                     scale=mcol[:, m, KD + k:KD + k + 1]).then_inc(x_hi, 1)

            def high_qk(s, t):
                act.wait_ge(rope_o, START + (t + 1 if not known(s, 1) else TPC + 2 * ((s - 1) * TPC + t) + 2))
                qr = b[f"qr{t}"]
                if known(s, 1):
                    nc.scalar.activation(qs[t][:, :, 0, :], qr[:, 0:512].rearrange("p (h d) -> p h d", h=NH), ACT.Copy,
                                         scale=HEAD_SCALE).then_inc(q_hi, 1)
                for z in range(NKV):
                    nc.scalar.activation(ks[t][:, z, 0], twice(qr, z), ACT.Copy, scale=HEAD_SCALE).then_inc(k_hi, 1)

            def high_v(s, t):
                at = t * P if not known(s, 1) else bass.ds((3 + t - TPC) * P + s * (TPC * P), P)
                dst = vhi[:, at:at + P] if not known(s, 1) else vhi[:, at]
                nc.scalar.activation(dst, ps[:, 5 + 2 * t, P:2 * P], ACT.Copy, scale=HEAD_SCALE).then_inc(v_hi, 1)

            def keep_qk(s, t):
                bank = 4 + 2 * t
                if known(s, 1):
                    n = (s - 1) * TPC + t
                    act.wait_ge(q_tr, START + n + 1)
                    act.wait_ge(q_st[t], START + (s - 1) * 16)
                    nc.scalar.activation(b[f"qTs{t}"].bitcast(F16), ps[:, bank, :].bitcast(F16), ACT.Copy).then_inc(q_ev, 1)
                act.wait_ge(k_tr, START + TPC * s + t + 1)
                dst = kT[:, :, t * P:(t + 1) * P] if not known(s, 1) else kT[:, :, bass.ds(K_LAT + t * P - CHUNK + s * CHUNK, P)]
                nc.scalar.activation(dst, ps[:, bank + 1, 256:512].bitcast(F16).rearrange("p (z n) -> p z n", z=2 * NKV),
                                     ACT.Copy).then_inc(k_ev, 1)

            def body(s, j):
                high_qk(s, 0)
                high_v(s, 0)
                high_qk(s, 1)
                high_v(s, 1)
                for c in range(C_RNN):
                    if known(s, 1):
                        act.wait_ge(g_mm, START + C_RNN * (s - 1) + c + 1)
                        if c == 0:
                            act.wait_ge(g_st[j], START + 16 * half(s - 1))
                        nc.scalar.activation(gout[j][:, c, :], ps[:, 3, 0:CHUNK], ACT.Gelu_apprx_tanh, scale=undo).then_inc(g_ev, 1)
                    if not (isinstance(s, int) and s == LAST):
                        high(s + 1, 1 - j, 2 * c)
                        high(s + 1, 1 - j, 2 * c + 1)
                    if c < TPC:
                        keep_qk(s, c)
            act.wait_ge(g["const_ld"], 16)
            nc.scalar.activation(idh[:], idn[:], ACT.Copy).then_inc(idh_ok, 1)
            act.wait_ge(pads, START + 8)
            act.wait_ge(sc_ok, START + 2)
            for k in range(KD):
                high(0, 0, k)
            steps(act, body)

        @block.gpsimd
        def _(pool):
            nc.gpsimd.memset(mh, -0.5).then_inc(pads, 1)
            k_words = arena[:, KT0:V0].rearrange("p (z t) -> p z t", z=2 * NKV)
            v_words = arena[:, V0:B0].rearrange("p (part t) -> p part t", part=2)
            for words, at in ((k_words, CTX // 2), (k_words, (K_ROW - P) // 2), (v_words, P), (v_words, (V_SLOTS - 1) * P // 2)):
                nc.gpsimd.memset(words[:, :, at:at + P // 2], 0.0).then_inc(pads, 1)
            for at, end in ((0, U_CTX), (U_CTX + CTX, U_LAT), (U_LAT + SEQ, U_ROW)):
                nc.gpsimd.memset(uT[:, :, at:end], 0.0).then_inc(pads, 1)
            pool.wait_ge(pads, START + 8)
            with pool.Fori(0, LAST + 1) as s:
                pool.wait_ge(var_e, START + s + 1)
                pool.sem_inc(g["alone"], 1)
                nc.gpsimd.tensor_tensor(rs, ve, mh, ALU.pow).then_inc(rstd, 1)

        @block.vector
        def _(dve):
            def norm(s, j):
                dve.wait_ge(x_ld[j], START + 16 * half(s) + 16)
                for t in range(TPC):
                    for a in range(2):
                        nc.vector.bn_stats(st[:, t, a, :], x[j][:, t, a * 512:(a + 1) * 512]).then_inc(stats, 1)
                dve.wait_ge(stats, START + 3 * TPC * s + 2 * TPC)
                dve.sem_inc(g["alone"], 1)
                for t in range(TPC):
                    nc.vector.bn_aggr(mv[:, t, :], st[:, t, :, :]).then_inc(stats, 1)
                dve.wait_ge(stats, START + 3 * TPC * s + 3 * TPC)
                nc.vector.tensor_scalar(ve, mv[:, :, 1], EPS, None, ALU.add).then_inc(var_e, 1)
                dve.wait_ge(rstd, START + s + 1)
                for t in range(TPC):
                    nc.vector.tensor_scalar(x[j][:, t, :], x[j][:, t, :], mv[:, t, 0:1], rs[:, t:t + 1],
                                            ALU.subtract, ALU.mult).then_inc(normed, 1)

            def low(s, j, k):
                m = 0 if known(s, 1) else 1
                dve.wait_ge(x_hi, START + KD * s + k + 1)
                nc.vector.tensor_scalar(tmp[:, k % 2, :], ps[:, k % 2, 0:CHUNK], mcol[:, m, KD + k:KD + k + 1],
                                        mcol[:, m, k:k + 1], ALU.mult, ALU.add).then_inc(x_tmp, 1)
                dve.wait_ge(x_tmp, START + KD * s + k + 1)
                nc.vector.tensor_tensor(lo[j][:, k, :], tmp[:, k % 2, :], hi[j][:, k, :], ALU.subtract).then_inc(x_lo, 1)

            def rope(s, t):
                bank = 4 + 2 * t
                dve.wait_ge(qkv_mm, START + TPC * s + t + 1)
                qr = b[f"qr{t}"]
                if not known(s, 1):
                    nc.vector.tensor_copy(qr[:, 512:640], ps[:, bank + 1, 0:P]).then_inc(rope_o, 1)
                    return
                n = (s - 1) * TPC + t
                raw = ps_row[:, bank * 512:bank * 512 + 640].rearrange("p (h a f d) -> p h a f d", a=2, f=2, d=16)
                rot = qr.rearrange("p (h a f d) -> p h a f d", a=2, f=2, d=16)
                co, si = (arena[:, bass.ds(at + n * 32, 32)].rearrange("p (o a d) -> p o a d", o=1, a=2).to_broadcast([P, 10, 2, 16])
                          for at in (COS0, SIN0))
                tav = b["ta"].rearrange("p (h a d) -> p h a d", a=2, d=16)
                tbv = b["tb"].rearrange("p (h a d) -> p h a d", a=2, d=16)
                for f, op in ((0, ALU.subtract), (1, ALU.add)):
                    dve.wait_ge(rope_o, START + TPC + 2 * n + f)
                    nc.vector.tensor_tensor(tav, raw[:, :, :, f, :], co, ALU.mult).then_inc(rope_a, 1)
                    nc.vector.tensor_tensor(tbv, raw[:, :, :, 1 - f, :], si, ALU.mult).then_inc(rope_a, 1)
                    dve.wait_ge(rope_a, START + 4 * n + 2 * f + 2)
                    nc.vector.tensor_tensor(rot[:, :, :, f, :], tav, tbv, op).then_inc(rope_o, 1)

            def low_qkv(s, t):
                qr, m = b[f"qr{t}"], TPC * s + t
                if known(s, 1):
                    dve.wait_ge(q_hi, START + (s - 1) * TPC + t + 1)
                    nc.vector.scalar_tensor_tensor(qs[t][:, :, 1, :], qr[:, 0:512].rearrange("p (h d) -> p h d", h=NH), HEAD_SCALE,
                                                   qs[t][:, :, 0, :], ALU.mult, ALU.subtract).then_inc(q_lo, 1)
                dve.wait_ge(k_hi, START + NKV * m + NKV)
                for z in range(NKV):
                    nc.vector.scalar_tensor_tensor(ks[t][:, z, 1], twice(qr, z), HEAD_SCALE, ks[t][:, z, 0],
                                                   ALU.mult, ALU.subtract).then_inc(k_lo, 1)
                dve.wait_ge(v_hi, START + m + 1)
                high, lows = (v[:, t * P:(t + 1) * P] if not known(s, 1) else
                              v[:, bass.ds((3 + t - TPC) * P + s * (TPC * P), P)] for v in (vhi, vlo))
                nc.vector.scalar_tensor_tensor(lows, ps[:, 5 + 2 * t, P:2 * P], HEAD_SCALE, high, ALU.mult, ALU.subtract)\
                    .then_inc(v_lo, 1)

            def body(s, j):
                rope(s, 0)
                low_qkv(s, 0)
                rope(s, 1)
                for c in range(C_RNN):
                    dve.wait_ge(u_mm, START + C_RNN * s + c + 1)
                    dst = uT[:, c, U_CTX:U_CTX + CTX] if not known(s, 1) else \
                        arena[:, bass.ds(UT0 + c * U_ROW + U_LAT - CHUNK + s * CHUNK, CHUNK)]
                    nc.vector.tensor_scalar(dst, ps[:, 2, 0:CHUNK], undo, None, ALU.mult).then_inc(u_ev, 1)
                    if not (isinstance(s, int) and s == LAST):
                        low(s + 1, 1 - j, 2 * c)
                        low(s + 1, 1 - j, 2 * c + 1)
                    if c == 0:
                        low_qkv(s, 1)
                if not (isinstance(s, int) and s >= LAST - 1):
                    norm(s + 2, j)
            dve.wait_ge(pads, START + 8)
            norm(0, 0)
            dve.wait_ge(mcol_tr, START + 1)
            dve.wait_ge(tab_ld, START + 16 * 4)
            nc.vector.tensor_scalar(mcol[:, :, KD:2 * KD], mcol_ps[:, :, KD:2 * KD], 1.0, X_SCALE, ALU.add, ALU.mult).then_inc(sc_ok, 1)
            nc.vector.tensor_scalar(mcol[:, :, 0:KD], mcol_ps[:, :, 0:KD], X_SCALE, None, ALU.mult).then_inc(sc_ok, 1)
            dve.wait_ge(sc_ok, START + 2)
            for k in range(KD):
                low(0, 0, k)
            norm(1, 1)
            steps(dve, body)

        @block.tensor
        def _(pe):
            def transposed(s, j, k):
                if k == 0:
                    pe.wait_ge(normed, START + TPC * s + TPC)
                if known(s, 1) or k > 1:
                    pe.wait_ge(x_lo, START + KD * s + k - 1)
                for t in range(TPC):
                    mm = pe.transpose(ps[:, k % 2, t * P:(t + 1) * P], x[j][:, t, k * P:(k + 1) * P], idn[:])
                mm.then_inc(tr_x, 1)

            def product(o, w, act_hi, act_lo, w_first, first, last):
                wh, wl = w
                pairs = ((wh, act_hi), (wh, act_lo), (wl, act_hi)) if w_first else ((act_hi, wh), (act_hi, wl), (act_lo, wh))
                for n, (lhs, rhs) in enumerate(pairs):
                    mm = pe.matmul(o, lhs, rhs, start=first and n == 0, stop=last and n == 2)
                return mm

            def qk_transposes(s, t):
                bank = 4 + 2 * t
                pe.wait_ge(v_lo, START + TPC * s + t + 1)
                pe.wait_ge(k_lo, START + NKV * (TPC * s + t) + NKV)
                if known(s, 1):
                    pe.wait_ge(q_lo, START + TPC * (s - 1) + t + 1)
                    for h in range(NH):
                        mm = pe.transpose(ps[:, bank, :].bitcast(F16)[:, h * P:(h + 1) * P],
                                          b[f"qs{t}"].bitcast(F16)[:, h * P:(h + 1) * P], idh[:])
                    mm.then_inc(q_tr, 1)
                for z in range(2 * NKV):
                    mm = pe.transpose(ps[:, bank + 1, 256:512].bitcast(F16)[:, z * P:(z + 1) * P],
                                      b[f"ks{t}"].bitcast(F16)[:, z * P:(z + 1) * P], idh[:])
                mm.then_inc(k_tr, 1)

            def body(s, j):
                pe.wait_ge(x_lo, START + KD * s + KD)
                for t in range(TPC):
                    bank = 4 + 2 * t
                    if known(s, 1):
                        pe.wait_ge(k_ev, START + TPC * (s - 1) + t + 1)
                    for k in range(KD):
                        ah, al = hi[j][:, k, t * P:(t + 1) * P], lo[j][:, k, t * P:(t + 1) * P]
                        if known(s, 1):
                            product(ps[:, bank, :], (whi[:, k, D:D + 512], wlo[:, k, D:D + 512]), ah, al, False, k == 0, k == KD - 1)
                        mm = product(ps[:, bank + 1, 0:256], (whi[:, k, D + 512:D_IN], wlo[:, k, D + 512:D_IN]), ah, al, False,
                                     k == 0, k == KD - 1)
                    mm.then_inc(qkv_mm, 1)
                for c in range(C_RNN):
                    for bank, done, read, col in ((2, u_mm, u_ev, 0), (3, g_mm, g_ev, D_RNN)):
                        if bank == 3 and not known(s, 1):
                            continue
                        pe.wait_ge(read, START + C_RNN * (s if bank == 2 else s - 1) + c)
                        cols = slice(col + c * P, col + (c + 1) * P)
                        for k in range(KD):
                            mm = product(ps[:, bank, 0:CHUNK], (whi[:, k, cols], wlo[:, k, cols]), hi[j][:, k, :], lo[j][:, k, :],
                                         True, k == 0, k == KD - 1)
                        mm.then_inc(done, 1)
                    if not (isinstance(s, int) and s == LAST):
                        transposed(s + 1, 1 - j, 2 * c)
                        transposed(s + 1, 1 - j, 2 * c + 1)
                    if c < TPC:
                        qk_transposes(s, c)
            pe.wait_ge(g["const_ld"], 16)
            pe.wait_ge(idh_ok, START + 1)
            pe.wait_ge(tab_ld, START + 16 * 4)
            pe.transpose(ps[:, 2, 0:4 * KD], mrow, idn[0:4 * KD, 0:4 * KD]).then_inc(mcol_tr, 1)
            for k in range(KD):
                transposed(0, 0, k)
            steps(pe, body)


def phase_recurrence(nc, env):
    g = env
    sem, arena, ps, small = g["sem"], g["arena"], g["ps"], g["small"]
    names = ["r00", "r01", "r10", "r11", "g00", "g01", "g10", "g11", "t0", "t1", "d0", "d1"]
    b = arena_slices(arena, B0, [(n, TIME) for n in names] + [("gate", SEQ), ("gw0", 4 * P), ("gw1", 4 * P)])
    gw = [b[f"gw{j}"].rearrange("p (q m) -> p q m", q=4) for j in range(2)]
    par = [small[:, at:at + NPAR] for at in (0, 128)]
    lam_all = small[:, 16:16 + 2 * C_RNN]
    neg_s = small[:, 32:32 + 2 * C_RNN]
    tmp = [small[:, 48 + 8 * n:56 + 8 * n] for n in range(6)]
    s_cur = [small[:, 112:116], small[:, 144:148]]

    lam_ld, gate_ld, zero = sem("c_lam_ld"), sem("c_gate_ld"), sem("c_zero")
    par_ld = [sem("c_par_ld0"), sem("c_par_ld1")]
    sp_v, sp_a, cur, conv = sem("c_sp_v"), sem("c_sp_a"), sem("c_cur"), sem("c_conv")
    g_mm, g_ev, func = sem("c_g_mm"), sem("c_g_ev"), sem("c_func")
    frac, drive, scan, y_done, y_st = sem("c_frac"), sem("c_drive"), sem("c_scan"), sem("c_y"), sem("c_y_st")
    segs = [(0, CTX)] + [(CTX + j * 512, 512) for j in range(4)]

    def tiles(eng, ahead, scans):
        ahead(0, 0)
        with eng.Fori(0, C_RNN // 2 - 1) as i:
            for j in range(2):
                ahead(2 * i + j + 1, 1 - j)
                scans(2 * i + j, j)
        ahead(C_RNN - 1, 1)
        scans(C_RNN - 2, 0)
        scans(C_RNN - 1, 1)

    def half(t):
        return t // 2 if isinstance(t, int) else t >> 1

    with nc.Block() as block:
        @block.sync
        def _(sp):
            sp.dma_start(lam_all, g["lam"]).then_inc(lam_ld, 16)
            sp.wait_ge(zero, START + 2)

            def ahead(t, j):
                if not isinstance(t, int) or t > 1:
                    sp.wait_ge(g_ev, START + 20 * t - 20)
                    sp.sem_inc(g["alone"], 1)
                sp.dma_start(par[j], g["rg_par"].rearrange("(c p) n -> c p n", p=P)[bass.ds(t, 1)]
                             .rearrange("c p n -> (c p) n")).then_inc(par_ld[j], 16)
                for d in range(2):
                    for q, w in enumerate((g["rg_wa"], g["rg_wx"])):
                        for h in range(2):
                            src = w[d].rearrange("(c h) i j -> c h i j", h=2)[bass.ds(t, 1), h]\
                                .rearrange("c i j -> (c i) j")
                            sp.dma_start(gw[j][64 * h:64 * h + 64, 2 * d + q, 64 * h:64 * h + 64], src).then_inc(par_ld[j], 16)

            def scans(t, j):
                sp.wait_ge(y_done, START + 2 * t)
                sp.sem_inc(g["alone"], 1)
                sp.dma_start(b["gate"], g["gate_d"][bass.ds(t, 1)].rearrange("c p t -> (c p) t")).then_inc(gate_ld, 16)
                sp.wait_ge(y_done, START + 2 * t + 2)
                sp.sem_inc(g["alone"], 1)
                sp.dma_start(g["yT_d"][bass.ds(t, 1)].rearrange("c p t -> (c p) t"), b["d0"][:, CTX:TIME]).then_inc(y_st, 16)
            tiles(sp, ahead, scans)
            sp.wait_ge(y_st, START + 16 * C_RNN)

        @block.vector
        def _(dve):
            for j in range(2):
                nc.vector.memset(gw[j], 0.0).then_inc(zero, 1)
            count = [0]

            def link(ins):
                count[0] += 1
                ins.then_inc(sp_v, 1)
                dve.wait_ge(sp_v, START + count[0])
            dve.wait_ge(lam_ld, START + 16)
            link(nc.vector.tensor_scalar(tmp[0], lam_all, -1.0, None, ALU.mult))
            link(nc.vector.tensor_tensor(tmp[1], tmp[0], lam_all, ALU.min))
            link(nc.vector.tensor_scalar(tmp[0], tmp[0], 0.0, None, ALU.max))
            dve.wait_ge(sp_a, START + 1)
            link(nc.vector.tensor_scalar(tmp[3], tmp[2], 2.0, None, ALU.add))
            link(nc.vector.reciprocal(tmp[4], tmp[3]))
            link(nc.vector.tensor_tensor(tmp[3], tmp[2], tmp[4], ALU.mult))
            link(nc.vector.tensor_tensor(tmp[4], tmp[3], tmp[3], ALU.mult))
            link(nc.vector.tensor_scalar(tmp[5], tmp[4], 1.0 / 17, 1.0 / 15, ALU.mult, ALU.add))
            for q in (13, 11, 9, 7, 5, 3, 1):
                link(nc.vector.tensor_tensor(tmp[5], tmp[5], tmp[4], ALU.mult))
                link(nc.vector.tensor_scalar(tmp[5], tmp[5], 1.0 / q, None, ALU.add))
            link(nc.vector.tensor_tensor(tmp[5], tmp[5], tmp[3], ALU.mult))
            link(nc.vector.scalar_tensor_tensor(tmp[5], tmp[5], 2.0, tmp[0], ALU.mult, ALU.add))
            link(nc.vector.tensor_scalar(neg_s, tmp[5], -8.0, None, ALU.mult))

            def ahead(t, j):
                dve.wait_ge(par_ld[j], START + 144 * half(t) + 144)
                for d in range(2):
                    for sgn in range(2):
                        nc.vector.tensor_scalar(s_cur[j][:, 2 * d + sgn:2 * d + sgn + 1],
                                                small[:, bass.ds(32 + d * C_RNN + t, 1)],
                                                -1.0 if sgn == 0 else 1.0, None, ALU.mult).then_inc(cur, 1)
                for q in range(CONV_W):
                    dve.wait_ge(conv, START + 8 * t + 2 * q)
                    for n, (lo, ln, at) in enumerate(((0, CTX, U_CTX), (CTX, SEQ, U_LAT))):
                        src = arena[:, bass.ds(UT0 + t * U_ROW + at - 2 + q, ln)]
                        dst = arena[:, bass.ds(X0 + t * U_ROW + lo, ln)]
                        if q == 0:
                            nc.vector.tensor_scalar(dst, src, par[j][:, 0:1], par[j][:, 4:5], ALU.mult, ALU.add)\
                                .then_inc(conv, 1)
                        else:
                            nc.vector.scalar_tensor_tensor(dst, src, par[j][:, q:q + 1], dst, ALU.mult, ALU.add)\
                                .then_inc(conv, 1)

            def scans(t, j):
                x = arena[:, bass.ds(X0 + t * U_ROW, TIME)]
                dve.wait_ge(y_st, START + 16 * t)
                for d in range(2):
                    T, Dn, G, R = b[f"t{d}"], b[f"d{d}"], b[f"g{d}{j}"], b[f"r{d}{j}"]
                    dve.wait_ge(func, START + 6 * t + d + 3)
                    nc.vector.tensor_tensor(Dn, R, R, ALU.mult).then_inc(frac, 1)
                    dve.wait_ge(frac, START + 4 * t + 2 * d + 1)
                    nc.vector.scalar_tensor_tensor(T, Dn, 1.0, T, ALU.add, ALU.mult).then_inc(frac, 1)
                for d in range(2):
                    dve.wait_ge(g_ev, START + 20 * t + 10 * d + 10)
                    nc.vector.tensor_tensor(b[f"g{d}{j}"], b[f"g{d}{j}"], x, ALU.mult).then_inc(drive, 1)
                for d in range(2):
                    T, Dn, G, R = b[f"t{d}"], b[f"d{d}"], b[f"g{d}{j}"], b[f"r{d}{j}"]
                    dve.wait_ge(func, START + 6 * t + d + 5)
                    dve.wait_ge(drive, START + 4 * t + d + 1)
                    nc.vector.tensor_tensor(G, G, T, ALU.mult).then_inc(drive, 1)
                    dve.wait_ge(drive, START + 4 * t + 3 + d)
                    if d == 0:
                        nc.vector.tensor_tensor_scan(Dn, R, G, 0.0, ALU.mult, ALU.add).then_inc(scan, 1)
                    else:
                        nc.vector.tensor_tensor_scan(Dn[:, CTX - 1::-1], R[:, CTX - 1::-1], G[:, CTX - 1::-1], 0.0,
                                                     ALU.mult, ALU.add).then_inc(scan, 1)
                        dve.wait_ge(scan, START + 3 * t + 2)
                        nc.vector.tensor_tensor_scan(Dn[:, TIME - 1:CTX - 1:-1], R[:, TIME - 1:CTX - 1:-1],
                                                     G[:, TIME - 1:CTX - 1:-1], Dn[:, 0:1],
                                                     ALU.mult, ALU.add).then_inc(scan, 1)
                dve.wait_ge(scan, START + 3 * t + 3)
                y = b["d0"][:, CTX:TIME]
                nc.vector.tensor_tensor(y, y, b["d1"][:, CTX:TIME], ALU.add).then_inc(y_done, 1)
                dve.wait_ge(y_done, START + 2 * t + 1)
                dve.wait_ge(gate_ld, START + 16 * t + 16)
                nc.vector.tensor_tensor(y, y, b["gate"], ALU.mult).then_inc(y_done, 1)
            tiles(dve, ahead, scans)

        @block.scalar
        def _(act):
            act.wait_ge(sp_v, START + 3)
            nc.scalar.activation(tmp[2], tmp[1], ACT.Exp).then_inc(sp_a, 1)

            def gates(t, j):
                if not isinstance(t, int) or t > 1:
                    act.wait_ge(scan, START + 3 * t - 3)
                for d in range(2):
                    for q in range(2):
                        dst = b[f"{'rg'[q]}{d}{j}"]
                        for n, (lo, ln) in enumerate(segs):
                            idx = (2 * d + q) * 5 + n
                            act.wait_ge(g_mm, START + 20 * t + idx + 1)
                            nc.scalar.activation(dst[:, lo:lo + ln], ps[:, idx % 4, 0:ln], ACT.Sigmoid,
                                                 bias=par[j][:, 5 + 2 * q + d:6 + 2 * q + d]).then_inc(g_ev, 1)

            def functions(t, j):
                act.wait_ge(cur, START + 4 * t + 4)
                act.wait_ge(g_ev, START + 20 * t + 20)
                act.wait_ge(drive, START + 4 * t)
                for d in range(2):
                    nc.scalar.activation(b[f"t{d}"], b[f"r{d}{j}"], ACT.Tanh, scale=s_cur[j][:, 2 * d:2 * d + 1])\
                        .then_inc(func, 1)
                act.wait_ge(func, START + 6 * t + 2)
                for d in range(2):
                    nc.scalar.activation(b[f"r{d}{j}"], b[f"r{d}{j}"], ACT.Exp, scale=s_cur[j][:, 2 * d + 1:2 * d + 2])\
                        .then_inc(func, 1)
                act.wait_ge(func, START + 6 * t + 4)
                for d in range(2):
                    act.wait_ge(frac, START + 4 * t + 2 * d + 2)
                    nc.scalar.activation(b[f"t{d}"], b[f"t{d}"], ACT.Sqrt).then_inc(func, 1)
            gates(0, 0)
            with act.Fori(0, C_RNN // 2 - 1) as i:
                for j in range(2):
                    functions(2 * i + j, j)
                    gates(2 * i + j + 1, 1 - j)
            functions(C_RNN - 2, 0)
            gates(C_RNN - 1, 1)
            functions(C_RNN - 1, 1)

        @block.tensor
        def _(pe):
            def gates(t, j):
                pe.wait_ge(par_ld[j], START + 144 * half(t) + 144)
                pe.wait_ge(conv, START + 8 * t + 8)
                for dq in range(4):
                    for n, (lo, ln) in enumerate(segs):
                        idx = dq * 5 + n
                        pe.wait_ge(g_ev, START + 20 * t + max(idx - 3, 0))
                        pe.matmul(ps[:, idx % 4, 0:ln], gw[j][:, dq, :], arena[:, bass.ds(X0 + t * U_ROW + lo, ln)],
                                  start=True, stop=True).then_inc(g_mm, 1)
            tiles(pe, gates, lambda t, j: None)


def phase_attention(nc, env):
    g = env
    sem, arena, ps, ps_row, small, idn = g["sem"], g["arena"], g["ps"], g["ps_row"], g["small"], g["idn"]
    b = arena_slices(arena, B0, [("mask0", KEYS), ("mask1", KEYS), ("q0", 512), ("q1", 512), ("s0", KEYS), ("s1", KEYS),
                                 ("phi0", KEYS // 2), ("phi1", KEYS // 2), ("plo0", KEYS // 2), ("plo1", KEYS // 2),
                                 ("o0", 512), ("o1", 512)])
    kT, vhi, vlo = arena[:, KT0:V0].bitcast(F16), *split_v(arena)
    sinks = small[:, 0:NH]
    mx = [small[:, 8 + 64 * j:16 + 64 * j] for j in range(2)]
    nm = [small[:, 16 + 64 * j:24 + 64 * j] for j in range(2)]
    den = [small[:, 24 + 64 * j:32 + 64 * j] for j in range(2)]
    es = [small[:, 32 + 64 * j:40 + 64 * j] for j in range(2)]
    rd = [small[:, 40 + 64 * j:48 + 64 * j] for j in range(2)]
    mask_ld, s_mm, s_max, nm_d, p_d = sem("d_mask_ld"), sem("d_s_mm"), sem("d_s_max"), sem("d_nm"), sem("d_p")
    q_ld, o_st = [sem("d_q_ld0"), sem("d_q_ld1")], [sem("d_o_st0"), sem("d_o_st1")]
    p_tr, p_hi, p_lo, pv_mm = sem("d_p_tr"), sem("d_p_hi"), sem("d_p_lo"), sem("d_pv")
    es_d, es_e, den_d, o_d = sem("d_es"), sem("d_es_e"), sem("d_den"), sem("d_o")
    w_ld, w_gate = sem("d_w_ld"), sem("d_w_gate")
    ow = output_weights(arena)
    wo = ow["wo"].rearrange("p (k n) -> p k n", k=KD)
    undo = HD ** -0.5 / (X_SCALE * X_SCALE)
    HEADS = [(j, h) for j in range(2) for h in range(NH)]

    def pT(h):
        return ps_row[:, 1024 * (1 + h % 2):1024 * (1 + h % 2) + KEYS]

    with nc.Block() as block:
        @block.sync
        def _(sp):
            sp.dma_start(sinks, g["sink"]).then_inc(mask_ld, 16)

            def load(i, j):
                kind = ((2 * i + j + 15) >> 4) + ((2 * i + j + 1) >> 4)
                sp.dma_start(b[f"mask{j}"], g["masks"][bass.ds(kind, 1)].rearrange("m p k -> (m p) k")).then_inc(q_ld[j], 16)
                sp.dma_start(b[f"q{j}"], g["qT_d"][bass.ds(2 * i + j, 1)].rearrange("n p d -> (n p) d")).then_inc(q_ld[j], 16)
            for j in range(2):
                load(0, j)
            sp.dma_start(wo, g["w_out"].rearrange("(k p) n -> p k n", p=P)).then_inc(w_ld, 16)
            sp.dma_start(ow["gnc"], g["gn"]).then_inc(w_ld, 16)
            for name, src in (("g1", g["mod_rows"][0:1, 2 * D:3 * D]), ("sh2", g["mod_rows"][0:1, 3 * D:4 * D]),
                              ("sc2", g["mod_rows"][0:1, 4 * D:5 * D]), ("l1g", g["ln1"][0:1, :]),
                              ("l1b", g["ln1"][1:2, :]), ("br", g["router_b"])):
                sp.dma_start(ow[name], src.to_broadcast([P, src.shape[1]])).then_inc(w_ld, 16)
            sp.dma_start(ow["wr"].rearrange("p (k n) -> p k n", k=KD), g["router"].rearrange("(k p) n -> p k n", p=P))\
                .then_inc(w_ld, 16)

            def store(i, j):
                t = 2 * i + j
                sp.wait_ge(o_d, START + t + 1)
                sp.sem_inc(g["alone"], 1)
                sp.dma_start(g["attn_d"][bass.ds(t, 1)].rearrange("n p d -> (n p) d"), b[f"o{j}"]).then_inc(o_st[j], 16)
            with sp.Fori(0, T_LAT // 2 - 1) as i:
                for j in range(2):
                    sp.wait_ge(s_max, START + 16 * i + NH * j + NH)
                    sp.sem_inc(g["alone"], 1)
                    load(i + 1, j)
                    store(i, j)
            for j in range(2):
                store(T_LAT // 2 - 1, j)
            for j in range(2):
                sp.wait_ge(o_st[j], START + 16 * (T_LAT // 2))

        @block.gpsimd
        def _(pool):
            pool.wait_ge(w_ld, START + 16 * 9)
            for k in range(KD):
                nc.gpsimd.tensor_tensor(wo[:, k, :], wo[:, k, :], ow["g1"], ALU.mult).then_inc(w_gate, 1)
            nc.gpsimd.tensor_scalar(ow["gnc"], ow["gnc"], W_SCALE, None, ALU.mult).then_inc(w_gate, 1)

        @block.tensor
        def _(pe):
            def scores(i, j, h):
                t = 2 * i + j
                z = h // GROUP
                if h == 0:
                    pe.wait_ge(q_ld[j], START + 32 * i + 32)
                pe.wait_ge(s_max, START + i * 16 + j * NH + h)
                q = b[f"q{j}"].bitcast(F16)[:, h * P:(h + 1) * P]
                for o, ln, key, moves in ((0, CTX, 0, False), (CTX, 256, K_LAT - P, True), (512, P, K_LAT + P, True)):
                    for part in range(2):
                        k0 = (2 * z + part) * K_ROW + key
                        keys = kT[:, bass.ds(k0 + t * P, ln)] if moves else kT[:, k0:k0 + ln]
                        mm = pe.matmul(ps_row[:, o:o + ln], q, keys, start=(part == 0), stop=(part == 1))
                mm.then_inc(s_mm, 1)

            def transposes(i, j, h):
                n = i * 16 + j * NH + h
                pe.wait_ge(p_d, START + n + 1)
                pe.wait_ge(p_lo, START + i * 16 + max(j * NH + h - 1, 0))
                for q in range(KEYS // P):
                    mm = pe.transpose(pT(h)[:, q * P:(q + 1) * P], b[f"s{h % 2}"][:, q * P:(q + 1) * P], idn[:])
                mm.then_inc(p_tr, 1)

            def values(i, j, h):
                t = 2 * i + j
                n = i * 16 + j * NH + h
                z = h // GROUP
                pe.wait_ge(p_lo, START + n + 1)
                if h == 0:
                    pe.wait_ge(o_d, START + (2 * i + j - 1 if j else 2 * i))
                phi, plo = (b[f"{part}{h % 2}"].bitcast(F16) for part in ("phi", "plo"))
                for q in range(KEYS // P):
                    at = q * P + z * HD
                    vh, vl = (v[:, at:at + HD] if q < 2 else v[:, bass.ds(at + t * P, HD)] for v in (vhi, vlo))
                    ph, pl = phi[:, q * P:(q + 1) * P], plo[:, q * P:(q + 1) * P]
                    o = ps[:, 6 + j, h * HD:(h + 1) * HD]
                    pe.matmul(o, ph, vh, start=(q == 0), stop=False)
                    pe.matmul(o, ph, vl, start=False, stop=False)
                    mm = pe.matmul(o, pl, vh, start=False, stop=(q == KEYS // P - 1))
                mm.then_inc(pv_mm, 1)
            with pe.Fori(0, T_LAT // 2) as i:
                scores(i, *HEADS[0])
                scores(i, *HEADS[1])
                for n, head in enumerate(HEADS):
                    if n > 1:
                        values(i, *HEADS[n - 2])
                    transposes(i, *head)
                    if n + 2 < len(HEADS):
                        scores(i, *HEADS[n + 2])
                values(i, *HEADS[-2])
                values(i, *HEADS[-1])

        @block.vector
        def _(dve):
            dve.wait_ge(mask_ld, START + 16)

            def smax(i, j, h):
                t = 2 * i + j
                n = i * 16 + j * NH + h
                dve.wait_ge(s_mm, START + n + 1)
                if h == 0:
                    dve.wait_ge(q_ld[j], START + 32 * i + 32)
                dve.wait_ge(p_tr, START + i * 16 + max(j * NH + h - 1, 0))
                dve.sem_inc(g["alone"], 1)
                nc.vector.tensor_tensor_reduce(b[f"s{h % 2}"], ps_row[:, 0:KEYS],
                                               b[f"mask{j}"],
                                               undo, NEG, ALU.add, ALU.max, mx[j][:, h:h + 1]).then_inc(s_max, 1)
                dve.wait_ge(s_max, START + n + 1)
                if h == 0:
                    dve.wait_ge(es_e, START + (t - 1 if j else t))
                nc.vector.tensor_scalar(nm[j][:, h:h + 1], mx[j][:, h:h + 1], sinks[:, h:h + 1], -1.0, ALU.max, ALU.mult)\
                    .then_inc(nm_d, 1)

            def low_p(i, j, h):
                n = i * 16 + j * NH + h
                dve.wait_ge(p_hi, START + n + 1)
                nc.vector.scalar_tensor_tensor(b[f"plo{h % 2}"].bitcast(F16), pT(h), P_SCALE,
                                               b[f"phi{h % 2}"].bitcast(F16), ALU.mult, ALU.subtract).then_inc(p_lo, 1)

            def sink_exponent(i, j):
                t = 2 * i + j
                dve.wait_ge(nm_d, START + NH * t + NH)
                nc.vector.tensor_tensor(es[j], sinks, nm[j], ALU.add).then_inc(es_d, 1)

            def normalise(i, j):
                t = 2 * i + j
                dve.wait_ge(es_e, START + t + 1)
                nc.vector.tensor_tensor(den[j], den[j], es[j], ALU.add).then_inc(den_d, 1)
                dve.wait_ge(den_d, START + 3 * t + 1)
                nc.vector.tensor_scalar(den[j], den[j], P_SCALE * X_SCALE, None, ALU.mult).then_inc(den_d, 1)
                dve.wait_ge(den_d, START + 3 * t + 2)
                nc.vector.reciprocal(rd[j], den[j]).then_inc(den_d, 1)
                dve.wait_ge(den_d, START + 3 * t + 3)
                dve.wait_ge(pv_mm, START + NH * t + NH)
                dve.wait_ge(o_st[j], START + 16 * i)
                nc.vector.tensor_tensor(b[f"o{j}"].rearrange("p (h d) -> p h d", h=NH),
                                        ps[:, 6 + j, :].rearrange("p (h d) -> p h d", h=NH),
                                        rd[j].rearrange("p (h o) -> p h o", o=1).to_broadcast([P, NH, HD]),
                                        ALU.mult).then_inc(o_d, 1)
            with dve.Fori(0, T_LAT // 2) as i:
                smax(i, *HEADS[0])
                for n in range(len(HEADS)):
                    if n + 1 < len(HEADS):
                        smax(i, *HEADS[n + 1])
                    if n:
                        low_p(i, *HEADS[n - 1])
                    if n == NH - 1:
                        sink_exponent(i, 0)
                    if n == NH + 3:
                        normalise(i, 0)
                sink_exponent(i, 1)
                low_p(i, *HEADS[-1])
                normalise(i, 1)

        @block.scalar
        def _(act):
            def high_p(i, j, h):
                n = i * 16 + j * NH + h
                act.wait_ge(p_tr, START + n + 1)
                act.wait_ge(pv_mm, START + i * 16 + max(j * NH + h - 1, 0))
                nc.scalar.activation(b[f"phi{h % 2}"].bitcast(F16), pT(h), ACT.Copy, scale=P_SCALE)\
                    .then_inc(p_hi, 1)

            def exp_sink(i, j):
                t = 2 * i + j
                act.wait_ge(es_d, START + t + 1)
                nc.scalar.activation(es[j], es[j], ACT.Exp).then_inc(es_e, 1)
            with act.Fori(0, T_LAT // 2) as i:
                for n, (j, h) in enumerate(HEADS):
                    act.wait_ge(nm_d, START + 16 * i + n + 1)
                    if h == 0:
                        act.wait_ge(den_d, START + 6 * i)
                    nc.scalar.activation(b[f"s{h % 2}"], b[f"s{h % 2}"], ACT.Exp, bias=nm[j][:, h:h + 1],
                                         accum_out=den[j][:, h:h + 1]).then_inc(p_d, 1)
                    if n:
                        high_p(i, *HEADS[n - 1])
                    if n == NH:
                        exp_sink(i, 0)
                exp_sink(i, 1)
                high_p(i, *HEADS[-1])


def phase_output(nc, env):
    g = env
    sem, arena, ps, ps_row, small, idn = g["sem"], g["arena"], g["ps"], g["ps_row"], g["small"], g["idn"]
    b = arena_slices(arena[:, 0:OUT_W0], 0, [("logits", T_LAT * 36), ("ones", 1), ("mh", 2), ("ysq", 512), ("asq", 512)]
                     + [(n, 256) for n in ("yhi", "ylo", "ahi", "alo")]
                     + [(f"{n}{j}", s) for n, s in (("yT", 512), ("at", 512), ("xt", D), ("x1", D), ("h2", D)) for j in range(2)]
                     + [("t0", D), ("t1", D), ("x1n", D), ("h2T", D)])
    b.update(output_weights(arena))
    wo = b["wo"].rearrange("p (k n) -> p k n", k=KD)
    whi, wlo = (b[n].bitcast(F16).rearrange("p (k n) -> p k n", k=KD) for n in ("whi", "wlo"))
    yhi, ylo, ahi, alo = (b[n].bitcast(F16) for n in ("yhi", "ylo", "ahi", "alo"))
    wr = b["wr"].rearrange("p (k n) -> p k n", k=KD)
    ss = [small[:, 8 * j:8 * j + 2] for j in range(2)]
    ssv = [small[:, 8 * j + 2:8 * j + 4] for j in range(2)]
    sr = [small[:, 8 * j + 4:8 * j + 6] for j in range(2)]
    st = small[:, 16:28]
    mv = small[:, 28:30]
    ve = small[:, 30:31]
    rs = small[:, 31:32]
    w_ok, w_hi, w_lo, p_ok = sem("e_w_ok"), sem("e_w_hi"), sem("e_w_lo"), sem("e_p_ok")
    in_ld, xt_ld = [sem("e_in_ld0"), sem("e_in_ld1")], [sem("e_xt_ld0"), sem("e_xt_ld1")]
    x_st, h_st = [sem("e_x_st0"), sem("e_x_st1")], [sem("e_h_st0"), sem("e_h_st1")]
    sq, hi, lo, ssm, ss_d, ssv_d, pw_s = (sem("e_sq"), sem("e_hi"), sem("e_lo"), sem("e_ssm"), sem("e_ss"), sem("e_ssv"),
                                              sem("e_pw_s"))
    a_tr = sem("e_a_tr")
    o_mm, o_act, v, pw = sem("e_o_mm"), sem("e_o_act"), sem("e_v"), sem("e_pw")
    h_tr, h_ev, r_mm, lg = sem("e_h_tr"), sem("e_h_ev"), sem("e_r_mm"), sem("e_lg")
    scale = W_SCALE * X_SCALE
    NV = 14

    def tiles(eng, prepare, project, normalise, route):
        def step(t, j, first=False, second=False, last=False):
            project(t, j)
            if not first:
                normalise(t - 1, 1 - j)
            if not last:
                prepare(t + 1, 1 - j)
            if not first and not second:
                route(t - 2, j)
        prepare(0, 0)
        step(0, 0, first=True)
        step(1, 1, second=True)
        with eng.Fori(1, T_LAT // 2 - 1) as i:
            step(2 * i, 0)
            step(2 * i + 1, 1)
        step(T_LAT - 2, 0)
        step(T_LAT - 1, 1, last=True)
        normalise(T_LAT - 1, 1)
        route(T_LAT - 2, 0)
        route(T_LAT - 1, 1)

    def none(t, j):
        pass

    def half(t):
        return t // 2 if isinstance(t, int) else t >> 1
    with nc.Block() as block:
        @block.sync
        def _(sp):
            def load_in(t, j):
                sp.dma_start(b[f"yT{j}"].rearrange("p (c t) -> p c t", c=C_RNN),
                             g["yT_d"][:, :, bass.ds(t * P, P)].rearrange("c p t -> p c t")).then_inc(in_ld[j], 16)
                sp.dma_start(b[f"at{j}"], g["attn_d"][bass.ds(t, 1)].rearrange("n p d -> (n p) d")).then_inc(in_ld[j], 16)

            def load_x(t, j):
                sp.dma_start(b[f"xt{j}"], g["x"][bass.ds(t * P, P), :]).then_inc(xt_ld[j], 16)

            def stores(t, j):
                sp.wait_ge(v, START + NV * t + 8)
                sp.sem_inc(g["alone"], 1)
                sp.dma_start(g["x1_d"][bass.ds(t * P, P), :], b[f"x1{j}"]).then_inc(x_st[j], 16)
                sp.wait_ge(v, START + NV * t + 14)
                sp.sem_inc(g["alone"], 1)
                sp.dma_start(g["h2_d"][bass.ds(t * P, P), :], b[f"h2{j}"]).then_inc(h_st[j], 16)

            for j in range(2):
                load_in(j, j)
                load_x(j, j)
            with sp.Fori(0, T_LAT // 2 - 1) as i:
                for j in range(2):
                    t = 2 * i + j
                    sp.wait_ge(lo, START + 2 * t + 2)
                    sp.sem_inc(g["alone"], 1)
                    sp.wait_ge(sq, START + 2 * t + 2)
                    sp.sem_inc(g["alone"], 1)
                    load_in(t + 2, j)
                    stores(t, j)
                    load_x(t + 2, j)
            for j in range(2):
                stores(T_LAT - 2 + j, j)
            for j in range(2):
                sp.wait_ge(x_st[j], START + 16 * (T_LAT // 2))
                sp.wait_ge(h_st[j], START + 16 * (T_LAT // 2))

        @block.gpsimd
        def _(pool):
            nc.gpsimd.memset(b["mh"], -0.5).then_inc(p_ok, 1)
            nc.gpsimd.memset(b["ones"], 1.0).then_inc(p_ok, 1)
            pool.wait_ge(p_ok, START + 2)

            def prepare(t, j):
                pool.wait_ge(ssv_d, START + t + 1)
                pool.sem_inc(g["alone"], 1)
                nc.gpsimd.tensor_tensor(sr[j], ssv[j], b["mh"], ALU.pow).then_inc(pw_s, 1)

            def normalise(t, j):
                for n in (6, 12):
                    pool.wait_ge(v, START + NV * t + n)
                    pool.sem_inc(g["alone"], 1)
                    nc.gpsimd.tensor_tensor(rs, ve, b["mh"][:, 0:1], ALU.pow).then_inc(pw, 1)
            tiles(pool, prepare, none, normalise, none)

        @block.vector
        def _(dve):
            nc.vector.tensor_scalar(b["sc2"], b["sc2"], 1.0, None, ALU.add).then_inc(w_ok, 1)
            dve.wait_ge(w_ok, START + 1)
            for k in range(KD):
                dve.wait_ge(w_hi, START + k + 1)
                nc.vector.scalar_tensor_tensor(wlo[:, k, :], wo[:, k, :], b["gnc"][:, k:k + 1], whi[:, k, :], ALU.mult, ALU.subtract)\
                    .then_inc(w_lo, 1)

            def prepare(t, j):
                dve.wait_ge(hi, START + 2 * t + 1)
                dve.wait_ge(o_mm, START + t)
                nc.vector.scalar_tensor_tensor(ylo, b[f"yT{j}"], X_SCALE, yhi, ALU.mult, ALU.subtract).then_inc(lo, 1)
                dve.wait_ge(hi, START + 2 * t + 2)
                nc.vector.scalar_tensor_tensor(alo, ps[:, 6, :], X_SCALE, ahi, ALU.mult, ALU.subtract).then_inc(lo, 1)
                dve.wait_ge(ss_d, START + t + 1)
                dve.wait_ge(sq, START + 2 * t + 2)
                nc.vector.tensor_scalar(ssv[j], ss[j], scale * scale / 512, scale * scale * EPS, ALU.mult, ALU.add)\
                    .then_inc(ssv_d, 1)

            def normalise(t, j):
                base = NV * t
                step = [0]

                def link(ins):
                    step[0] += 1
                    ins.then_inc(v, 1)
                    dve.wait_ge(v, START + base + step[0])
                t1, x1, x1n, h2 = b["t1"], b[f"x1{j}"], b["x1n"], b[f"h2{j}"]
                dve.wait_ge(o_act, START + t + 1)
                link(nc.vector.scalar_tensor_tensor(t1, ps_row[:, 2048:3072], sr[j][:, 1:2], b["t0"], ALU.mult, ALU.add))
                dve.wait_ge(xt_ld[j], START + 16 * half(t) + 16)
                link(nc.vector.scalar_tensor_tensor(t1, b[f"xt{j}"], ALPHA, t1, ALU.mult, ALU.add))
                nc.vector.bn_stats(st[:, 0:6], t1[:, 0:512]).then_inc(v, 1)
                step[0] += 1
                link(nc.vector.bn_stats(st[:, 6:12], t1[:, 512:1024]))
                dve.sem_inc(g["alone"], 1)
                link(nc.vector.bn_aggr(mv, st.rearrange("p (a s) -> p a s", a=2)))
                link(nc.vector.tensor_scalar(ve, mv[:, 1:2], EPS, None, ALU.add))
                link(nc.vector.scalar_tensor_tensor(t1, t1, mv[:, 0:1], b["l1g"], ALU.subtract, ALU.mult))
                dve.wait_ge(pw, START + 2 * t + 1)
                dve.wait_ge(x_st[j], START + 16 * half(t))
                link(nc.vector.scalar_tensor_tensor(x1, t1, rs, b["l1b"], ALU.mult, ALU.add))
                nc.vector.bn_stats(st[:, 0:6], x1[:, 0:512]).then_inc(v, 1)
                step[0] += 1
                link(nc.vector.bn_stats(st[:, 6:12], x1[:, 512:1024]))
                dve.sem_inc(g["alone"], 1)
                link(nc.vector.bn_aggr(mv, st.rearrange("p (a s) -> p a s", a=2)))
                link(nc.vector.tensor_scalar(ve, mv[:, 1:2], EPS, None, ALU.add))
                link(nc.vector.scalar_tensor_tensor(x1n, x1, mv[:, 0:1], b["sc2"], ALU.subtract, ALU.mult))
                dve.wait_ge(pw, START + 2 * t + 2)
                dve.wait_ge(h_st[j], START + 16 * half(t))
                if not isinstance(t, int) or t > 1:
                    dve.wait_ge(h_tr, START + 2 * t - 2)
                link(nc.vector.scalar_tensor_tensor(h2, x1n, rs, b["sh2"], ALU.mult, ALU.add))

            def route(t, j):
                dve.wait_ge(r_mm, START + t + 1)
                nc.vector.tensor_tensor(arena[:, bass.ds(t * 36, 36)], ps[:, 7, 0:36], b["br"], ALU.add).then_inc(lg, 1)
            tiles(dve, prepare, none, normalise, route)

        @block.scalar
        def _(act):
            for k in range(KD):
                nc.scalar.activation(whi[:, k, :], wo[:, k, :], ACT.Copy, scale=b["gnc"][:, k:k + 1]).then_inc(w_hi, 1)

            def prepare(t, j):
                act.wait_ge(in_ld[j], START + 32 * half(t) + 32)
                act.wait_ge(ssm, START + t)
                nc.scalar.activation(b["ysq"], b[f"yT{j}"], ACT.Square).then_inc(sq, 1)
                act.wait_ge(ssv_d, START + t)
                nc.scalar.activation(b["asq"], b[f"at{j}"], ACT.Square, accum_out=ss[j][:, 1:2]).then_inc(sq, 1)
                act.wait_ge(o_mm, START + t)
                nc.scalar.activation(yhi, b[f"yT{j}"], ACT.Copy, scale=X_SCALE).then_inc(hi, 1)
                act.wait_ge(a_tr, START + t + 1)
                nc.scalar.activation(ahi, ps[:, 6, :], ACT.Copy, scale=X_SCALE).then_inc(hi, 1)
                act.wait_ge(ssm, START + t + 1)
                nc.scalar.activation(ss[j][:, 0:1], ps[:, 0, 0:1], ACT.Copy).then_inc(ss_d, 1)

            def normalise(t, j):
                act.wait_ge(o_mm, START + t + 1)
                act.wait_ge(pw_s, START + t + 1)
                if not isinstance(t, int) or t > 0:
                    act.wait_ge(v, START + NV * t - NV + 1)
                nc.scalar.activation(b["t0"], ps_row[:, 1024:2048], ACT.Copy, scale=sr[j][:, 0:1]).then_inc(o_act, 1)

            def route(t, j):
                for n in range(2):
                    act.wait_ge(h_tr, START + 2 * t + n + 1)
                    if n == 0:
                        act.wait_ge(r_mm, START + t)
                    nc.scalar.activation(b["h2T"][:, n * 512:(n + 1) * 512], ps[:, n, :], ACT.Copy).then_inc(h_ev, 1)
            tiles(act, prepare, none, normalise, route)

        @block.tensor
        def _(pe):
            pe.wait_ge(p_ok, START + 2)
            pe.wait_ge(w_lo, START + KD)

            def prepare(t, j):
                pe.wait_ge(in_ld[j], START + 32 * half(t) + 32)
                pe.wait_ge(lo, START + 2 * t)
                for c in range(C_RNN):
                    mm = pe.transpose(ps[:, 6, c * P:(c + 1) * P], b[f"at{j}"][:, c * P:(c + 1) * P], idn[:])
                mm.then_inc(a_tr, 1)
                pe.wait_ge(sq, START + 2 * t + 1)
                if not isinstance(t, int) or t > 3:
                    pe.wait_ge(h_ev, START + 2 * t - 6)
                for c in range(C_RNN):
                    mm = pe.matmul(ps[:, 0, 0:1], b["ysq"][:, c * P:(c + 1) * P], b["ones"], start=(c == 0), stop=(c == C_RNN - 1))
                mm.then_inc(ssm, 1)

            def project(t, j):
                for bank, high, low, k0, ready in ((2, yhi, ylo, 0, 1), (4, ahi, alo, C_RNN, 2)):
                    pe.wait_ge(lo, START + 2 * t + ready)
                    if bank == 2:
                        pe.wait_ge(o_act, START + t)
                    elif not isinstance(t, int) or t > 0:
                        pe.wait_ge(v, START + NV * t - NV + 1)
                    for k in range(C_RNN):
                        for n in range(2):
                            o, cols = ps[:, bank + n, :], slice(n * 512, (n + 1) * 512)
                            lhs_hi, lhs_lo = high[:, k * P:(k + 1) * P], low[:, k * P:(k + 1) * P]
                            pe.matmul(o, lhs_hi, whi[:, k0 + k, cols], start=(k == 0), stop=False)
                            pe.matmul(o, lhs_hi, wlo[:, k0 + k, cols], start=False, stop=False)
                            mm = pe.matmul(o, lhs_lo, whi[:, k0 + k, cols], start=False, stop=(k == C_RNN - 1))
                mm.then_inc(o_mm, 1)

            def route(t, j):
                pe.wait_ge(v, START + NV * t + 14)
                pe.wait_ge(ss_d, START + t + 4 if not isinstance(t, int) else START + min(t + 4, T_LAT))
                pe.wait_ge(h_ev, START + 2 * t)
                for n in range(2):
                    for c in range(4):
                        mm = pe.transpose(ps[:, n, c * P:(c + 1) * P], b[f"h2{j}"][:, (4 * n + c) * P:(4 * n + c + 1) * P], idn[:])
                    mm.then_inc(h_tr, 1)
                pe.wait_ge(h_ev, START + 2 * t + 2)
                pe.wait_ge(lg, START + t)
                for k in range(KD):
                    mm = pe.matmul(ps[:, 7, 0:36], b["h2T"][:, k * P:(k + 1) * P], wr[:, k, :], start=(k == 0), stop=(k == KD - 1))
                mm.then_inc(r_mm, 1)
            tiles(pe, prepare, project, none, route)


W13 = 2 * KD * D_EXP
W2 = KE * D
WSZ = W13 + W2
PIECE = 2048
N13, N2 = W13 // PIECE, W2 // PIECE
STAGE0 = 2 * WSZ


def load_piece(sp, g, e, n):
    if n < N13:
        src = g[("w1", "w3")[n // (N13 // 2)]][bass.ds(e, 1)].rearrange("e (k p) n -> p (e k) n", p=P)
        k0, cols = n % (N13 // 2) * (PIECE // D_EXP), D_EXP
    else:
        src = g["w2"][bass.ds(e, 1)].rearrange("e (k p) n -> p (e k) n", p=P)
        k0, cols = (n - N13) * (PIECE // D), D
    at = STAGE0 + n * PIECE
    sp.dma_start(g["arena"][:, at:at + PIECE].rearrange("p (k n) -> p k n", n=cols), src[:, k0:k0 + PIECE // cols, :])\
        .then_inc(g["sem"](f"g_st_ld{n}"), 16)


def phase_route(nc, env):
    g = env
    sem, arena, ps, ps_row, idn = g["sem"], g["arena"], g["ps"], g["ps_row"], g["idn"]
    T = T_LAT
    names = [("logits", T * 36), ("pad8", T * 8), ("gm8", T * 8), ("gi8", T * 8), ("gif", T), ("goh", T * NG),
             ("elm", T * NE), ("em8", T * 8), ("ei8", T * 8), ("eif", 2 * T), ("gex", T * NG), ("gsum", T), ("pg", T),
             ("dif", T), ("q", T), ("oh0", T * NE), ("oh1", T * NE), ("ohs", T * NE), ("base", (T + 1) * NE),
             ("rank", T * NE), ("sel", T * NE), ("slotf", 2 * T), ("nbi", NE), ("nb", NE), ("pend", NE), ("pst", NE),
             ("one32", NE), ("ones", P), ("tri", P), ("iota", 64), ("tok", T), ("ge", 64 * NE), ("has", NE), ("rk", NE), ("rend", NE), ("ebf", 64), ("nw", 64),
             ("st_i", P), ("st_f", P)]
    b = arena_slices(arena, 0, names)
    v3 = lambda name, t, n: b[name].rearrange("p (t n) -> p t n", t=t)
    slot_i, gates, tab, gidx = g["slot_i"], g["gates"], g["blk_tab"], g["gidx"]
    f_ld, v, act_d, mm, scat, tr = sem("f_ld"), sem("f_v"), sem("f_act"), sem("f_mm"), g["plain_sem"]("f_scat"), sem("f_tr")
    mark = {}

    with nc.Block() as block:
        @block.vector
        def _(dve):
            n = [0]

            def link(ins, name=None):
                n[0] += 1
                ins.then_inc(v, 1)
                dve.wait_ge(v, START + n[0])
                if name:
                    mark[name] = n[0]
            V = nc.vector
            lg = v3("logits", T, 36)
            link(V.memset(b["pad8"], NEG))
            link(V.memset(b["one32"], 1.0))
            link(V.memset(b["ones"], 1.0))
            link(V.memset(b["base"][:, 0:NE], 0.0))
            link(V.tensor_copy(v3("pad8", T, 8)[:, :, 0:NG], lg[:, :, 0:NG]))
            for t in range(T):
                link(V.max(v3("gm8", T, 8)[:, t, :], v3("pad8", T, 8)[:, t, :]))
                link(V.max_index(v3("gi8", T, 8)[:, t, :].bitcast(U32), v3("gm8", T, 8)[:, t, :], v3("pad8", T, 8)[:, t, :]))
            link(V.tensor_copy(b["gif"], v3("gi8", T, 8)[:, :, 0].bitcast(U32)))
            dve.wait_ge(f_ld, START + 48)
            io4 = b["iota"][:, 0:NG].rearrange("p (o n) -> p o n", o=1).to_broadcast([P, T, NG])
            link(V.tensor_tensor(v3("goh", T, NG), io4, b["gif"].rearrange("p (t o) -> p t o", o=1).to_broadcast([P, T, NG]),
                                 ALU.is_equal))
            link(V.tensor_scalar(b["goh"], b["goh"], 1.0, -NEG, ALU.subtract, ALU.mult))
            link(V.tensor_tensor(b["elm"].rearrange("p (t g e) -> p t g e", t=T, g=NG),
                                 lg[:, :, NG:36].rearrange("p t (g e) -> p t g e", g=NG),
                                 v3("goh", T, NG).rearrange("p t (g o) -> p t g o", o=1).to_broadcast([P, T, NG, EPG]), ALU.add))
            for t in range(T):
                link(V.max(v3("em8", T, 8)[:, t, :], v3("elm", T, NE)[:, t, :]))
                link(V.max_index(v3("ei8", T, 8)[:, t, :].bitcast(U32), v3("em8", T, 8)[:, t, :], v3("elm", T, NE)[:, t, :]))
            link(V.tensor_copy(b["eif"].rearrange("p (k t) -> p t k", k=2), v3("ei8", T, 8)[:, :, 0:2].bitcast(U32)))
            io32 = b["iota"][:, 0:NE].rearrange("p (o n) -> p o n", o=1).to_broadcast([P, T, NE])
            for k in range(2):
                idx = b["eif"][:, k * T:(k + 1) * T].rearrange("p (t o) -> p t o", o=1).to_broadcast([P, T, NE])
                link(V.tensor_tensor(v3(f"oh{k}", T, NE), io32, idx, ALU.is_equal))
            link(V.tensor_tensor(b["ohs"], b["oh0"], b["oh1"], ALU.add), "onehot")
            link(V.tensor_tensor(v3("gex", T, NG), lg[:, :, 0:NG], v3("gm8", T, 8)[:, :, 0:1].to_broadcast([P, T, NG]),
                                 ALU.subtract))
            link(V.tensor_tensor(b["dif"], v3("em8", T, 8)[:, :, 1], v3("em8", T, 8)[:, :, 0], ALU.subtract), "exps")
            dve.wait_ge(mm, START + 2)
            for t in range(T):
                link(V.tensor_tensor(b["base"][:, (t + 1) * NE:(t + 2) * NE], b["base"][:, t * NE:(t + 1) * NE],
                                     ps[:, 1, t * NE:(t + 1) * NE], ALU.add))
            cnt = b["base"][:, T * NE:(T + 1) * NE]
            link(V.tensor_tensor(b["rank"], ps[:, 0, :], b["base"][:, 0:T * NE], ALU.add))
            link(V.tensor_scalar(b["nbi"].bitcast(I32), cnt, float(P - 1), None, ALU.add))
            link(V.tensor_scalar(b["nbi"].bitcast(I32), b["nbi"].bitcast(I32), 7, None, ALU.arith_shift_right))
            link(V.tensor_copy(b["nb"], b["nbi"].bitcast(I32)))
            link(V.tensor_tensor_scan(b["pend"], b["one32"], b["nb"], 0.0, ALU.mult, ALU.add))
            link(V.tensor_tensor(b["pst"], b["pend"], b["nb"], ALU.subtract))
            link(V.tensor_scalar(b["pst"], b["pst"], float(P), None, ALU.mult))
            link(V.tensor_tensor(v3("rank", T, NE), v3("rank", T, NE),
                                 b["pst"].rearrange("p (o n) -> p o n", o=1).to_broadcast([P, T, NE]), ALU.add))
            for k in range(2):
                link(V.tensor_tensor(b["sel"], b["rank"], b[f"oh{k}"], ALU.mult))
                link(V.tensor_reduce(b["slotf"][:, k * T:(k + 1) * T], v3("sel", T, NE), AX_X, ALU.add))
            link(V.tensor_copy(slot_i[:], b["slotf"]), "slots")
            one = lambda ap: ap[0:1]

            def count_le(dst, n, limit):
                link(V.tensor_tensor(one(b["ge"])[:, 0:n * NE].rearrange("p (b e) -> p b e", b=n),
                                     one(b["iota"])[:, 0:n].rearrange("p (b o) -> p b o", o=1).to_broadcast([1, n, NE]),
                                     one(limit).rearrange("p (o e) -> p o e", o=1).to_broadcast([1, n, NE]), ALU.is_ge))
                if dst is not None:
                    link(V.tensor_reduce(dst, one(b["ge"])[:, 0:n * NE].rearrange("p (b e) -> p b e", b=n), AX_X, ALU.add))
            link(V.tensor_scalar(one(b["has"]), one(b["nb"]), 0.5, None, ALU.is_ge))
            link(V.tensor_tensor_scan(one(b["rk"]), one(b["one32"]), one(b["has"]), 0.0, ALU.mult, ALU.add))
            link(V.tensor_copy(tab[:, TAB_NR:TAB_NR + 1], one(b["rk"])[:, NE - 1:NE]))
            link(V.tensor_scalar(tab[:, TAB_NR1:TAB_NR1 + 1], one(b["rk"])[:, NE - 1:NE], -1.0, None, ALU.add))
            count_le(one(b["ebf"])[:, 0:NE], NE, b["rk"])
            link(V.tensor_scalar(tab[:, TAB_EXPERT:TAB_EXPERT + NE], one(b["ebf"])[:, 0:NE], float(NE - 1), None, ALU.min),
                 "experts")
            link(V.tensor_scalar(one(b["rk"]), one(b["rk"]), -1.0, None, ALU.add))
            count_le(None, NE, b["rk"])
            gev = one(b["ge"])[:, 0:NE * NE].rearrange("p (b e) -> p b e", b=NE)
            link(V.tensor_tensor(gev, gev, one(b["nb"]).rearrange("p (o e) -> p o e", o=1).to_broadcast([1, NE, NE]), ALU.mult))
            link(V.tensor_reduce(one(b["rend"]), gev, AX_X, ALU.add))
            count_le(one(b["ebf"]), 64, b["rend"])
            link(V.tensor_scalar(tab[:, TAB_RANK:TAB_RANK + 64], one(b["ebf"]), float(NE - 1), None, ALU.min))
            link(V.tensor_scalar(tab[:, TAB_BUF:TAB_BUF + 64], tab[:, TAB_RANK:TAB_RANK + 64], 1, None, ALU.bitwise_and))
            nw = one(b["nw"])
            link(V.memset(nw, 1.0))
            link(V.tensor_tensor(nw[:, 1:64], one(b["ebf"])[:, 1:64], one(b["ebf"])[:, 0:63], ALU.not_equal))
            link(V.tensor_scalar(one(b["ebf"]), one(b["ebf"]), one(b["rk"])[:, NE - 1:NE], None, ALU.is_lt))
            link(V.tensor_tensor(tab[:, TAB_NEW:TAB_NEW + 64], nw, one(b["ebf"]), ALU.mult))
            for less in range(3):
                link(V.tensor_scalar(tab[:, TAB_NB + less:TAB_NB + less + 1], one(b["pend"])[:, NE - 1:NE], float(-less), None, ALU.add))
            link(V.tensor_scalar(tab[:, TAB_FREE:TAB_FREE + 1], one(b["pend"])[:, NE - 1:NE], -1.0, 64.0, ALU.mult, ALU.add))
            dve.wait_ge(act_d, START + 2)
            link(V.tensor_reduce(b["gsum"], v3("gex", T, NG), AX_X, ALU.add))
            link(V.reciprocal(b["pg"], b["gsum"]))
            link(V.tensor_scalar(b["q"], b["dif"], 1.0, None, ALU.add))
            link(V.reciprocal(b["q"], b["q"]))
            link(V.tensor_tensor(gates[:, 0:T], b["q"], b["pg"], ALU.mult))
            link(V.tensor_tensor(gates[:, T:2 * T], gates[:, 0:T], b["dif"], ALU.mult))
            dve.wait_ge(f_ld, START + 64)
            link(V.tensor_copy(b["st_f"][0:64, :], b["st_i"][0:64, :].bitcast(I32)), "slot_tok")
            dve.wait_ge(tr, START + 1)
            link(V.tensor_copy(gidx[:, 0:64], ps[:, 2, 0:64]))

        @block.scalar
        def _(act):
            act.wait_ge(v, START + mark["exps"])
            nc.scalar.activation(b["gex"], b["gex"], ACT.Exp).then_inc(act_d, 1)
            nc.scalar.activation(b["dif"], b["dif"], ACT.Exp).then_inc(act_d, 1)

        @block.tensor
        def _(pe):
            pe.wait_ge(f_ld, START + 48)
            pe.wait_ge(v, START + mark["onehot"])
            pe.matmul(ps[:, 0, :], b["tri"], b["ohs"], start=True, stop=True).then_inc(mm, 1)
            pe.matmul(ps[:, 1, :], b["ones"], b["ohs"], start=True, stop=True).then_inc(mm, 1)
            pe.wait_ge(v, START + mark["slot_tok"])
            pe.transpose(ps[:, 2, 0:64], b["st_f"][0:64, :], idn[0:64, 0:64]).then_inc(tr, 1)

        @block.gpsimd
        def _(pool):
            pool.wait_ge(f_ld, START + 48)
            pool.wait_ge(v, START + mark["slots"])
            for k in range(2):
                for t in range(T):
                    pool.indirect_dma_start(g["slot_tok_d"], bass.IndirectOffsetOnAxis(slot_i[:, k * T + t:k * T + t + 1], 0),
                                            b["tok"][:, t:t + 1].bitcast(I32), None).then_inc(scat, 16)
            pool.wait_ge(scat, 16 * 2 * T)

        @block.sync
        def _(sp):
            sp.dma_start(b["tri"], g["tri"]).then_inc(f_ld, 16)
            sp.dma_start(b["iota"], g["iota"]).then_inc(f_ld, 16)
            sp.dma_start(b["tok"].bitcast(I32), g["tok_id"]).then_inc(f_ld, 16)
            sp.wait_ge(v, START + mark["experts"])
            sp.sem_inc(g["alone"], 1)
            first = sp.value_load(tab[0:1, TAB_EXPERT:TAB_EXPERT + 1], min_val=0, max_val=NE - 1)
            for n in range(N13 + N2):
                load_piece(sp, g, first, n)
            sp.wait_ge(scat, 16 * 2 * T)
            sp.dma_start(b["st_i"][0:64, :].bitcast(I32), g["slot_tok_d"].rearrange("(a b) o -> a (b o)", a=64)).then_inc(f_ld, 16)


def phase_experts(nc, env):
    g = env
    sem, arena, ps, ps_row, idn = g["sem"], g["arena"], g["ps"], g["ps_row"], g["idn"]
    tab, gidx = g["blk_tab"], g["gidx"]
    b = arena_slices(arena, 0, [("whi", WSZ), ("wlo", WSZ), ("st", WSZ), ("x0", D), ("x1", D), ("xh", D // 2), ("xl", D // 2),
                                ("s", D_EXP), ("h", D_EXP), ("hh", D_EXP // 2), ("hl", D_EXP // 2), ("g2", D), ("y0", D),
                                ("zero", D)])
    whi, wlo, xh, xl, hh, hl = (b[n].bitcast(F16) for n in ("whi", "wlo", "xh", "xl", "hh", "hl"))
    ix = g["stack"].enter_context(nc.sbuf_tensor("ix", [P, 2], I32))
    st_ld = [sem("g_st_ld0"), sem("g_st_ld1"), sem("g_st_ld2"), sem("g_st_ld3"), sem("g_st_ld4"), sem("g_st_ld5")]
    hi13, lo13, hi2, lo2 = sem("g_hi13"), sem("g_lo13"), sem("g_hi2"), sem("g_lo2")
    g2_ld, x_ix, x_ld, x_tr, x_hi, x_lo = (sem("g_g2_ld"), sem("g_x_ix"), g["plain_sem"]("g_x_ld"), sem("g_x_tr"),
                                           sem("g_x_hi"), sem("g_x_lo"))
    up_mm, silu_d, h_d, h_tr, h_hi, h_lo = (sem("g_up_mm"), sem("g_silu"), sem("g_h"), sem("g_h_tr"), sem("g_h_hi"),
                                            sem("g_h_lo"))
    y_mm, y_ev, y_st = sem("g_y_mm"), sem("g_y_ev"), sem("g_y_st")
    zero_d, z_st = sem("g_zero"), sem("g_z_st")

    def blocks(eng):
        return eng.value_load(tab[0:1, TAB_NB:TAB_NB + 1], min_val=32, max_val=MAX_BLOCKS - 1)

    def rank_of(eng, n):
        return eng.value_load(tab[0:1, bass.ds(n + TAB_RANK, 1)], min_val=0, max_val=NE - 1)

    def buffer_of(eng, n):
        return eng.value_load(tab[0:1, bass.ds(n + TAB_BUF, 1)], min_val=0, max_val=1)

    def starts_rank(eng, n):
        return eng.value_load(tab[0:1, bass.ds(n + TAB_NEW, 1)], min_val=0, max_val=1)

    def part(buf, whole, at, size):
        return whole[:, bass.ds(buf * WSZ + at, size)] if not isinstance(buf, int) else \
            whole[:, buf * WSZ + at:buf * WSZ + at + size]

    with nc.Block() as block:
        @block.sync
        def _(sp):
            sp.dma_start(b["g2"], g["mod_rows"][0:1, 5 * D:6 * D].to_broadcast([P, D])).then_inc(g2_ld, 16)
            ranks = sp.value_load(tab[0:1, TAB_NR:TAB_NR + 1], min_val=2, max_val=NE)

            def pieces(r, lo, hi):
                e = sp.value_load(tab[0:1, bass.ds(r + TAB_EXPERT, 1)], min_val=0, max_val=NE - 1)
                for n in range(lo, hi):
                    done = (lo13, N13 * (r - 1) + n + 1) if n < N13 else (lo2, N2 * (r - 1) + n - N13 + 1)
                    sp.wait_ge(done[0], START + done[1])
                    sp.sem_inc(g["alone"], 1)
                    load_piece(sp, g, e, n)
            pieces(1, 0, N13)
            with sp.Fori(2, ranks) as r:
                pieces(r, 0, N13)
                pieces(r - 1, N13, N13 + N2)
            pieces(sp.value_load(tab[0:1, TAB_NR1:TAB_NR1 + 1], min_val=1, max_val=NE - 1), N13, N13 + N2)
            used = blocks(sp)
            sp.wait_ge(zero_d, START + 1)
            with sp.Fori(used, 64) as n:
                sp.dma_start(g["y_d"][bass.ds(n * P, P), :], b["zero"]).then_inc(z_st, 16)
            sp.wait_ge(z_st, START + sp.value_load(tab[0:1, TAB_FREE:TAB_FREE + 1], min_val=1, max_val=32) * 16)
            sp.sem_inc(g["alone"], 1)

        @block.gpsimd
        def _(pool):
            nb = blocks(pool)

            def gather(i, j):
                pool.wait_ge(x_tr, START + 2 * i)
                pool.sem_inc(g["alone"], 1)
                nc.gpsimd.tensor_copy(ix[:, j:j + 1], gidx[:, bass.ds(2 * i + j, 1)]).then_inc(x_ix, 1)
                pool.wait_ge(x_ix, START + 2 * i + j + 1)
                pool.sem_inc(g["alone"], 1)
                pool.indirect_dma_start(b[f"x{j}"], None, g["h2_d"], bass.IndirectOffsetOnAxis(ix[:, j:j + 1], 0))\
                    .then_inc(x_ld, 16)
                pool.wait_ge(x_ld, 16 * (2 * i + j + 1))
                pool.sem_inc(g["alone"], 1)
            with pool.Fori(0, (nb >> 1) + 1) as i:
                gather(i, 0)
                gather(i, 1)

        @block.scalar
        def _(act):
            nb = blocks(act)

            def split13(r, buf, lo, hi):
                for n in range(lo, hi):
                    act.wait_ge(st_ld[n], START + 16 * r + 16)
                    nc.scalar.activation(part(buf, whi, n * PIECE, PIECE), b["st"][:, n * PIECE:(n + 1) * PIECE],
                                         ACT.Copy, scale=W_SCALE).then_inc(hi13, 1)

            def split2(r, buf):
                for n in range(N13, N13 + N2):
                    act.wait_ge(st_ld[n], START + 16 * r + 16)
                    nc.scalar.activation(part(buf, whi, n * PIECE, PIECE), b["st"][:, n * PIECE:(n + 1) * PIECE],
                                         ACT.Copy, scale=W_SCALE).then_inc(hi2, 1)

            def x_high(n):
                act.wait_ge(x_tr, START + n + 1)
                act.wait_ge(up_mm, START + 2 * n)
                nc.scalar.activation(xh, ps_row[:, 1024:2048], ACT.Copy, scale=X_SCALE).then_inc(x_hi, 1)

            def silu(n):
                act.wait_ge(up_mm, START + 2 * n + 1)
                act.wait_ge(h_d, START + n)
                nc.scalar.activation(b["s"], ps[:, 0, :], ACT.Silu, scale=1.0 / (W_SCALE * X_SCALE)).then_inc(silu_d, 1)

            def h_high(n):
                act.wait_ge(h_tr, START + n + 1)
                act.wait_ge(y_mm, START + n)
                nc.scalar.activation(hh, ps[:, 4, :], ACT.Copy).then_inc(h_hi, 1)

            def store_y(n):
                act.wait_ge(y_ev, START + n + 1)
                act.dma_start(g["y_d"][bass.ds(n * P, P), :], b["y0"]).then_inc(y_st, 16)

            def step(n, prev, stored):
                new = starts_rank(act, n)
                rank, buf = rank_of(act, n), buffer_of(act, n)
                with act.If(new == 1):
                    act.wait_ge(up_mm, START + 2 * n)
                    split13(rank + 1, 1 - buf, 0, N13 // 2)
                h_high(prev)
                silu(n)
                with act.If(new == 1):
                    split13(rank + 1, 1 - buf, N13 // 2, N13)
                x_high(n + 1)
                if stored:
                    store_y(n - 2)
                newp = starts_rank(act, prev)
                rankp, bufp = rank_of(act, prev), buffer_of(act, prev)
                with act.If(newp == 1):
                    act.wait_ge(y_mm, START + prev)
                    split2(rankp + 1, 1 - bufp)
            split13(0, 0, 0, N13)
            x_high(0)
            split2(0, 0)
            split13(1, 1, 0, N13 // 2)
            silu(0)
            split13(1, 1, N13 // 2, N13)
            x_high(1)
            step(1, 0, False)
            with act.Fori(2, nb) as n:
                step(n, n - 1, True)
            last = act.value_load(tab[0:1, TAB_NB1:TAB_NB1 + 1], min_val=31, max_val=MAX_BLOCKS - 2)
            store_y(act.value_load(tab[0:1, TAB_NB2:TAB_NB2 + 1], min_val=30, max_val=MAX_BLOCKS - 3))
            h_high(last)
            store_y(last)
            act.wait_ge(y_st, START + nb * 16)
            act.sem_inc(g["alone"], 1)

        @block.vector
        def _(dve):
            nb = blocks(dve)

            def low(dst, src, scale, high):
                return nc.vector.scalar_tensor_tensor(dst, src, scale, high, ALU.mult, ALU.subtract)

            def split13(r, buf, lo, hi):
                for n in range(lo, hi):
                    dve.wait_ge(hi13, START + N13 * r + n + 1)
                    dve.sem_inc(g["alone"], 1)
                    low(part(buf, wlo, n * PIECE, PIECE), b["st"][:, n * PIECE:(n + 1) * PIECE], W_SCALE,
                        part(buf, whi, n * PIECE, PIECE)).then_inc(lo13, 1)

            def split2(r, buf):
                for n in range(N13, N13 + N2):
                    dve.wait_ge(hi2, START + N2 * r + n - N13 + 1)
                    dve.sem_inc(g["alone"], 1)
                    low(part(buf, wlo, n * PIECE, PIECE), b["st"][:, n * PIECE:(n + 1) * PIECE], W_SCALE,
                        part(buf, whi, n * PIECE, PIECE)).then_inc(lo2, 1)

            def x_low(n):
                dve.wait_ge(x_hi, START + n + 1)
                low(xl, ps_row[:, 1024:2048], X_SCALE, xh).then_inc(x_lo, 1)

            def hidden(n):
                dve.wait_ge(silu_d, START + n + 1)
                dve.wait_ge(up_mm, START + 2 * n + 2)
                dve.wait_ge(h_tr, START + n)
                nc.vector.scalar_tensor_tensor(b["h"], ps[:, 1, :], 1.0 / (W_SCALE * X_SCALE), b["s"], ALU.mult, ALU.mult)\
                    .then_inc(h_d, 1)

            def h_low(n):
                dve.wait_ge(h_hi, START + n + 1)
                low(hl, ps[:, 4, :], 1.0, hh).then_inc(h_lo, 1)

            def scale_y(n):
                dve.wait_ge(y_mm, START + n + 1)
                dve.wait_ge(y_st, START + 16 * n)
                nc.vector.scalar_tensor_tensor(b["y0"], ps_row[:, 2560:3584], 1.0 / W_SCALE, b["g2"], ALU.mult, ALU.mult)\
                    .then_inc(y_ev, 1)

            def step(n, prev):
                new = starts_rank(dve, n)
                rank, buf = rank_of(dve, n), buffer_of(dve, n)
                with dve.If(new == 1):
                    split13(rank + 1, 1 - buf, 0, N13 // 2)
                h_low(prev)
                with dve.If(new == 1):
                    split13(rank + 1, 1 - buf, N13 // 2, N13)
                hidden(n)
                x_low(n + 1)
                newp = starts_rank(dve, prev)
                rankp, bufp = rank_of(dve, prev), buffer_of(dve, prev)
                with dve.If(newp == 1):
                    split2(rankp + 1, 1 - bufp)
                scale_y(prev)
            nc.vector.memset(b["zero"], 0.0).then_inc(zero_d, 1)
            dve.wait_ge(g2_ld, START + 16)
            split13(0, 0, 0, N13)
            x_low(0)
            split2(0, 0)
            split13(1, 1, 0, N13)
            hidden(0)
            x_low(1)
            step(1, 0)
            with dve.Fori(2, nb) as n:
                step(n, n - 1)
            last = dve.value_load(tab[0:1, TAB_NB1:TAB_NB1 + 1], min_val=31, max_val=MAX_BLOCKS - 2)
            h_low(last)
            scale_y(last)

        @block.tensor
        def _(pe):
            def transposes_x(j, n):
                pe.wait_ge(x_ld, 16 * n + 16)
                pe.wait_ge(x_lo, START + n)
                for k in range(KD):
                    mm = pe.transpose(ps_row[:, 1024 + k * P:1024 + (k + 1) * P], b[f"x{j}"][:, k * P:(k + 1) * P], idn[:])
                mm.then_inc(x_tr, 1)

            def product(out, high, low, buf, at, first, last):
                pe.matmul(out, high, part(buf, whi, at, 512), start=first, stop=False)
                pe.matmul(out, high, part(buf, wlo, at, 512), start=False, stop=False)
                return pe.matmul(out, low, part(buf, whi, at, 512), start=False, stop=last)

            def up(bank, off, buf):
                for k in range(KD):
                    mm = product(ps[:, bank, :], xh[:, k * P:(k + 1) * P], xl[:, k * P:(k + 1) * P], buf,
                                 off + k * D_EXP, k == 0, k == KD - 1)
                mm.then_inc(up_mm, 1)

            def down(n):
                rank, buf = rank_of(pe, n), buffer_of(pe, n)
                pe.wait_ge(h_lo, START + n + 1)
                pe.wait_ge(y_ev, START + n)
                pe.wait_ge(lo2, START + N2 * rank + N2)
                for k in range(KE):
                    for c in range(2):
                        mm = product(ps[:, 5 + c, :], hh[:, k * P:(k + 1) * P], hl[:, k * P:(k + 1) * P], buf,
                                     W13 + k * D + c * 512, k == 0, k == KE - 1)
                mm.then_inc(y_mm, 1)

            def transposes_h(n):
                pe.wait_ge(h_d, START + n + 1)
                pe.wait_ge(h_lo, START + n)
                for k in range(KE):
                    mm = pe.transpose(ps[:, 4, k * P:(k + 1) * P], b["h"][:, k * P:(k + 1) * P], idn[:])
                mm.then_inc(h_tr, 1)

            def step(n, prev, j):
                rank, buf = rank_of(pe, n), buffer_of(pe, n)
                pe.wait_ge(x_lo, START + n + 1)
                pe.wait_ge(silu_d, START + n)
                pe.wait_ge(lo13, START + N13 * rank + N13 // 2)
                up(0, 0, buf)
                if prev is not None:
                    transposes_h(prev)
                    pe.wait_ge(h_d, START + n)
                pe.wait_ge(lo13, START + N13 * rank + N13)
                up(1, KD * D_EXP, buf)
                transposes_x(1 - j, n + 1)
                if prev is not None:
                    down(prev)
            last = pe.value_load(tab[0:1, TAB_NB1:TAB_NB1 + 1], min_val=31, max_val=MAX_BLOCKS - 2)
            before = pe.value_load(tab[0:1, TAB_NB2:TAB_NB2 + 1], min_val=30, max_val=MAX_BLOCKS - 3)
            transposes_x(0, 0)
            step(0, None, 0)
            with pe.Fori(0, last >> 1) as i:
                step(2 * i + 1, 2 * i, 1)
                step(2 * i + 2, 2 * i + 1, 0)
            with pe.If((last & 1) == 1):
                step(last, before, 1)
            transposes_h(last)
            down(last)


def phase_combine(nc, env):
    g = env
    sem, plain_sem, arena = g["sem"], g["plain_sem"], g["arena"]
    slot_i, gates = g["slot_i"], g["gates"]
    b = arena_slices(arena, 0, [("l2g", D), ("l2b", D), ("mh", 1), ("st", 12), ("mv", 2), ("ve", 1), ("rs", 1)]
                     + [(f"{n}{j}", D) for n in ("ya", "yb", "x1", "xa", "o") for j in range(2)])
    ix = g["stack"].enter_context(nc.sbuf_tensor("ixc", [P, 4], I32))
    ld, ix_d, v, pw, a_x, mh_d = sem("h_ld"), sem("h_ix"), sem("h_v"), sem("h_pw"), sem("h_a_x"), sem("h_mh")
    y_ld = [plain_sem("h_y_ld0"), plain_sem("h_y_ld1")]
    x_ld, o_st = [sem("h_x_ld0"), sem("h_x_ld1")], [sem("h_o_st0"), sem("h_o_st1")]
    NV = 8
    LAST = T_LAT // 2 - 1
    with nc.Block() as block:
        @block.sync
        def _(sp):
            for n, name in enumerate(("l2g", "l2b")):
                sp.dma_start(b[name], g["ln2"][n:n + 1, :].to_broadcast([P, D])).then_inc(ld, 16)
            for j in range(2):
                sp.dma_start(b[f"x1{j}"], g["x1_d"][j * P:(j + 1) * P, :]).then_inc(x_ld[j], 16)
            with sp.Fori(0, LAST) as i:
                for j in range(2):
                    sp.wait_ge(a_x, START + 2 * i + j + 1)
                    sp.sem_inc(g["alone"], 1)
                    sp.dma_start(b[f"x1{j}"], g["x1_d"][bass.ds((2 * i + j + 2) * P, P), :]).then_inc(x_ld[j], 16)

        @block.gpsimd
        def _(pool):
            nc.gpsimd.memset(b["mh"], -0.5).then_inc(mh_d, 1)

            def fetch(i, j):
                for k in range(2):
                    nc.gpsimd.tensor_copy(ix[:, 2 * j + k:2 * j + k + 1], slot_i[:, bass.ds(k * T_LAT + 2 * i + j, 1)]).then_inc(ix_d, 1)
                pool.wait_ge(ix_d, START + 4 * i + 2 * j + 2)
                pool.sem_inc(g["alone"], 1)
                for k in range(2):
                    pool.indirect_dma_start(b[f"{('ya', 'yb')[k]}{j}"], None, g["y_d"],
                                            bass.IndirectOffsetOnAxis(ix[:, 2 * j + k:2 * j + k + 1], 0)).then_inc(y_ld[j], 16)

            def rstd(i, j):
                pool.wait_ge(v, START + NV * (2 * i + j) + 6)
                pool.sem_inc(g["alone"], 1)
                nc.gpsimd.tensor_tensor(b["rs"], b["ve"], b["mh"], ALU.pow).then_inc(pw, 1)
            for j in range(2):
                fetch(0, j)
            pool.wait_ge(mh_d, START + 1)
            with pool.Fori(0, LAST) as i:
                for j in range(2):
                    rstd(i, j)
                    fetch(i + 1, j)
            for j in range(2):
                rstd(LAST, j)

        @block.scalar
        def _(act):
            def store(i, j):
                act.wait_ge(v, START + NV * (2 * i + j + 1))
                act.dma_start(g["out"][bass.ds((2 * i + j) * P, P), :], b[f"o{j}"]).then_inc(o_st[j], 16)
            for j in range(2):
                act.wait_ge(x_ld[j], START + 16)
                nc.scalar.activation(b[f"xa{j}"], b[f"x1{j}"], ACT.Copy, scale=ALPHA).then_inc(a_x, 1)
            with act.Fori(0, LAST) as i:
                for j in range(2):
                    store(i, j)
                    act.wait_ge(x_ld[j], START + 16 * i + 32)
                    nc.scalar.activation(b[f"xa{j}"], b[f"x1{j}"], ACT.Copy, scale=ALPHA).then_inc(a_x, 1)
            for j in range(2):
                store(LAST, j)
            for j in range(2):
                act.wait_ge(o_st[j], START + 16 * (T_LAT // 2))

        @block.vector
        def _(dve):
            dve.wait_ge(ld, START + 32)
            with dve.Fori(0, T_LAT // 2) as i:
                for j in range(2):
                    t = 2 * i + j
                    n = [0]

                    def link(ins):
                        n[0] += 1
                        ins.then_inc(v, 1)
                        dve.wait_ge(v, START + NV * t + n[0])
                    y0, y1, xa, o = b[f"ya{j}"], b[f"yb{j}"], b[f"xa{j}"], b[f"o{j}"]
                    dve.wait_ge(a_x, START + t + 1)
                    dve.wait_ge(y_ld[j], 32 * i + 32)
                    link(nc.vector.scalar_tensor_tensor(xa, y0, gates[:, bass.ds(t, 1)], xa, ALU.mult, ALU.add))
                    link(nc.vector.scalar_tensor_tensor(xa, y1, gates[:, bass.ds(T_LAT + t, 1)], xa, ALU.mult, ALU.add))
                    nc.vector.bn_stats(b["st"][:, 0:6], xa[:, 0:512]).then_inc(v, 1)
                    n[0] += 1
                    link(nc.vector.bn_stats(b["st"][:, 6:12], xa[:, 512:1024]))
                    dve.sem_inc(g["alone"], 1)
                    link(nc.vector.bn_aggr(b["mv"], b["st"].rearrange("p (a s) -> p a s", a=2)))
                    link(nc.vector.tensor_scalar(b["ve"], b["mv"][:, 1:2], EPS, None, ALU.add))
                    link(nc.vector.scalar_tensor_tensor(xa, xa, b["mv"][:, 0:1], b["l2g"], ALU.subtract, ALU.mult))
                    dve.wait_ge(pw, START + t + 1)
                    dve.wait_ge(o_st[j], START + 16 * i)
                    link(nc.vector.scalar_tensor_tensor(o, xa, b["rs"], b["l2b"], ALU.mult, ALU.add))


def _constants():
    grid_w, axis = 64, HD // 2
    inv = (10000.0 ** (-np.arange(0, axis, 2, dtype=np.float32) / np.float32(axis))).astype(np.float32)
    pos = np.arange(SEQ)
    ang = np.stack([(pos // grid_w).astype(np.float32)[:, None] * inv, (pos % grid_w).astype(np.float32)[:, None] * inv], 1)
    cos_t = np.cos(ang).astype(np.float32).reshape(T_LAT, P, 2 * inv.size)
    sin_t = np.sin(ang).astype(np.float32).reshape(T_LAT, P, 2 * inv.size)
    q, k = np.arange(P)[:, None], np.arange(WIN)[None, :] - P
    masks = np.zeros((4, P, KEYS), np.float32)
    for m in range(3):
        ok = np.abs(k - q) <= P
        if m == 0:
            ok = ok & (k >= 0)
        if m == 2:
            ok = ok & (k < P)
        masks[m, :, CTX:] = np.where(ok, 0.0, NEG)
    tri = np.triu(np.ones((P, P), np.float32), 1)
    iota = np.tile(np.arange(64, dtype=np.float32), (P, 1))
    tok = (np.arange(T_LAT)[None, :] * P + np.arange(P)[:, None]).astype(np.int32)
    return {"cos_t": cos_t, "sin_t": sin_t, "ident": np.eye(P, dtype=np.float32), "masks": masks, "tri": tri,
            "iota": iota, "tok_id": tok}


def _layout(i):
    c = np.ascontiguousarray
    cs = np.stack([np.asarray(i["c"])[0], np.asarray(i["c_ctx"])], 1)
    a = {k: np.asarray(i[k]) for k in i}
    return {
        "x": c(a["x"][0]), "c2": c(cs.reshape(KD, P, 2).transpose(1, 0, 2).reshape(P, 2 * KD)), "w_mod": c(a["w_mod"][0]),
        "b_mod": c(np.stack([a["b_mod"][0]] * 2)), "w_in": c(a["w_in"][0]),
        "rg_par": c(np.concatenate([a["conv_w"][0].T, a["conv_b"][0][:, None], a["rg_ba"][0].T, a["rg_bx"][0].T],
                                   1)),
        "lam": c(a["rg_lam"][0].reshape(2, C_RNN, P).transpose(2, 0, 1).reshape(P, 2 * C_RNN)),
        "rg_wa": c(a["rg_wa"][0]), "rg_wx": c(a["rg_wx"][0]), "ctx_x": c(a["ctx"][0]),
        "sink": c(np.stack([a["attn_sink"][0]] * P)), "w_out": c(a["w_out"][0]),
        "gn": c(np.concatenate([a["gn_rnn"][0], a["gn_attn"][0]]).reshape(KD, P).T),
        "ln1": c(np.stack([a["ln1_g"][0], a["ln1_b"][0]])),
        "router": c(np.concatenate([a["router_g"][0], a["router_e"][0]], 1)),
        "router_b": c(np.concatenate([a["router_gb"][0], a["router_eb"][0]])[None, :]),
        "w1": c(a["w1"][0]), "w3": c(a["w3"][0]), "w2": c(a["w2"][0]), "ln2": c(np.stack([a["ln2_g"][0], a["ln2_b"][0]])),
        **_constants(),
    }


_ARGS = ["x", "c2", "w_mod", "b_mod", "w_in", "rg_par", "lam", "rg_wa", "rg_wx", "ctx_x", "sink", "w_out", "gn", "ln1", "router",
         "router_b", "w1", "w3", "w2", "ln2", "cos_t", "sin_t", "ident", "masks", "tri", "iota", "tok_id"]


def kernel(**inputs):
    import concourse.bacc as bacc
    from concourse.bass_utils import run_bass_kernel_spmd

    arrays = _layout(inputs)
    nc = bacc.Bacc("TRN2", target_bir_lowering=False, num_devices=1)
    aps = {n: nc.dram_tensor(n, arrays[n].shape, mybir.dt.from_np(arrays[n].dtype), kind="ExternalInput").ap() for n in _ARGS}
    aps["out"] = nc.dram_tensor("out", (SEQ, D), F32, kind="ExternalOutput").ap()
    hybrid_layer(nc, **aps)
    r = run_bass_kernel_spmd(nc, [{n: arrays[n] for n in _ARGS}], core_ids=[0])
    return np.asarray(r.results[0]["out"]).reshape(1, SEQ, D)
```
